# Optimizing a Trainium2 kernel written in Bass

```python
import math
import jax, jax.numpy as jnp
from jax import lax
import numpy as np

D_MODEL = 1024
BATCH = 1
SEQ = 256
DEPTH = 2

DN_ALPHA = (2 * DEPTH) ** 0.25
DN_BETA = (8 * DEPTH) ** -0.25
LN_EPS = 1e-5

CONV_WIDTH = D_MODEL // 2
CONV_GROUPS = 8
CONV_TAPS = 3
LRU_WIDTH = D_MODEL // 2
LRU_HEADS = 8
LRU_HEAD_DIM = LRU_WIDTH // LRU_HEADS
LRU_CONV_TAPS = 4
LRU_C = 8.0
L0_IN_COLS = 3 * CONV_WIDTH + 2 * LRU_WIDTH

N_HEADS = 16
HEAD_DIM = 64
N_KV_GROUPS = 4
HEADS_PER_GROUP = N_HEADS // N_KV_GROUPS
KV_WIDTH = N_KV_GROUPS * HEAD_DIM
CMP_STRIDE = 16
CMP_BLOCK = 2 * CMP_STRIDE
CMP_HIDDEN = 256
SEL_BLOCK = 64
N_SEL = 16
WINDOW = 512
Q_BLOCK = 128
ROPE_THETA = 10000.0
L1_IN_COLS = N_HEADS * HEAD_DIM + 6 * KV_WIDTH + 3 * N_HEADS
FORCE = 1e4
NEG = -1e30
TINY = 1e-30

N_GROUPS = 4
EXPERTS_PER_GROUP = 8
N_EXPERTS = N_GROUPS * EXPERTS_PER_GROUP
TOP_K = 2
EXPERT_FF = 512
MOE_BLOCK = 256

kernel_name = "hybrid_conv_rglru_nsa_hiermoe_deepnorm"

F32 = jnp.float32

def _layernorm(x, g, b):
    xf = x.astype(F32)
    mu = jnp.mean(xf, -1, keepdims=True)
    var = jnp.mean(jnp.square(xf - mu), -1, keepdims=True)
    y = (xf - mu) * lax.rsqrt(var + LN_EPS)
    return (y * g.astype(F32) + b.astype(F32)).astype(x.dtype)

def _causal_dwconv(x, w):
    taps, S = w.shape[0], x.shape[1]
    xp = jnp.pad(x, ((0, 0), (taps - 1, 0), (0, 0)))
    y = xp[:, 0:S] * w[0]
    for k in range(1, taps):
        y = y + xp[:, k:k + S] * w[k]
    return y

def _rglru(xc, w_a, b_a, w_x, b_x, lam):
    Bn, S, C = xc.shape
    xh = xc.reshape(Bn, S, LRU_HEADS, LRU_HEAD_DIM)
    r = jax.nn.sigmoid((jnp.einsum('bshi,hij->bshj', xh, w_a).reshape(Bn, S, C) + b_a).astype(F32))
    i = jax.nn.sigmoid((jnp.einsum('bshi,hij->bshj', xh, w_x).reshape(Bn, S, C) + b_x).astype(F32))
    log_a = -LRU_C * r * jax.nn.softplus(-lam.astype(F32))
    a = jnp.exp(log_a)
    mult = jnp.sqrt(jnp.maximum(-jnp.expm1(2.0 * log_a), 0.0))
    u = mult * i * xc.astype(F32)

    def comb(left, right):
        a1, b1 = left
        a2, b2 = right
        return a1 * a2, a2 * b1 + b2

    _, h = lax.associative_scan(comb, (a, u), axis=1)
    return h.astype(xc.dtype)

def _even_mixer(x, w_in, conv_w, lru_conv_w, lru_conv_b, w_a, b_a, w_x, b_x, lam, w_out):
    z = x @ w_in
    W = CONV_WIDTH
    bg, cg, hc, gate, xl = jnp.split(z, [W, 2 * W, 3 * W, 3 * W + LRU_WIDTH], axis=-1)
    y_conv = bg * _causal_dwconv(cg * hc, conv_w)
    xc = _causal_dwconv(xl, lru_conv_w) + lru_conv_b
    y_lru = _rglru(xc, w_a, b_a, w_x, b_x, lam) * jax.nn.gelu(gate)
    return jnp.concatenate([y_conv, y_lru], axis=-1) @ w_out

def _rope(x, cos, sin):
    xf = x.astype(F32)
    x1, x2 = jnp.split(xf, 2, axis=-1)
    c = cos[None, :, None, :]
    s = sin[None, :, None, :]
    return jnp.concatenate([x1 * c - x2 * s, x2 * c + x1 * s], axis=-1).astype(x.dtype)

def _masked_softmax(s, mask):
    s = jnp.where(mask, s, NEG)
    s = s - jnp.max(s, axis=-1, keepdims=True)
    p = jnp.exp(s) * mask
    return p / jnp.maximum(jnp.sum(p, axis=-1, keepdims=True), TINY)

def _compress(k, pe, w1, w2):
    Bn, S, G, dk = k.shape
    ch = k.reshape(Bn, S // CMP_STRIDE, CMP_STRIDE, G, dk)
    blocks = jnp.concatenate([ch[:, :-1], ch[:, 1:]], axis=2)
    blocks = blocks + pe[None, None, :, None, :]
    flat = blocks.transpose(0, 1, 3, 2, 4).reshape(Bn, blocks.shape[1], G, CMP_BLOCK * dk)
    return jax.nn.gelu(flat @ w1) @ w2

def _nsa_mixer(x, w_in, cmp_k_pe, cmp_k_w1, cmp_k_w2, cmp_v_pe, cmp_v_w1, cmp_v_w2, w_out):
    Bn, S, _ = x.shape
    G, R, dk = N_KV_GROUPS, HEADS_PER_GROUP, HEAD_DIM
    z = x @ w_in
    qd = N_HEADS * HEAD_DIM
    cuts = [qd + j * KV_WIDTH for j in range(7)]
    q, kc, vc, ks, vs, kw, vw, gl = jnp.split(z, cuts, axis=-1)
    q = q.reshape(Bn, S, N_HEADS, dk)
    kc, vc, ks, vs, kw, vw = [t.reshape(Bn, S, G, dk) for t in (kc, vc, ks, vs, kw, vw)]

    pos = jnp.arange(S, dtype=F32)
    inv = ROPE_THETA ** (-jnp.arange(0, dk, 2, dtype=F32) / dk)
    ang = pos[:, None] * inv[None, :]
    cos, sin = jnp.cos(ang), jnp.sin(ang)
    q = _rope(q, cos, sin)
    kc = _rope(kc, cos, sin)
    ks = _rope(ks, cos, sin)
    kw = _rope(kw, cos, sin)
    gates = jax.nn.sigmoid(gl.astype(F32)).reshape(Bn, S, G, R, 3)

    kcmp = _compress(kc, cmp_k_pe, cmp_k_w1, cmp_k_w2)
    vcmp = _compress(vc, cmp_v_pe, cmp_v_w1, cmp_v_w2)
    n_cmp = kcmp.shape[1]
    n_slc = S // SEL_BLOCK
    n_top = min(N_SEL, n_slc)
    ksb = ks.reshape(Bn, n_slc, SEL_BLOCK, G, dk).transpose(0, 3, 1, 2, 4)
    vsb = vs.reshape(Bn, n_slc, SEL_BLOCK, G, dk).transpose(0, 3, 1, 2, 4)
    kwp = jnp.pad(kw, ((0, 0), (WINDOW, 0), (0, 0), (0, 0)))
    vwp = jnp.pad(vw, ((0, 0), (WINDOW, 0), (0, 0), (0, 0)))

    c_start = jnp.arange(n_cmp) * CMP_STRIDE
    j_idx = jnp.arange(n_slc)
    j_start = j_idx * SEL_BLOCK
    overlap = ((c_start[:, None] < j_start[None, :] + SEL_BLOCK)
               & (c_start[:, None] + CMP_BLOCK > j_start[None, :])).astype(F32)
    scale = HEAD_DIM ** -0.5
    bidx = jnp.arange(Bn)[:, None, None, None]
    gidx = jnp.arange(G)[None, :, None, None]

    def block(qi):
        qs = qi * Q_BLOCK
        t = qs + jnp.arange(Q_BLOCK)
        qb = lax.dynamic_slice_in_dim(q, qs, Q_BLOCK, 1).reshape(Bn, Q_BLOCK, G, R, dk)
        gb = lax.dynamic_slice_in_dim(gates, qs, Q_BLOCK, 1)
        s_c = jnp.einsum('bqgrd,bcgd->bgrqc', qb, kcmp).astype(F32) * scale
        m_c = (c_start + CMP_BLOCK - 1)[None, :] <= t[:, None]
        p_c = _masked_softmax(s_c, m_c)
        o_c = jnp.einsum('bgrqc,bcgd->bqgrd', p_c.astype(x.dtype), vcmp)
        imp = jnp.einsum('bgrqc,cj->bgqj', p_c, overlap)
        bt = t // SEL_BLOCK
        forced = ((j_idx[None, :] == 0) | (j_idx[None, :] == bt[:, None])
                  | (j_idx[None, :] == bt[:, None] - 1))
        future = j_idx[None, :] > bt[:, None]
        imp = jnp.where(forced, FORCE, jnp.where(future, -FORCE, imp))
        _, sel = lax.top_k(imp, n_top)
        ksel = ksb[bidx, gidx, sel]
        vsel = vsb[bidx, gidx, sel]
        s_s = jnp.einsum('bqgrd,bgqnkd->bgrqnk', qb, ksel).astype(F32) * scale
        kpos = sel[..., None] * SEL_BLOCK + jnp.arange(SEL_BLOCK)
        m_s = (kpos <= t[None, None, :, None, None]).reshape(Bn, G, 1, Q_BLOCK, n_top * SEL_BLOCK)
        p_s = _masked_softmax(s_s.reshape(Bn, G, R, Q_BLOCK, n_top * SEL_BLOCK), m_s)
        p_s = p_s.reshape(Bn, G, R, Q_BLOCK, n_top, SEL_BLOCK).astype(x.dtype)
        o_s = jnp.einsum('bgrqnk,bgqnkd->bqgrd', p_s, vsel)
        kwb = lax.dynamic_slice_in_dim(kwp, qs, WINDOW + Q_BLOCK, 1)
        vwb = lax.dynamic_slice_in_dim(vwp, qs, WINDOW + Q_BLOCK, 1)
        wpos = qs - WINDOW + jnp.arange(WINDOW + Q_BLOCK)
        m_w = ((wpos[None, :] <= t[:, None]) & (wpos[None, :] > t[:, None] - WINDOW)
               & (wpos[None, :] >= 0))
        s_w = jnp.einsum('bqgrd,bkgd->bgrqk', qb, kwb).astype(F32) * scale
        p_w = _masked_softmax(s_w, m_w).astype(x.dtype)
        o_w = jnp.einsum('bgrqk,bkgd->bqgrd', p_w, vwb)
        o = gb[..., 0:1] * o_c + gb[..., 1:2] * o_s + gb[..., 2:3] * o_w
        return o.astype(x.dtype).reshape(Bn, Q_BLOCK, N_HEADS * dk)

    out = lax.map(block, jnp.arange(S // Q_BLOCK))
    out = out.transpose(1, 0, 2, 3).reshape(Bn, S, N_HEADS * dk)
    return out @ w_out

def _hier_moe(x, w_rg, b_rg, w_re, b_re, w_gate, w_up, w_down):
    Bn, S, D = x.shape
    T = Bn * S
    xf = x.reshape(T, D)
    tok_ar = jnp.arange(T)
    lg = (xf @ w_rg).astype(F32) + b_rg.astype(F32)
    pg = jax.nn.softmax(lg, axis=-1)
    g_star = jnp.argmax(lg, axis=-1)
    p_grp = pg[tok_ar, g_star][:, None]
    le = ((xf @ w_re).astype(F32) + b_re.astype(F32)).reshape(T, N_GROUPS, EXPERTS_PER_GROUP)
    pe = jax.nn.softmax(le[tok_ar, g_star], axis=-1)
    v, idx = lax.top_k(pe, TOP_K)
    w = p_grp * v / jnp.sum(v, axis=-1, keepdims=True)
    e = g_star[:, None] * EXPERTS_PER_GROUP + idx

    A = T * TOP_K
    e_flat = e.reshape(A)
    w_flat = w.reshape(A)
    tok = jnp.repeat(tok_ar, TOP_K)
    order = jnp.argsort(e_flat)
    e_s, tok_s, w_s = e_flat[order], tok[order], w_flat[order]
    counts = jnp.bincount(e_flat, length=N_EXPERTS)
    starts = jnp.cumsum(counts) - counts
    padded = (counts + MOE_BLOCK - 1) // MOE_BLOCK * MOE_BLOCK
    pad_end = jnp.cumsum(padded)
    pad_start = pad_end - padded
    dest = pad_start[e_s] + jnp.arange(A) - starts[e_s]
    n_blocks = -(-A // MOE_BLOCK) + N_EXPERTS
    P = n_blocks * MOE_BLOCK
    xs = jnp.zeros((P, D), x.dtype).at[dest].set(xf[tok_s])
    block_e = jnp.minimum(jnp.searchsorted(pad_end, jnp.arange(n_blocks) * MOE_BLOCK, side='right'),
                          N_EXPERTS - 1)

    def expert_block(args):
        xb, eb = args
        h = jax.nn.silu(xb @ w_gate[eb]) * (xb @ w_up[eb])
        return h @ w_down[eb]

    ys = lax.map(expert_block, (xs.reshape(n_blocks, MOE_BLOCK, D), block_e)).reshape(P, D)
    y = jnp.zeros((T, D), x.dtype).at[tok_s].add(ys[dest] * w_s[:, None].astype(x.dtype))
    return y.reshape(Bn, S, D)

def _moe_params(key, prefix):
    k = jax.random.split(key, 7)
    D = D_MODEL
    return {
        prefix + "router_group_w": jax.random.normal(k[0], (D, N_GROUPS), F32) * D ** -0.5,
        prefix + "router_group_b": jax.random.normal(k[1], (N_GROUPS,), F32) * 0.01,
        prefix + "router_expert_w": jax.random.normal(k[2], (D, N_EXPERTS), F32) * D ** -0.5,
        prefix + "router_expert_b": jax.random.normal(k[3], (N_EXPERTS,), F32) * 0.01,
        prefix + "expert_w_gate": jax.random.normal(k[4], (N_EXPERTS, D, EXPERT_FF), F32) * D ** -0.5,
        prefix + "expert_w_up": jax.random.normal(k[5], (N_EXPERTS, D, EXPERT_FF), F32) * D ** -0.5,
        prefix + "expert_w_down": jax.random.normal(k[6], (N_EXPERTS, EXPERT_FF, D), F32)
        * (EXPERT_FF ** -0.5 * DN_BETA),
    }

def _ln_params(key, prefix):
    k1, k2 = jax.random.split(key)
    return {prefix + "_g": 1.0 + 0.02 * jax.random.normal(k1, (D_MODEL,), F32),
            prefix + "_b": 0.02 * jax.random.normal(k2, (D_MODEL,), F32)}

def setup_inputs(seed: int = 0) -> dict:
    key = jax.random.key(seed)
    ks = jax.random.split(key, 32)
    D = D_MODEL
    p = {}
    p["x"] = jax.random.normal(ks[0], (BATCH, SEQ, D), F32)
    p["l0_w_in"] = jax.random.normal(ks[1], (D, L0_IN_COLS), F32) * D ** -0.5
    p["l0_conv_w"] = jax.random.normal(ks[2], (CONV_TAPS, CONV_WIDTH), F32) * CONV_TAPS ** -0.5
    p["l0_lru_conv_w"] = jax.random.normal(ks[3], (LRU_CONV_TAPS, LRU_WIDTH), F32) * LRU_CONV_TAPS ** -0.5
    p["l0_lru_conv_b"] = jax.random.normal(ks[4], (LRU_WIDTH,), F32) * 0.01
    p["l0_lru_w_a"] = jax.random.normal(ks[5], (LRU_HEADS, LRU_HEAD_DIM, LRU_HEAD_DIM), F32) * LRU_HEAD_DIM ** -0.5
    p["l0_lru_b_a"] = jax.random.normal(ks[6], (LRU_WIDTH,), F32) * 0.01
    p["l0_lru_w_x"] = jax.random.normal(ks[7], (LRU_HEADS, LRU_HEAD_DIM, LRU_HEAD_DIM), F32) * LRU_HEAD_DIM ** -0.5
    p["l0_lru_b_x"] = jax.random.normal(ks[8], (LRU_WIDTH,), F32) * 0.01
    u = jax.random.uniform(ks[9], (LRU_WIDTH,), F32, minval=0.9, maxval=0.999)
    a0 = u ** (1.0 / LRU_C)
    p["l0_lru_lambda"] = jnp.log(a0) - jnp.log1p(-a0)
    p["l0_w_out"] = jax.random.normal(ks[10], (CONV_WIDTH + LRU_WIDTH, D), F32) * (D ** -0.5 * DN_BETA)
    p.update(_ln_params(ks[11], "l0_ln1"))
    p.update(_moe_params(ks[12], "l0_"))
    p.update(_ln_params(ks[13], "l0_ln2"))
    ones_kv = jnp.ones((KV_WIDTH,), F32)
    beta_kv = jnp.full((KV_WIDTH,), DN_BETA, F32)
    col_scale = jnp.concatenate([jnp.ones((N_HEADS * HEAD_DIM,), F32), ones_kv, beta_kv, ones_kv, beta_kv,
                                 ones_kv, beta_kv, jnp.ones((3 * N_HEADS,), F32)])
    p["l1_w_in"] = jax.random.normal(ks[14], (D, L1_IN_COLS), F32) * (D ** -0.5) * col_scale[None, :]
    p["l1_cmp_k_pe"] = jax.random.normal(ks[15], (CMP_BLOCK, HEAD_DIM), F32) * 0.02
    p["l1_cmp_k_w1"] = jax.random.normal(ks[16], (CMP_BLOCK * HEAD_DIM, CMP_HIDDEN), F32) * (CMP_BLOCK * HEAD_DIM) ** -0.5
    p["l1_cmp_k_w2"] = jax.random.normal(ks[17], (CMP_HIDDEN, HEAD_DIM), F32) * CMP_HIDDEN ** -0.5
    p["l1_cmp_v_pe"] = jax.random.normal(ks[18], (CMP_BLOCK, HEAD_DIM), F32) * 0.02
    p["l1_cmp_v_w1"] = jax.random.normal(ks[19], (CMP_BLOCK * HEAD_DIM, CMP_HIDDEN), F32) * (CMP_BLOCK * HEAD_DIM) ** -0.5
    p["l1_cmp_v_w2"] = jax.random.normal(ks[20], (CMP_HIDDEN, HEAD_DIM), F32) * CMP_HIDDEN ** -0.5
    p["l1_w_out"] = jax.random.normal(ks[21], (N_HEADS * HEAD_DIM, D), F32) * (D ** -0.5 * DN_BETA)
    p.update(_ln_params(ks[22], "l1_ln1"))
    p.update(_moe_params(ks[23], "l1_"))
    p.update(_ln_params(ks[24], "l1_ln2"))
    return p

def reference(x,
              l0_w_in, l0_conv_w, l0_lru_conv_w, l0_lru_conv_b, l0_lru_w_a, l0_lru_b_a, l0_lru_w_x,
              l0_lru_b_x, l0_lru_lambda, l0_w_out, l0_ln1_g, l0_ln1_b,
              l0_router_group_w, l0_router_group_b, l0_router_expert_w, l0_router_expert_b,
              l0_expert_w_gate, l0_expert_w_up, l0_expert_w_down, l0_ln2_g, l0_ln2_b,
              l1_w_in, l1_cmp_k_pe, l1_cmp_k_w1, l1_cmp_k_w2, l1_cmp_v_pe, l1_cmp_v_w1, l1_cmp_v_w2,
              l1_w_out, l1_ln1_g, l1_ln1_b,
              l1_router_group_w, l1_router_group_b, l1_router_expert_w, l1_router_expert_b,
              l1_expert_w_gate, l1_expert_w_up, l1_expert_w_down, l1_ln2_g, l1_ln2_b):
    mixers = (
        lambda h: _even_mixer(h, l0_w_in, l0_conv_w, l0_lru_conv_w, l0_lru_conv_b, l0_lru_w_a, l0_lru_b_a,
                              l0_lru_w_x, l0_lru_b_x, l0_lru_lambda, l0_w_out),
        lambda h: _nsa_mixer(h, l1_w_in, l1_cmp_k_pe, l1_cmp_k_w1, l1_cmp_k_w2, l1_cmp_v_pe, l1_cmp_v_w1,
                             l1_cmp_v_w2, l1_w_out),
    )
    norms1 = ((l0_ln1_g, l0_ln1_b), (l1_ln1_g, l1_ln1_b))
    norms2 = ((l0_ln2_g, l0_ln2_b), (l1_ln2_g, l1_ln2_b))
    moes = ((l0_router_group_w, l0_router_group_b, l0_router_expert_w, l0_router_expert_b,
             l0_expert_w_gate, l0_expert_w_up, l0_expert_w_down),
            (l1_router_group_w, l1_router_group_b, l1_router_expert_w, l1_router_expert_b,
             l1_expert_w_gate, l1_expert_w_up, l1_expert_w_down))
    for layer in range(DEPTH):
        x = _layernorm(DN_ALPHA * x + mixers[layer](x), *norms1[layer])
        x = _layernorm(DN_ALPHA * x + _hier_moe(x, *moes[layer]), *norms2[layer])
    return x


_drawn_inputs = setup_inputs


def setup_inputs(seed=0):
    import zlib

    import numpy as np

    out = dict(_drawn_inputs(seed))
    spreads = {}
    factors = {'l0_lru_conv_b': 7.359,
     'l0_lru_b_a': 64.0,
     'l0_lru_b_x': 64.0,
     'l0_router_group_b': 8.0,
     'l0_router_expert_b': 25.598,
     'l1_cmp_k_pe': 31.119,
     'l1_cmp_k_w1': 5.682,
     'l1_cmp_k_w2': 4.39,
     'l1_cmp_v_pe': 23.327,
     'l1_router_group_b': 64.0,
     'l1_router_expert_b': 31.259,
     'l1_ln2_g': 8.158,
     'l1_ln2_b': 7.805,
     'l0_ln2_g': 2.708}
    for name, (base, spread) in spreads.items():
        noise = np.random.default_rng([zlib.crc32(name.encode()), seed]).standard_normal(out[name].shape)
        drawn = base * np.exp(spread * noise) if base else spread * noise
        out[name] = __import__('jax').numpy.asarray(drawn.astype(out[name].dtype))
    for name, factor in factors.items():
        out[name] = (out[name] * factor).astype(out[name].dtype)
    return out
```

```python
import concourse.bass as bass
from concourse import mybir
from contextlib import ExitStack

SEQ, D, FF, NE, NG = 256, 1024, 512, 32, 4
CW = 512
KT = D // 128
NT = SEQ // 128
WIN = 64
NSLOT = 2 * SEQ
NPAD = NSLOT + WIN
NWIN = SEQ // WIN
ALPHA = (2 * 2) ** 0.25
LN_EPS = 1e-5
NH, DK, NKV = 16, 64, 4
NBLK = SEQ // 16 - 1
SCALE = DK ** -0.5
TINY = 1e-30
RING = 9
GL = 48

L0_COLS = [4 * CW, 3 * CW, CW, 2 * CW, 0]
L0_UNITS = 7
L1_UNITS = 9
MIX_BASE = [0, L0_UNITS + 3 * NE]
EXP_BASE = [L0_UNITS, L0_UNITS + 3 * NE + L1_UNITS]

C_ID, C_UP, C_ONE, C_CAUS, C_IOTA, C_EPS = 0, 128, 256, 384, 512, 1024
N_CONST = 1025
A_ROPE, A_CMPA, A_CMPM, N_ATT = 0, 128, 160, 192
P_CONV, P_LCONV, P_LCB, P_BA, P_BX, P_LAM = 0, 12, 28, 32, 36, 40
N_PARAM = 44


def program(nc, a, out):
    f32, i32, u32 = mybir.dt.float32, mybir.dt.int32, mybir.dt.uint32
    ALU, ACT, AX = mybir.AluOpType, mybir.ActivationFunctionType, mybir.AxisListType
    ctx = ExitStack()
    with ctx:
        def sb(name, shape, dt=f32):
            return ctx.enter_context(nc.sbuf_tensor(name, shape, dt))

        def sem(name):
            return ctx.enter_context(nc.semaphore(name))

        ring = sb("ring", [128, RING, 4096])
        x_tok = sb("x_tok", [128, NT, D])
        cst = sb("cst", [128, N_CONST])
        work = sb("work", [128, 12560])
        par = sb("par", [128, N_PARAM])
        sp_t = sb("sp_t", [128, 6, 4])
        stats = sb("stats", [128, NT, 2, 6])
        mv = sb("mv", [128, NT, 2])
        sd = sb("sd", [128, NT])
        rstd = sb("rstd", [128, NT])
        rbias = sb("rbias", [128, 36])
        slotw = sb("slotw", [128, 2, 2, NT])
        cntw = sb("cntw", [128, NWIN, NE])
        offi = sb("offi", [1, NWIN * NE], i32)
        mxi = sb("mxi", [1, 1], i32)
        small = sb("small", [128, 3 * WIN])
        mask = small[:, :].rearrange("p (b s) -> p b s", b=3)
        gates = small[:, 0:NT * GL].rearrange("p (t c) -> p t c", t=NT)
        asm = small[:, 96:108].rearrange("p (n c) -> p n c", n=2)
        arec = small[:, 108:112].rearrange("p (n c) -> p n c", n=2)
        cmx = small[:, 112:144].rearrange("p (t h) -> p t h", t=NT)
        bank = [ctx.enter_context(nc.psum_tensor(f"bank{i}", [128, 512], f32)) for i in range(8)]

        def w_(lo, n, parts=128, p0=0):
            return work[p0:p0 + parts, lo:lo + n]

        ident, upper, ones = cst[:, C_ID:C_ID + 128], cst[:, C_UP:C_UP + 128], cst[:, C_ONE:C_ONE + 128]
        causal, iota = cst[:, C_CAUS:C_CAUS + 128], cst[:, C_IOTA:C_IOTA + 512]
        catt = w_(11600, N_ATT)
        rope = catt[:, A_ROPE:A_ROPE + 128].rearrange("p (t s d) -> p t s d", t=NT, s=2)
        cmp_add = catt[:, A_CMPA:A_CMPA + 32].rearrange("p (t c) -> p t c", t=NT)
        cmp_mul = catt[:, A_CMPM:A_CMPM + 32].rearrange("p (t c) -> p t c", t=NT)
        eps = cst[:, C_EPS:C_EPS + 1]

        xT0 = w_(0, 2048).rearrange("p (k t) -> p k t", k=KT)
        xl = w_(2048, 1040).rearrange("p (c t) -> p c t", c=4)
        gate = w_(3088, 1024).rearrange("p (c t) -> p c t", c=4)
        cghc = w_(4112, 1040).rearrange("p (c t) -> p c t", c=4)
        xc = w_(5152, 1024).rearrange("p (c t) -> p c t", c=4)
        rg = w_(6176, 1024).rearrange("p (c t) -> p c t", c=4)
        ig = w_(7200, 1024).rearrange("p (c t) -> p c t", c=4)
        yT = w_(8224, 2048).rearrange("p (k t) -> p k t", k=KT)
        wbd = w_(10272, 1024).rearrange("p (c n) -> p c n", c=8)
        th = w_(11296, 1024).rearrange("p (c t) -> p c t", c=4)
        xsT = w_(0, 8 * NPAD).rearrange("p (k s) -> p k s", k=KT)
        ysT = w_(8 * NPAD, 8 * NPAD).rearrange("p (k s) -> p k s", k=KT)
        XW = 16 * NPAD
        xw = w_(XW, 1536).rearrange("p (b k s) -> p b k s", b=3, k=KT)
        hb = w_(XW + 1536, 768).rearrange("p (b m s) -> p b m s", b=3, m=4)
        selT = w_(XW + 2304, 1024).rearrange("p (s t) -> p s t", s=4)
        moe_xT = w_(8 * NPAD, 2048).rearrange("p (k t) -> p k t", k=KT)
        pick = w_(8 * NPAD + 2048, 1024).rearrange("p (t s) -> p t s", t=NT)
        selw = w_(8 * NPAD + 3072, 1024).rearrange("p (t s) -> p t s", t=NT)
        wr = w_(8 * NPAD + 4096, 288).rearrange("p (k n) -> p k n", k=KT)
        seltmp = w_(XW, 512)
        rt = w_(XW + 1536, 768)
        ys = w_(0, 4096).rearrange("p (s d) -> p s d", s=4)
        xT1 = w_(0, 2048).rearrange("p (k t) -> p k t", k=KT)
        z = w_(2048, 3584).rearrange("p (t c) -> p t c", t=NT)
        kd = w_(5632, 4096).rearrange("p (n t g u d) -> p n t g u d", n=4, t=NT, g=NKV, u=2)
        rtmp = w_(9728, 512)
        glw = w_(10240, 384).rearrange("p (k n) -> p k n", k=KT)
        w2k = w_(10624, 256).rearrange("p (m n) -> p m n", m=2)
        w2v = w_(10880, 128).rearrange("p (m n) -> p m n", m=2)
        pe_ = w_(11008, 32).rearrange("p (n k) -> p n k", n=2)
        CT2 = [(0, 1024), (1024, 1024)]
        blk = [w_(5632 + 960 * n, 960).rearrange("p (k g b) -> p k g b", k=16, g=NKV) for n in range(2)]
        hT = w_(11360, 240).rearrange("p (n m c) -> p n m c", n=2, m=2)
        kcT = w_(11040, 60)
        vcmp = w_(11100, 256, 15)
        kT = [w_(1024 * n, 1024).rearrange("p (g t) -> p g t", g=NKV) for n in range(2)]
        qT = w_(7680, 2048).rearrange("p (k t) -> p k t", k=KT)
        P = w_(2048, 1024).rearrange("p (n s) -> p n s", n=2)
        pc = w_(3840, 512).rearrange("p (t h c) -> p t h c", t=NT, h=NH)
        PT = w_(9728, 1280).rearrange("p (n s) -> p n s", n=2)
        o = w_(5632, 2048).rearrange("p (t c) -> p t c", t=NT)
        oT = w_(0, 2048).rearrange("p (k t) -> p k t", k=KT)
        GB = [[0, XW], [7680, XW]]

        S = {n: sem(n) for n in (
            "xT_loaded consts_loaded x_loaded params_loaded router_loaded rbias_loaded gb_loaded "
            "l1small_loaded pads_zeroed z0_done z0_act z0_dve xc_ready softplus_e softplus_done gate_ps gate_sig "
            "lru_T lru_T_used lru_m2 lru_mult lru_exp ylru_ready resid_ps var_ready sd_ready x_ready xT_ps xT_evac "
            "router_ps gneg_ready gexp_done eneg_ready eexp_done assign_ready pos_ps pick_ready selw_ready "
            "gather_ps gather_act gather_dve selT_ps selT_evac y_zeroed offs_ready xw_ready gate_used gateup_done "
            "silu_done h_ready down_done y_added ysT_ps ys_act ys_dve dve_step pool_step act_step "
            "z1_done z1_evac z1_rope kdup_done ct_ps ct_evac blk_ready cmp1_done cmp1_gelu cmp2_done cmp2_evac kT_ps kT_evac "
            "qT_ps qT_evac sc_cmp pc_sub pc_exp pc_ready sc_done nm_ready p_exp rs_ready p_norm pt_ps pt_evac ptc_evac pv_done "
            "o_evac oT_ps oT_evac out_done").split()}
        full = [sem(f"ring_full{i}") for i in range(RING)]
        ovf = [{n: sem(f"ovf{L}_{n}") for n in "gate_in up_in down_in mask xw gu silu h down y".split()} for L in range(2)]

        block = ctx.enter_context(nc.Block())

        def slot_of(n):
            return n % RING

        def arrived(n):
            return 16 * (n // RING + 1)

        def gb_view(L, which):
            lo = GB[L][which]
            return w_(lo, 1024), w_(lo + 1024, 1024)

        class Steps:
            def __init__(self, eng, s):
                self.eng, self.s, self.n, self.off = eng, s, 0, 0

            def step(self, ins):
                ins.then_inc(self.s, 1)
                self.n += 1

            def settle(self):
                self.eng.wait_ge(self.s, self.off + self.n)

        @block.sync
        def _(sp):
            def load(n, src):
                dst = ring[:, slot_of(n), :].rearrange("p (k c) -> p k c", k=src.shape[1])
                sp.dma_start(dst, src).then_inc(full[slot_of(n)], 16)

            def cols(w, lo, width):
                return w[:, lo:lo + width].rearrange("(k p) c -> p k c", p=128)

            def expert_srcs(L, e):
                g, u, d = a[f"l{L}_expert_w_gate"], a[f"l{L}_expert_w_up"], a[f"l{L}_expert_w_down"]
                if type(e) is int:
                    return [w[e].rearrange("(k p) c -> p k c", p=128) for w in (g, u, d)]
                return [w[bass.ds(e, 1)].rearrange("o (k p) c -> p (o k) c", p=128) for w in (g, u, d)]

            sp.dma_start(xT0, a["xT"].rearrange("(k p) t -> p k t", p=128)).then_inc(S["xT_loaded"], 16)
            for L in range(2):
                base = MIX_BASE[L]
                for n in range(L0_UNITS if L == 0 else L1_UNITS):
                    if L == 0:
                        src = cols(a["l0_w_in"], L0_COLS[n], 512) if n < 5 else cols(a["l0_w_out"], 512 * (n - 5), 512)
                    else:
                        prev = base + n - RING - EXP_BASE[0]
                        used = ("gate_used", "gateup_done", "down_done")[prev % 3]
                        sp.wait_ge(S[used], prev // 3 + 1)
                        if n < 5:
                            src = cols(a["l1_w_in"], 512 * n, 512)
                        elif n < 7:
                            src = cols(a["l1_cmp_k_w1" if n == 5 else "l1_cmp_v_w1"], 0, 256)
                        else:
                            src = cols(a["l1_w_out"], 512 * (n - 7), 512)
                    load(base + n, src)
                for e in range(3):
                    for k, src in enumerate(expert_srcs(L, e)):
                        n = EXP_BASE[L] + 3 * e + k
                        m = n - RING - MIX_BASE[L]
                        if m >= 0:
                            if L == 0:
                                sp.wait_ge(*((S["z0_done"], 2 * m + 2) if m < 5 else (S["resid_ps"], 2 * (m - 4))))
                            else:
                                sp.wait_ge(*((S["z1_done"], 2 * m + 2) if m < 5 else
                                             (S["cmp1_done"], m - 4) if m < 7 else (S["resid_ps"], 8 + 2 * (m - 6))))
                        load(n, src)

                def expert_loads(e, r):
                    for k, src in enumerate(expert_srcs(L, e)):
                        used = ("gate_used", "gateup_done", "down_done")[k]
                        sp.wait_ge(S[used], NE * L + e - 2)
                        load(EXP_BASE[L] + 3 * r + k, src)
                with sp.Fori(0, 9) as i:
                    for r in range(3):
                        e = sp.snap(i * 3 + 3 + r)
                        expert_loads(e, r)
                for e in (30, 31):
                    expert_loads(e, e % 3)
                sp.wait_ge(S["offs_ready"], L + 1)
                most = sp.value_load(mxi[0:1, 0:1], min_val=0, max_val=SEQ)
                with sp.If(most > WIN):
                    v = ovf[L]
                    sp.wait_ge(S["down_done"], NE * L + NE)

                    def again(e):
                        srcs = expert_srcs(L, e)
                        if not (type(e) is int and e == 0):
                            sp.wait_ge(v["down"], e * (NWIN - 1))
                        for k, src in enumerate(srcs):
                            dst = ring[:, slot_of(EXP_BASE[L] + k), :].rearrange("p (k c) -> p k c", k=src.shape[1])
                            sp.dma_start(dst, src).then_inc(v[("gate_in", "up_in", "down_in")[k]], 16)
                    again(0)
                    with sp.Fori(1, NE) as e:
                        again(sp.snap(e + 0))
                    sp.wait_ge(v["down"], NE * (NWIN - 1))
            for t in range(NT):
                sp.wait_ge(S["x_ready"], 6 + t + 1)
                sp.dma_start(out[0, 128 * t:128 * (t + 1), :], x_tok[:, t, :]).then_inc(S["out_done"], 16)
            sp.wait_ge(S["out_done"], 32)

        @block.gpsimd
        def _(pool):
            pool.memset(xl[:, :, 0:3], 0.0).then_inc(S["pads_zeroed"], 1)
            pool.memset(cghc[:, :, 0:2], 0.0).then_inc(S["pads_zeroed"], 1)

            def bcast(src, n):
                return src.rearrange("(o n) -> o n", o=1).to_broadcast([128, n])

            def load_gb(L, which):
                g, b = gb_view(L, which)
                k = f"l{L}_ln{which + 1}"
                pool.dma_start(g, bcast(a[k + "_g"], D)).then_inc(S["gb_loaded"], 16)
                pool.dma_start(b, bcast(a[k + "_b"], D)).then_inc(S["gb_loaded"], 16)

            for L in range(2):
                if L == 1:
                    pool.wait_ge(S["x_ready"], 4)
                    pool.dma_start(glw, a["l1_w_in"][:, 2560:2608].rearrange("(k p) c -> p k c", p=128)).then_inc(S["l1small_loaded"], 16)
                    for u in range(2):
                        pool.dma_start(w2k[:, :, 64 * u:64 * u + 64], a["l1_cmp_k_w2"].rearrange("(m p) c -> p m c", p=128)).then_inc(S["l1small_loaded"], 16)
                    pool.dma_start(w2v, a["l1_cmp_v_w2"].rearrange("(m p) c -> p m c", p=128)).then_inc(S["l1small_loaded"], 16)
                    pool.dma_start(pe_, a["pe"]).then_inc(S["l1small_loaded"], 16)
                    pool.dma_start(catt, a["att_consts"]).then_inc(S["l1small_loaded"], 16)
                    for n in range(2 * NH):
                        N = 128 * (n // NH + 1)
                        pool.wait_ge(S["rs_ready"], n + 1)
                        pv = P[:, n % 2, 0:2 * N].rearrange("p (b s) -> p b s", b=2)
                        pool.tensor_tensor(pv, pv, arec[:, n % 2, :].unsqueeze(2).to_broadcast([128, 2, N]), ALU.mult).then_inc(S["p_norm"], 1)
                    pool.wait_ge(S["sc_done"], 2 * NH)
                    pool.wait_ge(S["pv_done"], 2 * NH)
                else:
                    pool.wait_ge(S["z0_done"], 10)
                load_gb(L, 0)
                pool.wait_ge(S["x_ready"], 4 * L + 2)
                pool.dma_start(wr, a[f"wr{L}"].rearrange("(k p) n -> p k n", p=128)).then_inc(S["router_loaded"], 16)
                pool.dma_start(rbias[:, :], bcast(a[f"br{L}"], 36)).then_inc(S["rbias_loaded"], 16)
                pool.memset(xsT[:, :, NSLOT:NPAD], 0.0).then_inc(S["pads_zeroed"], 1)
                pool.wait_ge(S["gather_ps"], 8 * (L + 1))
                pool.wait_ge(S["selT_ps"], 2 * (L + 1))
                pool.memset(w_(8 * NPAD, 8 * NPAD), 0.0).then_inc(S["y_zeroed"], 1)
                pool.wait_ge(S["y_added"], NE * (L + 1))
                pool.wait_ge(S["down_done"], NE * (L + 1))
                most = pool.value_load(mxi[0:1, 0:1], min_val=0, max_val=SEQ)
                with pool.If(most > WIN):
                    pool.wait_ge(ovf[L]["y"], NE * (NWIN - 1))
                load_gb(L, 1)

        @block.tensor
        def _(pe):
            mm, tr = nc.tensor.matmul, nc.tensor.transpose

            def unit(n, k=KT):
                pe.wait_ge(full[slot_of(n)], arrived(n))
                return ring[:, slot_of(n), :].rearrange("p (k c) -> p k c", k=k)

            def transpose_x(q, dep, count, src, s_ps):
                for t in range(NT):
                    pe.wait_ge(dep, count + t)
                    for hf in range(2):
                        for c in range(4):
                            last = tr(bank[4 + 2 * t + hf][:, 128 * c:128 * c + 128],
                                      src[:, t, 512 * hf + 128 * c:512 * hf + 128 * c + 128], ident)
                        last.then_inc(s_ps, 1)

            def project_out(L, src):
                for h in range(2):
                    w = unit(MIX_BASE[L] + (5 if L == 0 else 7) + h)
                    for t in range(NT):
                        for k in range(KT):
                            last = mm(bank[2 * t + h][:, :], src[:, k, 128 * t:128 * t + 128], w[:, k, :],
                                      start=(k == 0), stop=(k == KT - 1))
                        last.then_inc(S["resid_ps"], 1)

            def mixer0():
                pe.wait_ge(S["xT_loaded"], 16)
                for u in range(5):
                    w = unit(u)
                    if u >= 2:
                        pe.wait_ge(S["z0_act"], 2 * (u - 1))
                    for m in range(4):
                        for k in range(KT):
                            last = mm(bank[2 * (u % 2) + m // 2][:, 256 * (m % 2):256 * (m % 2) + 256],
                                      w[:, k, 128 * m:128 * m + 128], xT0[:, k, :], start=(k == 0), stop=(k == KT - 1))
                        if m % 2:
                            last.then_inc(S["z0_done"], 1)
                    if u == 1:
                        pe.wait_ge(S["params_loaded"], 32)
                        pe.wait_ge(S["xc_ready"], 4)
                        for g in range(8):
                            last = mm(bank[4 + g // 2][:, 256 * (g % 2):256 * (g % 2) + 256], wbd[:, g, :], xc[:, g % 4, :],
                                      start=True, stop=True)
                            if g % 2:
                                last.then_inc(S["gate_ps"], 1)
                pe.wait_ge(S["ylru_ready"], 4)
                pe.wait_ge(S["z0_dve"], 4)
                project_out(0, yT)

            def mixer1():
                transpose_x(1, S["x_ready"], 3, x_tok, S["xT_ps"])
                pe.wait_ge(S["xT_evac"], 4 * 2)
                for c in range(5):
                    w = unit(MIX_BASE[1] + c)
                    for t in range(NT):
                        if c >= 2:
                            pe.wait_ge(S["z1_evac"], 2 * (c - 2) + t + 1)
                        for k in range(KT):
                            last = mm(bank[2 * (c % 2) + t][:, :], xT1[:, k, 128 * t:128 * t + 128], w[:, k, :],
                                      start=(k == 0), stop=(k == KT - 1))
                        last.then_inc(S["z1_done"], 1)
                pe.wait_ge(S["l1small_loaded"], 96)
                for t in range(NT):
                    for k in range(KT):
                        last = mm(bank[4][:, 64 * t:64 * t + GL], xT1[:, k, 128 * t:128 * t + 128], glw[:, k, :],
                                  start=(k == 0), stop=(k == KT - 1))
                last.then_inc(S["z1_done"], 1)
                pe.wait_ge(S["z1_evac"], 11)
                for n in range(2):
                    for t in range(NT):
                        if n == 0:
                            pe.wait_ge(S["kdup_done"], t + 1)
                        if n == 1:
                            pe.wait_ge(S["ct_evac"], t + 1)
                        for g in range(NKV):
                            last = tr(bank[5 + t][:, 128 * g:128 * g + 128], kd[:, n, t].rearrange("p g u d -> p g (u d)")[:, g, :], ident)
                        last.then_inc(S["ct_ps"], 1)
                for n in range(2):
                    w = unit(MIX_BASE[1] + 5 + n, 16)
                    pe.wait_ge(S["blk_ready"], n + 1)
                    for m in range(2):
                        for k in range(16):
                            last = mm(bank[7][:, 128 * n + 64 * m:128 * n + 64 * m + 60], w[:, k, 128 * m:128 * m + 128],
                                      blk[n][:, k].rearrange("p g b -> p (g b)"), start=(k == 0), stop=(k == 15))
                    last.then_inc(S["cmp1_done"], 1)
                for n in range(2):
                    for t in range(NT):
                        pe.wait_ge(S["kdup_done"], 2 * (n + 1) + t + 1)
                        b = 2 * n + t
                        if b == 0:
                            pe.wait_ge(S["z1_evac"], 11)
                        for g in range(NKV):
                            last = tr(bank[b][:, 128 * g:128 * g + 128], kd[:, 2 + n, t].rearrange("p g u d -> p g (u d)")[:, g, :], ident)
                        last.then_inc(S["kT_ps"], 1)
                pe.wait_ge(S["cmp1_gelu"], 4)
                for m in range(2):
                    mm(bank[4][:, 0:60], w2k[:, m, :], hT[:, 0, m, :], start=(m == 0), stop=(m == 1))
                for g in range(NKV):
                    for m in range(2):
                        last = mm(bank[4][0:NBLK, 64 + 64 * g:128 + 64 * g], hT[:, 1, m, NBLK * g:NBLK * g + NBLK], w2v[:, m, :],
                                  start=(m == 0), stop=(m == 1))
                last.then_inc(S["cmp2_done"], 1)
                for t in range(NT):
                    pe.wait_ge(S["z1_rope"], 2 + 2 * t)
                    for hf in range(2):
                        b = 2 * t + hf
                        pe.wait_ge(S["kT_evac"], b + 1)
                        for c in range(4):
                            last = tr(bank[b][:, 128 * c:128 * c + 128], z[:, t, 512 * hf + 128 * c:512 * hf + 128 * c + 128], ident)
                        last.then_inc(S["qT_ps"], 1)
                pe.wait_ge(S["qT_evac"], 4)
                pe.wait_ge(S["cmp2_evac"], 2)
                pe.wait_ge(S["ct_evac"], 4)
                for par_ in range(2):
                    lo = 64 * par_
                    for t in range(NT):
                        for j in range(8):
                            g = (2 * j + par_) // 4
                            last = mm(bank[5 + par_][:, 128 * t + 16 * j:128 * t + 16 * j + NBLK],
                                      qT[lo:lo + 64, j, 128 * t:128 * t + 128], kcT[lo:lo + 64, NBLK * g:NBLK * g + NBLK],
                                      start=True, stop=True)
                    last.then_inc(S["sc_cmp"], 1)

                def scores(n):
                    t, h = n // NH, n % NH
                    N, lo, g = 128 * (t + 1), 64 * (h % 2), h // 4
                    if n >= 2:
                        pe.wait_ge(S["p_exp"], 2 * (n - 1))
                    for b in range(2):
                        last = mm(bank[n % 2][:, b * N:b * N + N], qT[lo:lo + 64, h // 2, 128 * t:128 * t + 128],
                                  kT[b][lo:lo + 64, g, 0:N], start=True, stop=True)
                    last.then_inc(S["sc_done"], 1)

                def turn(n):
                    t, h = n // NH, n % NH
                    N = 128 * (t + 1)
                    pe.wait_ge(S["p_norm"], n + 1)
                    if n >= 2:
                        pe.wait_ge(S["pt_evac"], n - 1)
                        pe.wait_ge(S["ptc_evac"], n - 1)
                    for kb in range(2 * (t + 1)):
                        tr(bank[2 + n % 2][:, 128 * kb:128 * kb + 128], P[:, n % 2, 128 * kb:128 * kb + 128], ident)
                    if n == 0:
                        pe.wait_ge(S["pc_ready"], 1)
                    tr(bank[4 if n % 2 else 7][0:NBLK, 0:128], pc[:, t, h, 0:NBLK], ident).then_inc(S["pt_ps"], 1)

                def values(n):
                    t, h = n // NH, n % NH
                    g, kb = h // 4, t + 1
                    ob = bank[(5, 6)[(n // 8) % 2]][:, 64 * (n % 8):64 * (n % 8) + 64]
                    pe.wait_ge(S["pt_evac"], n + 1)
                    pe.wait_ge(S["ptc_evac"], n + 1)
                    if n % 8 == 0 and n >= 16:
                        pe.wait_ge(S["o_evac"], n // 8 - 1)
                    pt = PT[:, n % 2, :]
                    mm(ob, pt[0:NBLK, 512:640], vcmp[0:NBLK, 64 * g:64 * g + 64], start=True, stop=False)
                    for b in range(2):
                        for k in range(kb):
                            i = b * kb + k
                            last = mm(ob, pt[:, 128 * i:128 * i + 128], z[:, k, 1280 + 256 * b + 64 * g:1280 + 256 * b + 64 * g + 64],
                                      start=False, stop=(i == 2 * kb - 1))
                    last.then_inc(S["pv_done"], 1)

                scores(0)
                scores(1)
                for n in range(2 * NH):
                    turn(n)
                    if n + 2 < 2 * NH:
                        scores(n + 2)
                    if n:
                        values(n - 1)
                values(2 * NH - 1)
                for t in range(NT):
                    for hf in range(2):
                        pe.wait_ge(S["o_evac"], 2 * t + hf + 1)
                        b = 2 * t + hf
                        if b == 0:
                            pe.wait_ge(S["pt_evac"], 2 * NH)
                        for c in range(4):
                            last = tr(bank[(2, 3, 4, 7)[b]][:, 128 * c:128 * c + 128], o[:, t, 512 * hf + 128 * c:512 * hf + 128 * c + 128], ident)
                        last.then_inc(S["oT_ps"], 1)
                pe.wait_ge(S["oT_evac"], 4)
                project_out(1, oT)

            def moe(L):
                transpose_x(0, S["x_ready"], 4 * L + 1, x_tok, S["xT_ps"])
                pe.wait_ge(S["router_loaded"], 16 * (L + 1))
                pe.wait_ge(S["xT_evac"], 4 * (2 * L + 1))
                for t in range(NT):
                    for k in range(KT):
                        last = mm(bank[0][:, 64 * t:64 * t + 36], moe_xT[:, k, 128 * t:128 * t + 128], wr[:, k, :],
                                  start=(k == 0), stop=(k == KT - 1))
                last.then_inc(S["router_ps"], 1)
                am = rt[:, 256:320].rearrange("p (t e) -> p t e", t=NT)
                pe.wait_ge(S["assign_ready"], L + 1)
                mm(bank[1][:, 0:32], upper, am[:, 0, :], start=True, stop=True)
                mm(bank[1][:, 32:64], upper, am[:, 1, :], start=True, stop=False)
                mm(bank[1][:, 32:64], ones, am[:, 0, :], start=False, stop=True)
                mm(bank[1][:, 64:96], ones, am[:, 0, :], start=True, stop=False)
                mm(bank[1][:, 64:96], ones, am[:, 1, :], start=False, stop=True).then_inc(S["pos_ps"], 1)
                pe.wait_ge(S["pick_ready"], L + 1)
                for c in range(KT):
                    for t in range(NT):
                        last = mm(bank[(2 + c) % 8][:, :], x_tok[:, t, 128 * c:128 * c + 128], pick[:, t, :],
                                  start=(t == 0), stop=(t == NT - 1))
                    last.then_inc(S["gather_ps"], 1)
                pe.wait_ge(S["selw_ready"], L + 1)
                pe.wait_ge(S["gather_act"], 4 * L + 1)
                pe.wait_ge(S["gather_dve"], 4 * L + 1)
                for t in range(NT):
                    for s in range(4):
                        last = tr(bank[2 + t][:, 128 * s:128 * s + 128], selw[:, t, 128 * s:128 * s + 128], ident)
                    last.then_inc(S["selT_ps"], 1)
                pe.wait_ge(S["gather_act"], 4 * L + 4)
                pe.wait_ge(S["gather_dve"], 4 * L + 4)
                pe.wait_ge(S["selT_evac"], 2 * L + 2)

                def gate_up(w, xin, b, s_gate, s_up):
                    for i in range(2):
                        wv = w[i]()
                        for m in range(4):
                            for k in range(KT):
                                last = mm(b[:, 256 * i + WIN * m:256 * i + WIN * m + WIN], wv[:, k, 128 * m:128 * m + 128],
                                          xin[:, k, :], start=(k == 0), stop=(k == KT - 1))
                        if i == 0 and s_gate is not None:
                            last.then_inc(s_gate, 1)
                    last.then_inc(s_up, 1)

                def down(wv, hin, b, s):
                    for m in range(KT):
                        for k in range(4):
                            last = mm(b[:, WIN * m:WIN * m + WIN], wv[:, k, 128 * m:128 * m + 128], hin[:, k, :],
                                      start=(k == 0), stop=(k == 3))
                    last.then_inc(s, 1)

                def in_loop(n0, i):
                    s = slot_of(n0)

                    def get(k=KT):
                        pe.wait_ge(full[s], i * 16 + arrived(n0))
                        return ring[:, s, :].rearrange("p (k c) -> p k c", k=k)
                    return get

                def expert_in(e, r, i):
                    pe.wait_ge(S["xw_ready"], NE * L + e + 1)
                    if not (type(e) is int and e == 0):
                        pass
                    gate_up([in_loop(EXP_BASE[L] + 3 * r + k, i) for k in range(2)], xw[:, r % 3], bank[2 + r % 3],
                            S["gate_used"], S["gateup_done"])

                def expert_out(e, r, i):
                    pe.wait_ge(S["h_ready"], NE * L + e + 1)
                    wv = in_loop(EXP_BASE[L] + 3 * r + 2, i)(4)
                    down(wv, hb[:, r % 3], bank[5 + r % 3], S["down_done"])

                expert_in(0, 0, 0)
                with pe.Fori(0, 10) as i:
                    for r in range(1, 4):
                        expert_in(i * 3 + r, r, i)
                        expert_out(i * 3 + (r - 1), r - 1, i)
                expert_in(31, 31, 0)
                expert_out(30, 30, 0)
                expert_out(31, 31, 0)
                most = pe.value_load(mxi[0:1, 0:1], min_val=0, max_val=SEQ)
                with pe.If(most > WIN):
                    v = ovf[L]
                    with pe.Fori(0, NE) as e:
                        pe.wait_ge(v["gate_in"], e * 16 + 16)
                        pe.wait_ge(v["up_in"], e * 16 + 16)
                        pe.wait_ge(v["down_in"], e * 16 + 16)
                        wg, wu = [ring[:, slot_of(EXP_BASE[L] + k), :].rearrange("p (k c) -> p k c", k=KT) for k in range(2)]
                        wd = ring[:, slot_of(EXP_BASE[L] + 2), :].rearrange("p (k c) -> p k c", k=4)
                        for w in range(1, NWIN):
                            pe.wait_ge(v["xw"], e * (NWIN - 1) + w)
                            gate_up([lambda: wg, lambda: wu], xw[:, 0], bank[2], None, v["gu"])
                            pe.wait_ge(v["h"], e * (NWIN - 1) + w)
                            down(wd, hb[:, 0], bank[5], v["down"])
                    pe.wait_ge(v["y"], NE * (NWIN - 1))
                pe.wait_ge(S["y_added"], NE * L + NE)
                for s in range(4):
                    for hf in range(2):
                        q = 2 * s + hf
                        if q >= 4:
                            pe.wait_ge(S["ys_act" if q % 2 == 0 else "ys_dve"], 4 * L + (q - 4) // 2 + 1)
                        for c in range(4):
                            last = tr(bank[4 + q % 4][:, 128 * c:128 * c + 128], ysT[:, 4 * hf + c, 128 * s:128 * s + 128], ident)
                        last.then_inc(S["ysT_ps"], 1)
                for s in range(4):
                    pe.wait_ge(S["ys_act"], 4 * L + s + 1)
                    pe.wait_ge(S["ys_dve"], 4 * L + s + 1)
                    for h in range(2):
                        for t in range(NT):
                            last = mm(bank[2 * t + h][:, :], selT[:, s, 128 * t:128 * t + 128], ys[:, s, 512 * h:512 * h + 512],
                                      start=(s == 0), stop=(s == 3))
                            if s == 3:
                                last.then_inc(S["resid_ps"], 1)

            pe.wait_ge(S["consts_loaded"], 16)
            mixer0()
            moe(0)
            mixer1()
            moe(1)

        @block.scalar
        def _(act):
            fn = nc.scalar.activation
            act.dma_start(par[:, :], a["params"]).then_inc(S["params_loaded"], 16)
            act.dma_start(wbd, a["wbd"]).then_inc(S["params_loaded"], 16)
            act.dma_start(cst[:, :], a["consts"]).then_inc(S["consts_loaded"], 16)
            act.dma_start(x_tok[:, :, :], a["x"][0].rearrange("(t p) d -> p t d", p=128)).then_inc(S["x_loaded"], 16)

            def evac_T(dst, s_ps, base, s_done, banks=(4, 5, 6, 7)):
                for t in range(NT):
                    for hf in range(2):
                        act.wait_ge(s_ps, base + 2 * t + hf + 1)
                        fn(dst[:, 4 * hf:4 * hf + 4, 128 * t:128 * t + 128],
                           bank[banks[2 * t + hf]][:, :].rearrange("p (c t) -> p c t", c=4), ACT.Copy).then_inc(s_done, 1)

            def layernorm(q):
                act.wait_ge(S["consts_loaded"], 16)
                act.wait_ge(S["var_ready"], 2 * (q + 1))
                fn(sd[:, :], mv[:, :, 1], ACT.Sqrt, bias=eps).then_inc(S["sd_ready"], 1)

            def mixer0():
                act.wait_ge(S["softplus_e"], 1)
                fn(sp_t[:, 2, :], sp_t[:, 1, :], ACT.Exp, scale=-1.0).then_inc(S["act_step"], 1)
                act.wait_ge(S["pads_zeroed"], 1)
                for b in range(2):
                    act.wait_ge(S["z0_done"], b + 1)
                    fn(xl[:, 2 * b:2 * b + 2, 3:259], bank[b][:, :].rearrange("p (c t) -> p c t", c=2), ACT.Copy).then_inc(S["z0_act"], 1)
                for b in range(2):
                    act.wait_ge(S["z0_done"], 2 + b + 1)
                    fn(gate[:, 2 * b:2 * b + 2, :], bank[2 + b][:, :].rearrange("p (c t) -> p c t", c=2), ACT.Gelu_apprx_tanh).then_inc(S["z0_act"], 1)
                for g in range(8):
                    act.wait_ge(S["gate_ps"], g // 2 + 1)
                    dst = (rg if g < 4 else ig)[:, g % 4, :]
                    bias = par[:, (P_BA if g < 4 else P_BX) + g % 4:(P_BA if g < 4 else P_BX) + g % 4 + 1]
                    fn(dst, bank[4 + g // 2][:, 256 * (g % 2):256 * (g % 2) + 256], ACT.Sigmoid, bias=bias).then_inc(S["gate_sig"], 1)
                act.wait_ge(S["softplus_done"], 1)
                act.wait_ge(S["gate_sig"], 8)
                for c in range(4):
                    fn(th[:, c, :], rg[:, c, :], ACT.Tanh, scale=sp_t[:, 4, c:c + 1]).then_inc(S["lru_T"], 1)
                act.wait_ge(S["lru_T"], 4)
                for c in range(4):
                    fn(rg[:, c, :], rg[:, c, :], ACT.Exp, scale=sp_t[:, 5, c:c + 1]).then_inc(S["lru_exp"], 1)
                act.wait_ge(S["lru_m2"], 1)
                fn(th[:, :, :], th[:, :, :], ACT.Sqrt, scale=2.0).then_inc(S["lru_mult"], 1)
                act.wait_ge(S["pads_zeroed"], 2)
                for b in range(2):
                    act.wait_ge(S["z0_done"], 4 + b + 1)
                    fn(cghc[:, 2 * b:2 * b + 2, 2:258], bank[b][:, :].rearrange("p (c t) -> p c t", c=2), ACT.Copy).then_inc(S["z0_act"], 1)

            def mixer1():
                evac_T(xT1, S["xT_ps"], 4, S["xT_evac"])
                for c in range(5):
                    for t in range(NT):
                        act.wait_ge(S["z1_done"], 2 * c + t + 1)
                        bk = bank[2 * (c % 2) + t]
                        if c < 2:
                            fn(z[:, t, 512 * c:512 * c + 512], bk[:, :], ACT.Copy).then_inc(S["z1_evac"], 1)
                            continue
                        if c > 2:
                            act.wait_ge(S["z1_rope"], 4 + 2 * (c - 3) + t + 1)
                        if c == 2:
                            src = bk[:, 256:512].rearrange("p (g d) -> p g d", g=NKV)
                            for u in range(2):
                                fn(kd[:, 1, t, :, u, :], src, ACT.Copy).then_inc(S["act_step"], 1)
                        else:
                            fn(z[:, t, 1280 + 256 * (c - 3):1536 + 256 * (c - 3)], bk[:, 256:512], ACT.Copy).then_inc(S["act_step"], 1)
                        fn(z[:, t, 1024:1280], bk[:, 0:256], ACT.Copy).then_inc(S["z1_evac"], 1)
                act.wait_ge(S["z1_done"], 11)
                fn(gates[:, :, :], bank[4][:, 0:128].rearrange("p (t c) -> p t c", t=NT)[:, :, 0:GL], ACT.Sigmoid).then_inc(S["z1_evac"], 1)
                for n in range(2):
                    lo = CT2[n][0]
                    for t in range(NT):
                        act.wait_ge(S["ct_ps"], 2 * n + t + 1)
                        v0 = w_(lo, 1024, 64).rearrange("p (g t) -> p g t", g=NKV)
                        v1 = w_(lo, 1024, 64, 64).rearrange("p (g t) -> p g t", g=NKV)
                        src = bank[5 + t][:, :].rearrange("p (g t) -> p g t", g=NKV)
                        s0 = 1 - t
                        fn(v1[:, :, 128 * t - 1 + s0:128 * t + 127], src[64:128, :, s0:128], ACT.Copy).then_inc(S["act_step"], 1)
                        fn(v0[:, :, 128 * t:128 * t + 128], src[0:64, :, :], ACT.Copy).then_inc(S["ct_evac"], 1)
                act.wait_ge(S["blk_ready"], 2)
                for n in range(2):
                    for t in range(NT):
                        act.wait_ge(S["kT_ps"], 2 * n + t + 1)
                        fn(kT[n][:, :, 128 * t:128 * t + 128], bank[2 * n + t][:, :].rearrange("p (g t) -> p g t", g=NKV), ACT.Copy).then_inc(S["kT_evac"], 1)
                for n in range(2):
                    for m in range(2):
                        act.wait_ge(S["cmp1_done"], 2)
                        fn(hT[:, n, m, :], bank[7][:, 128 * n + 64 * m:128 * n + 64 * m + 60], ACT.Gelu_apprx_tanh).then_inc(S["cmp1_gelu"], 1)
                act.wait_ge(S["cmp2_done"], 1)
                fn(kcT, bank[4][:, 0:60], ACT.Copy).then_inc(S["cmp2_evac"], 1)
                fn(vcmp, bank[4][0:NBLK, 64:320], ACT.Copy).then_inc(S["cmp2_evac"], 1)
                for t in range(NT):
                    for hf in range(2):
                        act.wait_ge(S["qT_ps"], 2 * t + hf + 1)
                        fn(qT[:, 4 * hf:4 * hf + 4, 128 * t:128 * t + 128],
                           bank[2 * t + hf][:, :].rearrange("p (c t) -> p c t", c=4), ACT.Copy).then_inc(S["qT_evac"], 1)
                act.wait_ge(S["pc_sub"], 1)
                fn(pc[:, :, :, 0:NBLK], pc[:, :, :, 0:NBLK], ACT.Exp).then_inc(S["pc_exp"], 1)

                def exps(n):
                    N = 128 * (n // NH + 1)
                    act.wait_ge(S["nm_ready"], n + 1)
                    if n >= 2:
                        act.wait_ge(S["pt_ps"], n - 1)
                    for b in range(2):
                        fn(P[:, n % 2, b * N:b * N + N], bank[n % 2][:, b * N:b * N + N], ACT.Exp, scale=SCALE,
                           bias=asm[:, n % 2, 2 + b:3 + b], accum_out=asm[:, n % 2, 4 + b:5 + b]).then_inc(S["p_exp"], 1)

                def evac(n):
                    N = 256 * (n // NH + 1)
                    act.wait_ge(S["pt_ps"], n + 1)
                    if n >= 2:
                        act.wait_ge(S["pv_done"], n - 1)
                    fn(PT[:, n % 2, 0:N], bank[2 + n % 2][:, 0:N], ACT.Copy).then_inc(S["pt_evac"], 1)

                exps(0)
                exps(1)
                for n in range(2 * NH):
                    evac(n)
                    if n + 2 < 2 * NH:
                        exps(n + 2)
                evac_T(oT, S["oT_ps"], 0, S["oT_evac"], (2, 3, 4, 7))

            def moe(L):
                evac_T(moe_xT, S["xT_ps"], 8 * L, S["xT_evac"])
                for t in range(NT):
                    act.wait_ge(S["gneg_ready"], L + 1)
                    fn(rt[:, 640 + 4 * t:644 + 4 * t], rt[:, 0:72].rearrange("p (t c) -> p t c", t=NT)[:, t, 0:4], ACT.Exp,
                       bias=rt[:, 120 + t:121 + t], accum_out=rt[:, 122 + t:123 + t]).then_inc(S["gexp_done"], 1)
                for t in range(NT):
                    act.wait_ge(S["eneg_ready"], L + 1)
                    fn(rt[:, 144 + 8 * t:152 + 8 * t], rt[:, 128 + 8 * t:136 + 8 * t], ACT.Exp,
                       bias=rt[:, 160 + t:161 + t], accum_out=rt[:, 162 + t:163 + t]).then_inc(S["eexp_done"], 1)
                for c in range(0, KT, 2):
                    act.wait_ge(S["gather_ps"], 8 * L + c + 1)
                    fn(xsT[:, c, 0:NSLOT], bank[(2 + c) % 8][:, :], ACT.Copy).then_inc(S["gather_act"], 1)
                for t in range(NT):
                    act.wait_ge(S["selT_ps"], 2 * L + t + 1)
                    fn(selT[:, :, 128 * t:128 * t + 128], bank[2 + t][:, :].rearrange("p (s t) -> p s t", s=4), ACT.Copy).then_inc(S["selT_evac"], 1)

                def silu(e, r):
                    act.wait_ge(S["gateup_done"], NE * L + e + 1)
                    fn(hb[:, r % 3], bank[2 + r % 3][:, 0:256].rearrange("p (m s) -> p m s", m=4), ACT.Silu).then_inc(S["silu_done"], 1)
                silu(0, 0)
                with act.Fori(0, 10) as i:
                    for r in range(1, 4):
                        silu(i * 3 + r, r)
                silu(31, 31)
                most = act.value_load(mxi[0:1, 0:1], min_val=0, max_val=SEQ)
                with act.If(most > WIN):
                    v = ovf[L]
                    with act.Fori(0, NE) as e:
                        for w in range(1, NWIN):
                            act.wait_ge(v["gu"], e * (NWIN - 1) + w)
                            fn(hb[:, 0], bank[2][:, 0:256].rearrange("p (m s) -> p m s", m=4), ACT.Silu).then_inc(v["silu"], 1)
                for q in range(0, 8, 2):
                    act.wait_ge(S["ysT_ps"], 8 * L + q + 1)
                    fn(ys[:, q // 2, 0:512], bank[4 + q % 4][:, :], ACT.Copy).then_inc(S["ys_act"], 1)

            mixer0()
            layernorm(0)
            moe(0)
            layernorm(1)
            mixer1()
            layernorm(2)
            moe(1)
            layernorm(3)

        @block.vector
        def _(dve):
            v = nc.vector
            st = Steps(dve, S["dve_step"])
            step, settle = st.step, st.settle

            def layernorm(q):
                L, which = q // 2, q % 2
                g, b = gb_view(L, which)
                if q == 0:
                    dve.wait_ge(S["x_loaded"], 16)
                order = [(t, h) for h in range(2) for t in range(NT)]
                for n, (t, h) in enumerate(order):
                    dve.wait_ge(S["resid_ps"], 4 * q + n + 1)
                    xs = x_tok[:, t, 512 * h:512 * h + 512]
                    step(v.scalar_tensor_tensor(xs, xs, ALPHA, bank[2 * t + h][:, :], ALU.mult, ALU.add))
                settle()
                for t, h in order:
                    step(v.bn_stats(stats[:, t, h, :], x_tok[:, t, 512 * h:512 * h + 512]))
                settle()
                for t in range(NT):
                    v.bn_aggr(mv[:, t, :], stats[:, t, :, :].rearrange("p h s -> p (h s)")).then_inc(S["var_ready"], 1)
                dve.wait_ge(S["sd_ready"], q + 1)
                step(v.reciprocal(rstd[:, :], sd[:, :]))
                settle()
                for t in range(NT):
                    step(v.tensor_scalar(x_tok[:, t, :], x_tok[:, t, :], mv[:, t, 0:1], rstd[:, t:t + 1], ALU.subtract, ALU.mult))
                dve.wait_ge(S["gb_loaded"], 32 * (q + 1))
                settle()
                for t in range(NT):
                    step(v.tensor_tensor(x_tok[:, t, :], x_tok[:, t, :], g, ALU.mult))
                settle()
                for t in range(NT):
                    v.tensor_tensor(x_tok[:, t, :], x_tok[:, t, :], b, ALU.add).then_inc(S["x_ready"], 1)

            def mixer0():
                dve.wait_ge(S["params_loaded"], 32)
                lam = par[:, P_LAM:P_LAM + 4]
                step(v.tensor_scalar(sp_t[:, 0, :], lam, -1.0, 0.0, ALU.mult, ALU.max))
                step(v.tensor_scalar(sp_t[:, 3, :], lam, -1.0, None, ALU.mult))
                settle()
                v.tensor_tensor(sp_t[:, 1, :], lam, sp_t[:, 3, :], ALU.max).then_inc(S["softplus_e"], 1)
                dve.wait_ge(S["act_step"], 1)
                y, s_, s2, p = sp_t[:, 2, :], sp_t[:, 1, :], sp_t[:, 3, :], sp_t[:, 4, :]
                step(v.tensor_scalar(p, y, 2.0, None, ALU.add))
                settle()
                step(v.reciprocal(s2, p))
                settle()
                step(v.tensor_tensor(s_, y, s2, ALU.mult))
                settle()
                step(v.tensor_tensor(s2, s_, s_, ALU.mult))
                settle()
                step(v.tensor_scalar(p, s2, 1.0 / 17, 1.0 / 15, ALU.mult, ALU.add))
                for c in (13, 11, 9, 7, 5, 3, 1):
                    settle()
                    step(v.tensor_tensor(p, p, s2, ALU.mult))
                    settle()
                    step(v.tensor_scalar(p, p, 1.0 / c, None, ALU.add))
                settle()
                step(v.tensor_tensor(p, p, s_, ALU.mult))
                settle()
                step(v.scalar_tensor_tensor(s2, p, 2.0, sp_t[:, 0, :], ALU.mult, ALU.add))
                settle()
                step(v.tensor_scalar(sp_t[:, 4, :], s2, 8.0, None, ALU.mult))
                v.tensor_scalar(sp_t[:, 5, :], s2, -8.0, None, ALU.mult).then_inc(S["softplus_done"], 1)
                settle()
                for c in range(4):
                    dve.wait_ge(S["z0_act"], c // 2 + 1)
                    step(v.tensor_scalar(xc[:, c, :], xl[:, c, 0:256], par[:, P_LCONV + 4 * c:P_LCONV + 4 * c + 1],
                                         par[:, P_LCB + c:P_LCB + c + 1], ALU.mult, ALU.add))
                for k in range(1, 4):
                    settle()
                    for c in range(4):
                        ins = v.scalar_tensor_tensor(xc[:, c, :], xl[:, c, k:k + 256],
                                                     par[:, P_LCONV + 4 * c + k:P_LCONV + 4 * c + k + 1], xc[:, c, :], ALU.mult, ALU.add)
                        if k < 3:
                            step(ins)
                        else:
                            ins.then_inc(S["xc_ready"], 1)
                dve.wait_ge(S["xc_ready"], 4)
                dve.wait_ge(S["lru_T"], 4)
                m2 = yT[:, 4:8, :]
                step(v.tensor_scalar(m2, th, 1.0, None, ALU.add))
                dve.wait_ge(S["gate_sig"], 8)
                step(v.tensor_tensor(ig, ig, xc, ALU.mult))
                settle()
                step(v.reciprocal(m2, m2))
                settle()
                v.tensor_tensor(th, th, m2, ALU.mult).then_inc(S["lru_m2"], 1)
                dve.wait_ge(S["lru_mult"], 1)
                step(v.tensor_tensor(ig, ig, th, ALU.mult))
                settle()
                for c in range(4):
                    dve.wait_ge(S["lru_exp"], c + 1)
                    step(v.tensor_tensor_scan(yT[:, 4 + c, :], rg[:, c, :], ig[:, c, :], 0.0, ALU.mult, ALU.add))
                settle()
                dve.wait_ge(S["z0_act"], 4)
                for c in range(4):
                    v.tensor_tensor(yT[:, 4 + c, :], yT[:, 4 + c, :], gate[:, c, :], ALU.mult).then_inc(S["ylru_ready"], 1)
                for b in range(2):
                    dve.wait_ge(S["z0_act"], 4 + b + 1)
                    dve.wait_ge(S["z0_done"], 6 + b + 1)
                    cv = cghc[:, 2 * b:2 * b + 2, 2:258]
                    v.tensor_tensor(cv, bank[2 + b][:, :].rearrange("p (c t) -> p c t", c=2), cv, ALU.mult).then_inc(S["z0_dve"], 1)
                for c in range(4):
                    dve.wait_ge(S["z0_dve"], c // 2 + 1)
                    step(v.tensor_scalar(yT[:, c, :], cghc[:, c, 0:256], par[:, P_CONV + 3 * c:P_CONV + 3 * c + 1], None, ALU.mult))
                for k in range(1, 3):
                    settle()
                    for c in range(4):
                        step(v.scalar_tensor_tensor(yT[:, c, :], cghc[:, c, k:k + 256],
                                                    par[:, P_CONV + 3 * c + k:P_CONV + 3 * c + k + 1], yT[:, c, :], ALU.mult, ALU.add))
                settle()
                for b in range(2):
                    dve.wait_ge(S["z0_done"], 8 + b + 1)
                    yv = yT[:, 2 * b:2 * b + 2, :]
                    v.tensor_tensor(yv, bank[b][:, :].rearrange("p (c t) -> p c t", c=2), yv, ALU.mult).then_inc(S["z0_dve"], 1)

            def rotate(src, dst, t, H, s_done):
                cs = rope[:, t, 0, :].unsqueeze(1).to_broadcast([128, H, 32])
                sn = rope[:, t, 1, :].unsqueeze(1).to_broadcast([128, H, 32])
                tm = rtmp[:, 0:64 * H].rearrange("p (h d) -> p h d", h=H)
                step(v.tensor_tensor(tm[:, :, 0:32], src[:, :, 32:64], sn, ALU.mult))
                step(v.tensor_tensor(tm[:, :, 32:64], src[:, :, 0:32], sn, ALU.mult))
                settle()
                step(v.tensor_tensor(dst[:, :, 0:32], src[:, :, 0:32], cs, ALU.mult))
                step(v.tensor_tensor(dst[:, :, 32:64], src[:, :, 32:64], cs, ALU.mult))
                settle()
                step(v.tensor_tensor(dst[:, :, 0:32], dst[:, :, 0:32], tm[:, :, 0:32], ALU.subtract))
                v.tensor_tensor(dst[:, :, 32:64], dst[:, :, 32:64], tm[:, :, 32:64], ALU.add).then_inc(s_done, 1)
                settle()

            def mixer1():
                dve.wait_ge(S["l1small_loaded"], 96)
                nr = 0
                for c in range(2):
                    for t in range(NT):
                        dve.wait_ge(S["z1_evac"], 2 * c + t + 1)
                        q = z[:, t, 512 * c:512 * c + 512].rearrange("p (h d) -> p h d", d=64)
                        rotate(q, q, t, 8, S["z1_rope"])
                        nr += 1
                        dve.wait_ge(S["z1_rope"], nr)
                for c in range(2, 5):
                    n = (0, 2, 3)[c - 2]
                    for t in range(NT):
                        dve.wait_ge(S["z1_evac"], 2 * c + t + 1)
                        rotate(z[:, t, 1024:1280].rearrange("p (g d) -> p g d", d=64), kd[:, n, t, :, 0, :], t, NKV, S["z1_rope"])
                        nr += 1
                        dve.wait_ge(S["z1_rope"], nr)
                        v.tensor_copy(kd[:, n, t, :, 1, :], kd[:, n, t, :, 0, :]).then_inc(S["kdup_done"], 1)
                dve.wait_ge(S["l1small_loaded"], 96)
                for n in range(2):
                    dve.wait_ge(S["ct_evac"], 2 * n + 2)
                    if n == 0:
                        dve.wait_ge(S["ct_ps"], 4)
                    ct = w_(CT2[n][0], 1024).rearrange("p (g t) -> p g t", g=NKV)
                    for g in range(NKV):
                        lo = ct[:, g, 0:240].rearrange("p (b k u) -> p k b u", b=15, u=2)[:, :, :, 0]
                        hi = ct[:, g, 16:256].rearrange("p (b k u) -> p k b u", b=15, u=2)[:, :, :, 0]
                        for half, src in ((0, lo), (1, hi)):
                            ins = v.tensor_tensor(blk[n][:, 8 * half:8 * half + 8, g, :], src,
                                                  pe_[:, n, 8 * half:8 * half + 8].unsqueeze(2).to_broadcast([128, 8, 15]), ALU.add)
                            if g == NKV - 1 and half:
                                settle()
                                ins.then_inc(S["blk_ready"], 1)
                            else:
                                step(ins)
                dve.wait_ge(S["qT_ps"], 4)
                for par_ in range(2):
                    dve.wait_ge(S["sc_cmp"], par_ + 1)
                    src = bank[5 + par_][:, 0:256].rearrange("p (t j c) -> p t j c", t=NT, c=16)
                    dst = pc.rearrange("p t (j u) c -> p t j u c", u=2)
                    for t in range(NT):
                        step(v.scalar_tensor_tensor(dst[:, t, :, par_, 0:NBLK], src[:, t, :, 0:NBLK], SCALE,
                                                    cmp_add[:, t, 0:NBLK].unsqueeze(1).to_broadcast([128, 8, NBLK]), ALU.mult, ALU.add))
                settle()
                pv = pc[:, :, :, 0:NBLK]
                step(v.tensor_reduce(cmx[:, :, :], pv, axis=AX.X, op=ALU.max))
                settle()
                v.tensor_tensor(pv, pv, cmx[:, :, :].unsqueeze(3).to_broadcast([128, NT, NH, NBLK]), ALU.subtract).then_inc(S["pc_sub"], 1)
                dve.wait_ge(S["pc_exp"], 1)
                step(v.tensor_tensor(pv, pv, cmp_mul[:, :, 0:NBLK].unsqueeze(2).to_broadcast([128, NT, NH, NBLK]), ALU.mult))
                settle()
                step(v.tensor_reduce(cmx[:, :, :], pv, axis=AX.X, op=ALU.add))
                settle()
                step(v.tensor_scalar(cmx[:, :, :], cmx[:, :, :], TINY, None, ALU.max))
                settle()
                step(v.reciprocal(cmx[:, :, :], cmx[:, :, :]))
                settle()
                gv = gates[:, :, :].rearrange("p t (h b) -> p t h b", b=3)
                step(v.tensor_tensor(cmx[:, :, :], cmx[:, :, :], gv[:, :, :, 0], ALU.mult))
                settle()
                v.tensor_tensor(pv, pv, cmx[:, :, :].unsqueeze(3).to_broadcast([128, NT, NH, NBLK]), ALU.mult).then_inc(S["pc_ready"], 1)

                def maxes(n):
                    t = n // NH
                    N = 128 * (t + 1)
                    sc = bank[n % 2][:, 0:2 * N].rearrange("p (b s) -> p b s", b=2)
                    dve.wait_ge(S["sc_done"], n + 1)
                    diag = sc[:, :, 128 * t:128 * t + 128]
                    step(v.tensor_tensor(diag, diag, causal.unsqueeze(1).to_broadcast([128, 2, 128]), ALU.add))
                    settle()
                    step(v.tensor_reduce(asm[:, n % 2, 0:2], sc, axis=AX.X, op=ALU.max))
                    settle()
                    v.tensor_scalar(asm[:, n % 2, 2:4], asm[:, n % 2, 0:2], -SCALE, None, ALU.mult).then_inc(S["nm_ready"], 1)

                def scales(n):
                    t, h = n // NH, n % NH
                    dve.wait_ge(S["p_exp"], 2 * n + 2)
                    step(v.reciprocal(arec[:, n % 2, :], asm[:, n % 2, 4:6]))
                    settle()
                    v.tensor_tensor(arec[:, n % 2, :], arec[:, n % 2, :], gv[:, t, h, 1:3], ALU.mult).then_inc(S["rs_ready"], 1)

                def evac_c(n):
                    dve.wait_ge(S["pt_ps"], n + 1)
                    if n >= 2:
                        dve.wait_ge(S["pv_done"], n - 1)
                    v.tensor_copy(PT[0:NBLK, n % 2, 512:640], bank[4 if n % 2 else 7][0:NBLK, 0:128]).then_inc(S["ptc_evac"], 1)

                maxes(0)
                maxes(1)
                for n in range(2 * NH):
                    if n >= 2:
                        dve.wait_ge(S["p_norm"], n - 1)
                    scales(n)
                    evac_c(n)
                    if n + 2 < 2 * NH:
                        maxes(n + 2)
                    if n % 8 == 0 and n:
                        q = n // 8 - 1
                        dve.wait_ge(S["pv_done"], n)
                        v.tensor_copy(o[:, q // 2, 512 * (q % 2):512 * (q % 2) + 512], bank[(5, 6)[q % 2]][:, :]).then_inc(S["o_evac"], 1)
                dve.wait_ge(S["pv_done"], 2 * NH)
                v.tensor_copy(o[:, 1, 512:1024], bank[6][:, :]).then_inc(S["o_evac"], 1)

            def moe(L):
                lg = rt[:, 0:72].rearrange("p (t c) -> p t c", t=NT)
                g8 = rt[:, 72:88].rearrange("p (t c) -> p t c", t=NT)
                gm = rt[:, 88:104].rearrange("p (t c) -> p t c", t=NT)
                gi = rt[:, 104:120].rearrange("p (t c) -> p t c", t=NT)
                oh = rt[:, 112:120].rearrange("p (t c) -> p t c", t=NT)
                le = rt[:, 128:144].rearrange("p (t c) -> p t c", t=NT)
                pr = rt[:, 144:160].rearrange("p (t c) -> p t c", t=NT)
                ev = rt[:, 168:184].rearrange("p (t c) -> p t c", t=NT)
                ei = rt[:, 184:200].rearrange("p (t c) -> p t c", t=NT)
                gidx, eidx, wsum = rt[:, 200:202], rt[:, 202:206].rearrange("p (t c) -> p t c", t=NT), rt[:, 206:208]
                am = rt[:, 256:320].rearrange("p (t e) -> p t e", t=NT)
                onehot = rt[:, 320:448].rearrange("p (c t e) -> p c t e", c=2, t=NT)
                prod = rt[:, 448:576].rearrange("p (c t e) -> p c t e", c=2, t=NT)
                incl, offs, scol = rt[:, 576:608], rt[:, 608:640], rt[:, 640:704].rearrange("p (t e) -> p t e", t=NT)
                offw = rt[:, 0:128].rearrange("p (w e) -> p w e", w=NWIN)
                gif = rt[:, 704:720].bitcast(u32).rearrange("p (t c) -> p t c", t=NT)
                eif = rt[:, 720:736].bitcast(u32).rearrange("p (t c) -> p t c", t=NT)
                slot, wt = slotw[:, 0], slotw[:, 1]
                dve.wait_ge(S["x_ready"], 4 * L + 2)
                step(v.memset(g8, -3.0e38))
                dve.wait_ge(S["router_ps"], L + 1)
                dve.wait_ge(S["rbias_loaded"], 16 * (L + 1))
                step(v.tensor_tensor(lg, bank[0][:, 0:128].rearrange("p (t c) -> p t c", t=NT)[:, :, 0:36],
                                     rbias[:, :].unsqueeze(1).to_broadcast([128, NT, 36]), ALU.add))
                settle()
                step(v.tensor_copy(g8[:, :, 0:4], lg[:, :, 0:4]))
                settle()
                for t in range(NT):
                    step(v.max(gm[:, t, :], g8[:, t, :]))
                settle()
                for t in range(NT):
                    step(v.max_index(gif[:, t, :], gm[:, t, :], g8[:, t, :]))
                v.tensor_scalar(rt[:, 120:122], gm[:, :, 0], -1.0, None, ALU.mult).then_inc(S["gneg_ready"], 1)
                settle()
                step(v.tensor_copy(gidx, gif[:, :, 0]))
                settle()
                for t in range(NT):
                    step(v.tensor_scalar(oh[:, t, :], iota[:, 0:4], gidx[:, t:t + 1], None, ALU.is_equal))
                settle()
                for t in range(NT):
                    step(v.tensor_scalar(le[:, t, :], lg[:, t, 4:12], oh[:, t, 0:1], None, ALU.mult))
                for g in range(1, NG):
                    settle()
                    for t in range(NT):
                        step(v.scalar_tensor_tensor(le[:, t, :], lg[:, t, 4 + 8 * g:12 + 8 * g], oh[:, t, g:g + 1], le[:, t, :], ALU.mult, ALU.add))
                settle()
                step(v.tensor_reduce(rt[:, 164:166], le, axis=AX.X, op=ALU.max))
                settle()
                v.tensor_scalar(rt[:, 160:162], rt[:, 164:166], -1.0, None, ALU.mult).then_inc(S["eneg_ready"], 1)
                dve.wait_ge(S["gexp_done"], 2 * (L + 1))
                step(v.reciprocal(rt[:, 124:126], rt[:, 122:124]))
                dve.wait_ge(S["eexp_done"], 2 * (L + 1))
                step(v.reciprocal(rt[:, 166:168], rt[:, 162:164]))
                settle()
                for t in range(NT):
                    step(v.tensor_scalar(pr[:, t, :], pr[:, t, :], rt[:, 166 + t:167 + t], None, ALU.mult))
                settle()
                for t in range(NT):
                    step(v.max(ev[:, t, :], pr[:, t, :]))
                settle()
                for t in range(NT):
                    step(v.max_index(eif[:, t, :], ev[:, t, :], pr[:, t, :]))
                step(v.tensor_tensor(wsum, ev[:, :, 0], ev[:, :, 1], ALU.add))
                settle()
                step(v.tensor_copy(eidx, eif[:, :, 0:2]))
                step(v.reciprocal(wsum, wsum))
                settle()
                for t in range(NT):
                    step(v.scalar_tensor_tensor(eidx[:, t, :], gidx[:, t:t + 1].to_broadcast([128, 2]), 8.0, eidx[:, t, :], ALU.mult, ALU.add))
                step(v.tensor_tensor(wsum, wsum, rt[:, 124:126], ALU.mult))
                settle()
                for c in range(2):
                    step(v.tensor_tensor(wt[:, c, :], ev[:, :, c], wsum, ALU.mult))
                    for t in range(NT):
                        step(v.tensor_scalar(onehot[:, c, t, :], iota[:, 0:NE], eidx[:, t, c:c + 1], None, ALU.is_equal))
                settle()
                v.tensor_tensor(am, onehot[:, 0], onehot[:, 1], ALU.add).then_inc(S["assign_ready"], 1)
                dve.wait_ge(S["pos_ps"], L + 1)
                cnt = cntw[:, 0, :]
                step(v.tensor_copy(cnt, bank[1][:, 64:96]))
                settle()
                step(v.tensor_tensor_scan(incl, ones[:, 0:NE], cnt, 0.0, ALU.mult, ALU.add))
                settle()
                step(v.tensor_tensor(offs, incl, cnt, ALU.subtract))
                settle()
                step(v.tensor_tensor(scol, bank[1][:, 0:64].rearrange("p (t e) -> p t e", t=NT),
                                     offs.unsqueeze(1).to_broadcast([128, NT, NE]), ALU.add))
                settle()
                step(v.tensor_tensor(prod, onehot, scol.unsqueeze(1).to_broadcast([128, 2, NT, NE]), ALU.mult))
                settle()
                step(v.tensor_reduce(slot, prod, axis=AX.X, op=ALU.add))
                settle()
                for t in range(NT):
                    step(v.tensor_scalar(pick[:, t, :], iota, slot[:, 0, t:t + 1], None, ALU.is_equal))
                settle()
                for t in range(NT):
                    ins = v.scalar_tensor_tensor(pick[:, t, :], iota, slot[:, 1, t:t + 1], pick[:, t, :], ALU.is_equal, ALU.add)
                    if t == NT - 1:
                        ins.then_inc(S["pick_ready"], 1)
                    else:
                        step(ins)
                        settle()
                for w in range(1, NWIN):
                    step(v.tensor_scalar(cntw[:, w, :], cnt, float(-WIN * w), None, ALU.add))
                for w in range(NWIN):
                    step(v.tensor_scalar(offw[:, w, :], offs, float(WIN * w), float(NSLOT), ALU.add, ALU.min))
                step(v.tensor_reduce(rt[:, 736:737], cnt, axis=AX.X, op=ALU.max))
                settle()
                step(v.tensor_copy(offi[0:1, :], offw[0:1].rearrange("p w e -> p (w e)")))
                settle()
                v.tensor_copy(mxi[0:1, 0:1], rt[0:1, 736:737]).then_inc(S["offs_ready"], 1)
                for t in range(NT):
                    step(v.tensor_scalar(selw[:, t, :], iota, slot[:, 0, t:t + 1], wt[:, 0, t:t + 1], ALU.is_equal, ALU.mult))
                    step(v.tensor_scalar(seltmp, iota, slot[:, 1, t:t + 1], wt[:, 1, t:t + 1], ALU.is_equal, ALU.mult))
                    settle()
                    ins = v.tensor_tensor(selw[:, t, :], selw[:, t, :], seltmp, ALU.add)
                    if t == NT - 1:
                        ins.then_inc(S["selw_ready"], 1)
                    else:
                        step(ins)
                        settle()
                dve.wait_ge(S["selw_ready"], L + 1)
                for c in range(1, KT, 2):
                    dve.wait_ge(S["gather_ps"], 8 * L + c + 1)
                    v.tensor_copy(xsT[:, c, 0:NSLOT], bank[(2 + c) % 8][:, :]).then_inc(S["gather_dve"], 1)
                dve.wait_ge(S["gather_dve"], 4 * (L + 1))
                dve.wait_ge(S["gather_act"], 4 * (L + 1))
                dve.wait_ge(S["pads_zeroed"], 3 + L)
                dve.wait_ge(S["offs_ready"], L + 1)

                def first_column(i):
                    return dve.value_load(offi[0:1, bass.ds(i, 1)], min_val=0, max_val=NSLOT)

                def window(i, w, e, b, off, ins_to):
                    step(v.tensor_scalar(mask[:, b, :], iota[:, 0:WIN], cntw[:, w, bass.ds(e, 1)], None, ALU.is_lt))
                    settle()
                    v.tensor_tensor(xw[:, b], xsT[:, :, bass.ds(off, WIN)], mask[:, b, :].unsqueeze(1).to_broadcast([128, KT, WIN]),
                                    ALU.mult).then_inc(ins_to, 1)

                def times_up(b, s):
                    v.tensor_tensor(hb[:, b], hb[:, b], bank[2 + b][:, 256:512].rearrange("p (m s) -> p m s", m=4), ALU.mult).then_inc(s, 1)

                def add_out(off, b, s):
                    yv = ysT[:, :, bass.ds(off, WIN)]
                    v.tensor_tensor(yv, bank[5 + b][:, :].rearrange("p (k s) -> p k s", k=KT), yv, ALU.add).then_inc(s, 1)

                def xw_step(e, r):
                    off = first_column(e)
                    if not (type(e) is int and e < 3):
                        dve.wait_ge(S["gateup_done"], NE * L + e - 2)
                    window(e, 0, e, r % 3, off, S["xw_ready"])

                def h_step(e, r):
                    dve.wait_ge(S["silu_done"], NE * L + e + 1)
                    times_up(r % 3, S["h_ready"])

                def y_step(e, r):
                    off = first_column(e)
                    dve.wait_ge(S["down_done"], NE * L + e + 1)
                    if type(e) is int and e == 0:
                        dve.wait_ge(S["y_zeroed"], L + 1)
                    else:
                        dve.wait_ge(S["y_added"], NE * L + e)
                    add_out(off, r % 3, S["y_added"])

                xw_step(0, 0)
                xw_step(1, 1)
                h_step(0, 0)
                for e in (1, 2):
                    xw_step(e + 1, e + 1)
                    h_step(e, e)
                    y_step(e - 1, e - 1)
                n0 = st.n
                with dve.Fori(0, 9) as i:
                    st.off = i * 3
                    for r in range(3):
                        xw_step(i * 3 + (r + 4), r + 4)
                        h_step(i * 3 + (r + 3), r + 3)
                        y_step(i * 3 + (r + 2), r + 2)
                assert st.n - n0 == 3
                st.off, st.n = 0, n0 + 27
                xw_step(31, 31)
                for e in (30, 31):
                    h_step(e, e)
                    y_step(e - 1, e - 1)
                y_step(31, 31)
                most = dve.value_load(mxi[0:1, 0:1], min_val=0, max_val=SEQ)
                with dve.If(most > WIN):
                    vo = ovf[L]
                    dve.wait_ge(S["y_added"], NE * L + NE)
                    with dve.Fori(0, NE) as e:
                        for w in range(1, NWIN):
                            c = e * (NWIN - 1) + w
                            off = first_column(e + NE * w)
                            v.tensor_scalar(mask[:, 0, :], iota[:, 0:WIN], cntw[:, w, bass.ds(e, 1)], None, ALU.is_lt).then_inc(vo["mask"], 1)
                            dve.wait_ge(vo["mask"], c)
                            v.tensor_tensor(xw[:, 0], xsT[:, :, bass.ds(off, WIN)],
                                            mask[:, 0, :].unsqueeze(1).to_broadcast([128, KT, WIN]), ALU.mult).then_inc(vo["xw"], 1)
                            dve.wait_ge(vo["silu"], c)
                            times_up(0, vo["h"])
                            dve.wait_ge(vo["down"], c)
                            add_out(off, 0, vo["y"])
                            dve.wait_ge(vo["y"], c)
                for q in range(1, 8, 2):
                    dve.wait_ge(S["ysT_ps"], 8 * L + q + 1)
                    v.tensor_copy(ys[:, q // 2, 512:1024], bank[4 + q % 4][:, :]).then_inc(S["ys_dve"], 1)

            dve.wait_ge(S["consts_loaded"], 16)
            mixer0()
            layernorm(0)
            moe(0)
            layernorm(1)
            mixer1()
            layernorm(2)
            moe(1)
            layernorm(3)


def constants():
    import numpy as np
    c = np.zeros((128, N_CONST), np.float32)
    i = np.arange(128)
    c[:, C_ID:C_ID + 128] = np.eye(128)
    c[:, C_UP:C_UP + 128] = i[:, None] < i[None, :]
    c[:, C_ONE:C_ONE + 128] = 1.0
    c[:, C_CAUS:C_CAUS + 128] = np.where(i[None, :] <= i[:, None], 0.0, -1e30)
    c[:, C_IOTA:C_IOTA + 512] = np.arange(512)
    c[:, C_EPS] = LN_EPS
    return c


def attention_constants():
    import numpy as np
    c = np.zeros((128, N_ATT), np.float32)
    i = np.arange(128)
    inv = np.float32(10000.0) ** (-np.arange(0, DK, 2, dtype=np.float32) / DK)
    for t in range(NT):
        ang = ((i + 128 * t).astype(np.float32)[:, None] * inv[None, :].astype(np.float32)).astype(np.float32)
        c[:, A_ROPE + 64 * t:A_ROPE + 64 * t + 32] = np.cos(ang)
        c[:, A_ROPE + 64 * t + 32:A_ROPE + 64 * t + 64] = np.sin(ang)
        seen = (16 * np.arange(NBLK) + 31)[None, :] <= (i + 128 * t)[:, None]
        c[:, A_CMPA + 16 * t:A_CMPA + 16 * t + NBLK] = np.where(seen, 0.0, -1e30)
        c[:, A_CMPM + 16 * t:A_CMPM + 16 * t + NBLK] = seen
    return c


def kernel(**inputs):
    import numpy as np
    import concourse.bacc as bacc
    from concourse.bass_utils import run_bass_kernel_spmd as run

    x = {k: np.ascontiguousarray(np.asarray(v)) for k, v in inputs.items()}

    def channels(v):
        v = v.reshape(-1, 4, 128)
        return np.transpose(v, (2, 1, 0)).reshape(128, -1)

    arrays = {"x": x["x"], "xT": np.ascontiguousarray(x["x"][0].T), "consts": constants(),
              "att_consts": attention_constants()}
    arrays["params"] = np.concatenate([channels(x[k]) for k in (
        "l0_conv_w", "l0_lru_conv_w", "l0_lru_conv_b", "l0_lru_b_a", "l0_lru_b_x", "l0_lru_lambda")], axis=1)
    wbd = np.zeros((128, 8, 128), np.float32)
    for n, k in enumerate(("l0_lru_w_a", "l0_lru_w_x")):
        for c in range(4):
            for u in range(2):
                wbd[64 * u:64 * u + 64, 4 * n + c, 64 * u:64 * u + 64] = x[k][2 * c + u]
    arrays["wbd"] = wbd
    arrays["pe"] = np.stack([np.transpose(x[k].reshape(16, 2, 64), (1, 2, 0)).reshape(128, 16)
                             for k in ("l1_cmp_k_pe", "l1_cmp_v_pe")], axis=1)
    for L in range(2):
        arrays[f"wr{L}"] = np.concatenate([x[f"l{L}_router_group_w"], x[f"l{L}_router_expert_w"]], axis=1)
        arrays[f"br{L}"] = np.concatenate([x[f"l{L}_router_group_b"], x[f"l{L}_router_expert_b"]])
    for k in ("l0_w_in l0_w_out l0_ln1_g l0_ln1_b l0_ln2_g l0_ln2_b l1_w_in l1_cmp_k_w1 l1_cmp_k_w2 l1_cmp_v_w1 "
              "l1_cmp_v_w2 l1_w_out l1_ln1_g l1_ln1_b l1_ln2_g l1_ln2_b").split():
        arrays[k] = x[k]
    for L in range(2):
        for k in ("gate", "up", "down"):
            arrays[f"l{L}_expert_w_{k}"] = x[f"l{L}_expert_w_{k}"]

    nc = bacc.Bacc("TRN2", target_bir_lowering=False, num_devices=1)
    arrays = {k: np.ascontiguousarray(v) for k, v in arrays.items()}
    aps = {k: nc.dram_tensor("in_" + k, v.shape, mybir.dt.from_np(v.dtype), kind="ExternalInput").ap()
           for k, v in arrays.items()}
    out = nc.dram_tensor("out", (1, SEQ, D), mybir.dt.float32, kind="ExternalOutput").ap()
    program(nc, aps, out)
    r = run(nc, [{"in_" + k: v for k, v in arrays.items()}], core_ids=[0])
    return r.results[0]["out"]
```

```python
import concourse.bass as bass
from concourse import mybir
from contextlib import ExitStack

SEQ, D, FF, NE, NG = 256, 1024, 512, 32, 4
CW = 512
KT = D // 128
NT = SEQ // 128
WIN = 64
NSLOT = 2 * SEQ
NPAD = NSLOT + WIN
NWIN = SEQ // WIN
ALPHA = (2 * 2) ** 0.25
LN_EPS = 1e-5
NH, DK, NKV = 16, 64, 4
NBLK = SEQ // 16 - 1
SCALE = DK ** -0.5
TINY = 1e-30
RING = 9
GL = 48

L0_COLS = [4 * CW, 3 * CW, CW, 2 * CW, 0]
L0_UNITS = 7
L1_UNITS = 9
MIX_BASE = [0, L0_UNITS + 3 * NE]
EXP_BASE = [L0_UNITS, L0_UNITS + 3 * NE + L1_UNITS]

C_ID, C_UP, C_ONE, C_CAUS, C_IOTA, C_EPS, C_ROW = 0, 128, 256, 384, 512, 1024, 1025
N_CONST = 1026
A_ROPE, A_CMPA, A_CMPM, N_ATT = 0, 128, 160, 192
P_CONV, P_LCONV, P_LCB, P_BA, P_BX, P_LAM = 0, 12, 28, 32, 36, 40
N_PARAM = 44


def program(nc, a, out):
    f32, i32, u32 = mybir.dt.float32, mybir.dt.int32, mybir.dt.uint32
    ALU, ACT, AX = mybir.AluOpType, mybir.ActivationFunctionType, mybir.AxisListType
    ctx = ExitStack()
    with ctx:
        def sb(name, shape, dt=f32):
            return ctx.enter_context(nc.sbuf_tensor(name, shape, dt))

        def sem(name):
            return ctx.enter_context(nc.semaphore(name))

        ring = sb("ring", [128, RING, 4096])
        x_tok = sb("x_tok", [128, NT, D])
        cst = sb("cst", [128, N_CONST])
        work = sb("work", [128, 12560])
        par = sb("par", [128, N_PARAM])
        sp_t = sb("sp_t", [128, 6, 4])
        stats = sb("stats", [128, NT, 2, 6])
        mv = sb("mv", [128, NT, 2])
        sd = sb("sd", [128, NT])
        rstd = sb("rstd", [128, NT])
        rbias = sb("rbias", [128, 36])
        slotw = sb("slotw", [128, 2, 2, NT])
        offi = sb("offi", [1, NWIN * NE], i32)
        mxi = sb("mxi", [1, 1], i32)
        small = sb("small", [128, 144])
        gates = small[:, 0:NT * GL].rearrange("p (t c) -> p t c", t=NT)
        asm = small[:, 96:108].rearrange("p (n c) -> p n c", n=2)
        arec = small[:, 108:112].rearrange("p (n c) -> p n c", n=2)
        cmx = small[:, 112:144].rearrange("p (t h) -> p t h", t=NT)
        bank = [ctx.enter_context(nc.psum_tensor(f"bank{i}", [128, 512], f32)) for i in range(8)]

        def w_(lo, n, parts=128, p0=0):
            return work[p0:p0 + parts, lo:lo + n]

        ident, upper, ones = cst[:, C_ID:C_ID + 128], cst[:, C_UP:C_UP + 128], cst[:, C_ONE:C_ONE + 128]
        causal, iota = cst[:, C_CAUS:C_CAUS + 128], cst[:, C_IOTA:C_IOTA + 512]
        catt = w_(11600, N_ATT)
        rope = catt[:, A_ROPE:A_ROPE + 128].rearrange("p (t s d) -> p t s d", t=NT, s=2)
        cmp_add = catt[:, A_CMPA:A_CMPA + 32].rearrange("p (t c) -> p t c", t=NT)
        cmp_mul = catt[:, A_CMPM:A_CMPM + 32].rearrange("p (t c) -> p t c", t=NT)
        eps = cst[:, C_EPS:C_EPS + 1]
        row = cst[:, C_ROW:C_ROW + 1]

        xT0 = w_(0, 2048).rearrange("p (k t) -> p k t", k=KT)
        xl = w_(2048, 1040).rearrange("p (c t) -> p c t", c=4)
        gate = w_(3088, 1024).rearrange("p (c t) -> p c t", c=4)
        cghc = w_(4112, 1040).rearrange("p (c t) -> p c t", c=4)
        xc = w_(5152, 1024).rearrange("p (c t) -> p c t", c=4)
        rg = w_(6176, 1024).rearrange("p (c t) -> p c t", c=4)
        ig = w_(7200, 1024).rearrange("p (c t) -> p c t", c=4)
        yT = w_(8224, 2048).rearrange("p (k t) -> p k t", k=KT)
        wbd = w_(10272, 1024).rearrange("p (c n) -> p c n", c=8)
        th = w_(11296, 1024).rearrange("p (c t) -> p c t", c=4)
        xsT = w_(0, 8 * NPAD).rearrange("p (k s) -> p k s", k=KT)
        rows = w_(4608, 1024).rearrange("p (n c t) -> p n c t", n=2, c=2)
        xw = w_(5632, 512).rearrange("p (k s) -> p k s", k=KT)
        gu = w_(6144, 512)
        hT = w_(6656, 256).rearrange("p (k s) -> p k s", k=4)
        sel = [w_(6912 + 256 * h, 256) for h in range(2)]
        yw = w_(7424, 512)
        colid = w_(7936, 128).rearrange("p (w e) -> p w e", w=NWIN)
        eq = [w_(8064 + 256 * c, 256) for c in range(2)]
        hT2 = w_(8576, 256).rearrange("p (k s) -> p k s", k=4)
        moe_xT = w_(9728, 2048).rearrange("p (k t) -> p k t", k=KT)
        pick = w_(8320, 1024).rearrange("p (t s) -> p t s", t=NT)
        wr = w_(9344, 288).rearrange("p (k n) -> p k n", k=KT)
        rt = w_(11776, 768)
        xT1 = w_(0, 2048).rearrange("p (k t) -> p k t", k=KT)
        z = w_(2048, 3584).rearrange("p (t c) -> p t c", t=NT)
        kd = w_(5632, 4096).rearrange("p (n t g u d) -> p n t g u d", n=4, t=NT, g=NKV, u=2)
        rtmp = w_(9728, 512)
        glw = w_(10240, 384).rearrange("p (k n) -> p k n", k=KT)
        w2k = w_(10624, 256).rearrange("p (m n) -> p m n", m=2)
        w2v = w_(10880, 128).rearrange("p (m n) -> p m n", m=2)
        pe_ = w_(11008, 32).rearrange("p (n k) -> p n k", n=2)
        CT2 = [(0, 1024), (1024, 1024)]
        blk = [w_(5632 + 960 * n, 960).rearrange("p (k g b) -> p k g b", k=16, g=NKV) for n in range(2)]
        hC = w_(11360, 240).rearrange("p (n m c) -> p n m c", n=2, m=2)
        kcT = w_(11040, 60)
        vcmp = w_(11100, 256, 15)
        kT = [w_(1024 * n, 1024).rearrange("p (g t) -> p g t", g=NKV) for n in range(2)]
        qT = w_(7680, 2048).rearrange("p (k t) -> p k t", k=KT)
        P = w_(2048, 1024).rearrange("p (n s) -> p n s", n=2)
        pc = w_(3840, 512).rearrange("p (t h c) -> p t h c", t=NT, h=NH)
        PT = w_(9728, 1280).rearrange("p (n s) -> p n s", n=2)
        o = w_(5632, 2048).rearrange("p (t c) -> p t c", t=NT)
        oT = w_(0, 2048).rearrange("p (k t) -> p k t", k=KT)
        GB = [[0, 8832], [7680, 8832]]

        S = {n: sem(n) for n in (
            "xT_loaded consts_loaded x_loaded params_loaded router_loaded rbias_loaded gb_loaded "
            "l1small_loaded pads_zeroed z0_done z0_act z0_dve xc_ready softplus_e softplus_done gate_ps gate_sig "
            "lru_T lru_T_used lru_m2 lru_mult lru_exp ylru_ready resid_ps var_ready sd_ready x_ready xT_ps xT_evac "
            "router_ps gneg_ready gexp_done eneg_ready eexp_done assign_ready pos_ps slot_ready pick_ready "
            "gather_ps gather_act gather_dve rows_ps rows_evac sel_zeroed offs_ready colid_ready xw_ready gu_done gu_evac turn_done "
            "silu_done h_ready down_done y_evac sel_ready sel_half eq_done sc_out dve_step act_step "
            "z1_done z1_evac z1_rope kdup_done ct_ps ct_evac blk_ready cmp1_done cmp1_gelu cmp2_done cmp2_evac kT_ps kT_evac "
            "qT_ps qT_evac sc_cmp pc_sub pc_exp pc_ready sc_done nm_ready p_exp rs_ready p_norm pt_ps pt_evac ptc_evac pv_done "
            "o_evac oT_ps oT_evac out_done").split()}
        full = [sem(f"ring_full{i}") for i in range(RING)]
        ovf = [{n: sem(f"ovf{L}_{n}") for n in "gate_in up_in down_in xw gu gu_evac turn silu h down y_evac sel eq out".split()} for L in range(2)]

        block = ctx.enter_context(nc.Block())

        def slot_of(n):
            return n % RING

        def arrived(n):
            return 16 * (n // RING + 1)

        def gb_view(L, which):
            lo = GB[L][which]
            return w_(lo, 1024), w_(lo + 1024, 1024)

        class Steps:
            def __init__(self, eng, s):
                self.eng, self.s, self.n, self.off = eng, s, 0, 0

            def step(self, ins):
                ins.then_inc(self.s, 1)
                self.n += 1

            def settle(self):
                self.eng.wait_ge(self.s, self.off + self.n)

        @block.sync
        def _(sp):
            def load(n, src):
                dst = ring[:, slot_of(n), :].rearrange("p (k c) -> p k c", k=src.shape[1])
                sp.dma_start(dst, src).then_inc(full[slot_of(n)], 16)

            def cols(w, lo, width):
                return w[:, lo:lo + width].rearrange("(k p) c -> p k c", p=128)

            def expert_srcs(L, e):
                g, u, d = a[f"l{L}_expert_w_gate"], a[f"l{L}_expert_w_up"], a[f"l{L}_expert_w_down"]
                if type(e) is int:
                    return [w[e].rearrange("(k p) c -> p k c", p=128) for w in (g, u, d)]
                return [w[bass.ds(e, 1)].rearrange("o (k p) c -> p (o k) c", p=128) for w in (g, u, d)]

            sp.dma_start(xT0, a["xT"].rearrange("(k p) t -> p k t", p=128)).then_inc(S["xT_loaded"], 16)
            for L in range(2):
                base = MIX_BASE[L]
                for n in range(L0_UNITS if L == 0 else L1_UNITS):
                    if L == 0:
                        src = cols(a["l0_w_in"], L0_COLS[n], 512) if n < 5 else cols(a["l0_w_out"], 512 * (n - 5), 512)
                    else:
                        prev = base + n - RING - EXP_BASE[0]
                        used = ("gu_done", "gu_done", "down_done")[prev % 3]
                        sp.wait_ge(S[used], prev // 3 + 1)
                        if n < 5:
                            src = cols(a["l1_w_in"], 512 * n, 512)
                        elif n < 7:
                            src = cols(a["l1_cmp_k_w1" if n == 5 else "l1_cmp_v_w1"], 0, 256)
                        else:
                            src = cols(a["l1_w_out"], 512 * (n - 7), 512)
                    load(base + n, src)
                for e in range(3):
                    for k, src in enumerate(expert_srcs(L, e)):
                        n = EXP_BASE[L] + 3 * e + k
                        m = n - RING - MIX_BASE[L]
                        if m >= 0:
                            if L == 0:
                                sp.wait_ge(*((S["z0_done"], 2 * m + 2) if m < 5 else (S["resid_ps"], 2 * (m - 4))))
                            else:
                                sp.wait_ge(*((S["z1_done"], 2 * m + 2) if m < 5 else
                                             (S["cmp1_done"], m - 4) if m < 7 else (S["resid_ps"], 8 + 2 * (m - 6))))
                        load(n, src)

                def expert_loads(e, r):
                    for k, src in enumerate(expert_srcs(L, e)):
                        used = ("gu_done", "gu_done", "down_done")[k]
                        sp.wait_ge(S[used], NE * L + e - 2)
                        load(EXP_BASE[L] + 3 * r + k, src)
                with sp.Fori(0, 9) as i:
                    for r in range(3):
                        e = sp.snap(i * 3 + 3 + r)
                        expert_loads(e, r)
                for e in (30, 31):
                    expert_loads(e, e % 3)
                sp.wait_ge(S["offs_ready"], L + 1)
                most = sp.value_load(mxi[0:1, 0:1], min_val=0, max_val=SEQ)
                with sp.If(most > WIN):
                    v = ovf[L]
                    sp.wait_ge(S["down_done"], NE * L + NE - 1)

                    def again(e):
                        srcs = expert_srcs(L, e)
                        if not (type(e) is int and e == 0):
                            sp.wait_ge(v["down"], e * (NWIN - 1))
                        for k, src in enumerate(srcs):
                            dst = ring[:, slot_of(EXP_BASE[L] + k), :].rearrange("p (k c) -> p k c", k=src.shape[1])
                            sp.dma_start(dst, src).then_inc(v[("gate_in", "up_in", "down_in")[k]], 16)
                    again(0)
                    with sp.Fori(1, NE) as e:
                        again(sp.snap(e + 0))
                    sp.wait_ge(v["down"], NE * (NWIN - 1))
            for t in range(NT):
                sp.wait_ge(S["x_ready"], 6 + t + 1)
                sp.dma_start(out[0, 128 * t:128 * (t + 1), :], x_tok[:, t, :]).then_inc(S["out_done"], 16)
            sp.wait_ge(S["out_done"], 32)

        @block.gpsimd
        def _(pool):
            pool.memset(xl[:, :, 0:3], 0.0).then_inc(S["pads_zeroed"], 1)
            pool.memset(cghc[:, :, 0:2], 0.0).then_inc(S["pads_zeroed"], 1)

            def bcast(src, n):
                return src.rearrange("(o n) -> o n", o=1).to_broadcast([128, n])

            def load_gb(L, which):
                g, b = gb_view(L, which)
                k = f"l{L}_ln{which + 1}"
                pool.dma_start(g, bcast(a[k + "_g"], D)).then_inc(S["gb_loaded"], 16)
                pool.dma_start(b, bcast(a[k + "_b"], D)).then_inc(S["gb_loaded"], 16)

            for L in range(2):
                if L == 1:
                    pool.wait_ge(S["x_ready"], 4)
                    pool.dma_start(glw, a["l1_w_in"][:, 2560:2608].rearrange("(k p) c -> p k c", p=128)).then_inc(S["l1small_loaded"], 16)
                    for u in range(2):
                        pool.dma_start(w2k[:, :, 64 * u:64 * u + 64], a["l1_cmp_k_w2"].rearrange("(m p) c -> p m c", p=128)).then_inc(S["l1small_loaded"], 16)
                    pool.dma_start(w2v, a["l1_cmp_v_w2"].rearrange("(m p) c -> p m c", p=128)).then_inc(S["l1small_loaded"], 16)
                    pool.dma_start(pe_, a["pe"]).then_inc(S["l1small_loaded"], 16)
                    pool.dma_start(catt, a["att_consts"]).then_inc(S["l1small_loaded"], 16)
                    for n in range(2 * NH):
                        N = 128 * (n // NH + 1)
                        pool.wait_ge(S["rs_ready"], n + 1)
                        pv = P[:, n % 2, 0:2 * N].rearrange("p (b s) -> p b s", b=2)
                        pool.tensor_tensor(pv, pv, arec[:, n % 2, :].unsqueeze(2).to_broadcast([128, 2, N]), ALU.mult).then_inc(S["p_norm"], 1)
                    pool.wait_ge(S["sc_done"], 2 * NH)
                    pool.wait_ge(S["pv_done"], 2 * NH)
                else:
                    pool.wait_ge(S["z0_done"], 10)
                load_gb(L, 0)
                pool.wait_ge(S["x_ready"], 4 * L + 2)
                pool.dma_start(wr, a[f"wr{L}"].rearrange("(k p) n -> p k n", p=128)).then_inc(S["router_loaded"], 16)
                pool.dma_start(rbias[:, :], bcast(a[f"br{L}"], 36)).then_inc(S["rbias_loaded"], 16)
                pool.memset(xsT[:, :, NSLOT:NPAD], 0.0).then_inc(S["pads_zeroed"], 1)
                for h in range(2):
                    pool.wait_ge(*((S["pads_zeroed"], 3 + L) if h == 0 else (S["sel_zeroed"], 2 * L + 1)))
                    pool.memset(sel[h][64 - 64 * h:128 - 64 * h, :], 0.0).then_inc(S["sel_zeroed"], 1)
                pool.wait_ge(S["gather_ps"], 8 * (L + 1))
                load_gb(L, 1)
                pool.wait_ge(S["gather_act"], 4 * (L + 1))
                pool.wait_ge(S["gather_dve"], 4 * (L + 1))
                pool.wait_ge(S["pads_zeroed"], 3 + L)
                pool.wait_ge(S["offs_ready"], L + 1)

                def window(i, s):
                    off = pool.value_load(offi[0:1, bass.ds(i, 1)], min_val=0, max_val=NSLOT)
                    return lambda: pool.tensor_copy(xw, xsT[:, :, bass.ds(off, WIN)]).then_inc(s, 1)

                window(0, S["xw_ready"])()
                with pool.Fori(1, NE) as e:
                    copy = window(e, S["xw_ready"])
                    pool.wait_ge(S["gu_done"], e + NE * L)
                    copy()
                pool.wait_ge(S["gu_done"], NE * (L + 1))
                most = pool.value_load(mxi[0:1, 0:1], min_val=0, max_val=SEQ)
                with pool.If(most > WIN):
                    with pool.Fori(0, NE) as e:
                        for w in range(1, NWIN):
                            window(e + NE * w, ovf[L]["xw"])()
                            pool.wait_ge(ovf[L]["gu"], e * (NWIN - 1) + w)

        @block.tensor
        def _(pe):
            mm, tr = nc.tensor.matmul, nc.tensor.transpose

            def unit(n, k=KT):
                pe.wait_ge(full[slot_of(n)], arrived(n))
                return ring[:, slot_of(n), :].rearrange("p (k c) -> p k c", k=k)

            def transpose_x(q, dep, count, src, s_ps):
                for t in range(NT):
                    pe.wait_ge(dep, count + t)
                    for hf in range(2):
                        for c in range(4):
                            last = tr(bank[4 + 2 * t + hf][:, 128 * c:128 * c + 128],
                                      src[:, t, 512 * hf + 128 * c:512 * hf + 128 * c + 128], ident)
                        last.then_inc(s_ps, 1)

            def project_out(L, src):
                for h in range(2):
                    w = unit(MIX_BASE[L] + (5 if L == 0 else 7) + h)
                    for t in range(NT):
                        for k in range(KT):
                            last = mm(bank[2 * t + h][:, :], src[:, k, 128 * t:128 * t + 128], w[:, k, :],
                                      start=(k == 0), stop=(k == KT - 1))
                        last.then_inc(S["resid_ps"], 1)

            def mixer0():
                pe.wait_ge(S["xT_loaded"], 16)
                for u in range(5):
                    w = unit(u)
                    if u >= 2:
                        pe.wait_ge(S["z0_act"], 2 * (u - 1))
                    for m in range(4):
                        for k in range(KT):
                            last = mm(bank[2 * (u % 2) + m // 2][:, 256 * (m % 2):256 * (m % 2) + 256],
                                      w[:, k, 128 * m:128 * m + 128], xT0[:, k, :], start=(k == 0), stop=(k == KT - 1))
                        if m % 2:
                            last.then_inc(S["z0_done"], 1)
                    if u == 1:
                        pe.wait_ge(S["params_loaded"], 32)
                        pe.wait_ge(S["xc_ready"], 4)
                        for g in range(8):
                            last = mm(bank[4 + g // 2][:, 256 * (g % 2):256 * (g % 2) + 256], wbd[:, g, :], xc[:, g % 4, :],
                                      start=True, stop=True)
                            if g % 2:
                                last.then_inc(S["gate_ps"], 1)
                pe.wait_ge(S["ylru_ready"], 4)
                pe.wait_ge(S["z0_dve"], 4)
                project_out(0, yT)

            def mixer1():
                transpose_x(1, S["x_ready"], 3, x_tok, S["xT_ps"])
                pe.wait_ge(S["xT_evac"], 4 * 2)
                for c in range(5):
                    w = unit(MIX_BASE[1] + c)
                    for t in range(NT):
                        if c >= 2:
                            pe.wait_ge(S["z1_evac"], 2 * (c - 2) + t + 1)
                        for k in range(KT):
                            last = mm(bank[2 * (c % 2) + t][:, :], xT1[:, k, 128 * t:128 * t + 128], w[:, k, :],
                                      start=(k == 0), stop=(k == KT - 1))
                        last.then_inc(S["z1_done"], 1)
                pe.wait_ge(S["l1small_loaded"], 96)
                for t in range(NT):
                    for k in range(KT):
                        last = mm(bank[4][:, 64 * t:64 * t + GL], xT1[:, k, 128 * t:128 * t + 128], glw[:, k, :],
                                  start=(k == 0), stop=(k == KT - 1))
                last.then_inc(S["z1_done"], 1)
                pe.wait_ge(S["z1_evac"], 11)
                for n in range(2):
                    for t in range(NT):
                        if n == 0:
                            pe.wait_ge(S["kdup_done"], t + 1)
                        if n == 1:
                            pe.wait_ge(S["ct_evac"], t + 1)
                        for g in range(NKV):
                            last = tr(bank[5 + t][:, 128 * g:128 * g + 128], kd[:, n, t].rearrange("p g u d -> p g (u d)")[:, g, :], ident)
                        last.then_inc(S["ct_ps"], 1)
                for n in range(2):
                    w = unit(MIX_BASE[1] + 5 + n, 16)
                    pe.wait_ge(S["blk_ready"], n + 1)
                    for m in range(2):
                        for k in range(16):
                            last = mm(bank[7][:, 128 * n + 64 * m:128 * n + 64 * m + 60], w[:, k, 128 * m:128 * m + 128],
                                      blk[n][:, k].rearrange("p g b -> p (g b)"), start=(k == 0), stop=(k == 15))
                    last.then_inc(S["cmp1_done"], 1)
                for n in range(2):
                    for t in range(NT):
                        pe.wait_ge(S["kdup_done"], 2 * (n + 1) + t + 1)
                        b = 2 * n + t
                        if b == 0:
                            pe.wait_ge(S["z1_evac"], 11)
                        for g in range(NKV):
                            last = tr(bank[b][:, 128 * g:128 * g + 128], kd[:, 2 + n, t].rearrange("p g u d -> p g (u d)")[:, g, :], ident)
                        last.then_inc(S["kT_ps"], 1)
                pe.wait_ge(S["cmp1_gelu"], 4)
                for m in range(2):
                    mm(bank[4][:, 0:60], w2k[:, m, :], hC[:, 0, m, :], start=(m == 0), stop=(m == 1))
                for g in range(NKV):
                    for m in range(2):
                        last = mm(bank[4][0:NBLK, 64 + 64 * g:128 + 64 * g], hC[:, 1, m, NBLK * g:NBLK * g + NBLK], w2v[:, m, :],
                                  start=(m == 0), stop=(m == 1))
                last.then_inc(S["cmp2_done"], 1)
                for t in range(NT):
                    pe.wait_ge(S["z1_rope"], 2 + 2 * t)
                    for hf in range(2):
                        b = 2 * t + hf
                        pe.wait_ge(S["kT_evac"], b + 1)
                        for c in range(4):
                            last = tr(bank[b][:, 128 * c:128 * c + 128], z[:, t, 512 * hf + 128 * c:512 * hf + 128 * c + 128], ident)
                        last.then_inc(S["qT_ps"], 1)
                pe.wait_ge(S["qT_evac"], 4)
                pe.wait_ge(S["cmp2_evac"], 2)
                pe.wait_ge(S["ct_evac"], 4)
                for par_ in range(2):
                    lo = 64 * par_
                    for t in range(NT):
                        for j in range(8):
                            g = (2 * j + par_) // 4
                            last = mm(bank[5 + par_][:, 128 * t + 16 * j:128 * t + 16 * j + NBLK],
                                      qT[lo:lo + 64, j, 128 * t:128 * t + 128], kcT[lo:lo + 64, NBLK * g:NBLK * g + NBLK],
                                      start=True, stop=True)
                    last.then_inc(S["sc_cmp"], 1)

                def scores(n):
                    t, h = n // NH, n % NH
                    N, lo, g = 128 * (t + 1), 64 * (h % 2), h // 4
                    if n >= 2:
                        pe.wait_ge(S["p_exp"], 2 * (n - 1))
                    for b in range(2):
                        last = mm(bank[n % 2][:, b * N:b * N + N], qT[lo:lo + 64, h // 2, 128 * t:128 * t + 128],
                                  kT[b][lo:lo + 64, g, 0:N], start=True, stop=True)
                    last.then_inc(S["sc_done"], 1)

                def turn(n):
                    t, h = n // NH, n % NH
                    N = 128 * (t + 1)
                    pe.wait_ge(S["p_norm"], n + 1)
                    if n >= 2:
                        pe.wait_ge(S["pt_evac"], n - 1)
                        pe.wait_ge(S["ptc_evac"], n - 1)
                    for kb in range(2 * (t + 1)):
                        tr(bank[2 + n % 2][:, 128 * kb:128 * kb + 128], P[:, n % 2, 128 * kb:128 * kb + 128], ident)
                    if n == 0:
                        pe.wait_ge(S["pc_ready"], 1)
                    tr(bank[4 if n % 2 else 7][0:NBLK, 0:128], pc[:, t, h, 0:NBLK], ident).then_inc(S["pt_ps"], 1)

                def values(n):
                    t, h = n // NH, n % NH
                    g, kb = h // 4, t + 1
                    ob = bank[(5, 6)[(n // 8) % 2]][:, 64 * (n % 8):64 * (n % 8) + 64]
                    pe.wait_ge(S["pt_evac"], n + 1)
                    pe.wait_ge(S["ptc_evac"], n + 1)
                    if n % 8 == 0 and n >= 16:
                        pe.wait_ge(S["o_evac"], n // 8 - 1)
                    pt = PT[:, n % 2, :]
                    mm(ob, pt[0:NBLK, 512:640], vcmp[0:NBLK, 64 * g:64 * g + 64], start=True, stop=False)
                    for b in range(2):
                        for k in range(kb):
                            i = b * kb + k
                            last = mm(ob, pt[:, 128 * i:128 * i + 128], z[:, k, 1280 + 256 * b + 64 * g:1280 + 256 * b + 64 * g + 64],
                                      start=False, stop=(i == 2 * kb - 1))
                    last.then_inc(S["pv_done"], 1)

                scores(0)
                scores(1)
                for n in range(2 * NH):
                    turn(n)
                    if n + 2 < 2 * NH:
                        scores(n + 2)
                    if n:
                        values(n - 1)
                values(2 * NH - 1)
                for t in range(NT):
                    for hf in range(2):
                        pe.wait_ge(S["o_evac"], 2 * t + hf + 1)
                        b = 2 * t + hf
                        if b == 0:
                            pe.wait_ge(S["pt_evac"], 2 * NH)
                        for c in range(4):
                            last = tr(bank[(2, 3, 4, 7)[b]][:, 128 * c:128 * c + 128], o[:, t, 512 * hf + 128 * c:512 * hf + 128 * c + 128], ident)
                        last.then_inc(S["oT_ps"], 1)
                pe.wait_ge(S["oT_evac"], 4)
                project_out(1, oT)

            def moe(L):
                transpose_x(0, S["x_ready"], 4 * L + 1, x_tok, S["xT_ps"])
                pe.wait_ge(S["router_loaded"], 16 * (L + 1))
                pe.wait_ge(S["xT_evac"], 4 * (2 * L + 1))
                for t in range(NT):
                    for k in range(KT):
                        last = mm(bank[0][:, 64 * t:64 * t + 36], moe_xT[:, k, 128 * t:128 * t + 128], wr[:, k, :],
                                  start=(k == 0), stop=(k == KT - 1))
                last.then_inc(S["router_ps"], 1)
                am = rt[:, 256:320].rearrange("p (t e) -> p t e", t=NT)
                pe.wait_ge(S["assign_ready"], L + 1)
                mm(bank[1][:, 0:32], upper, am[:, 0, :], start=True, stop=True)
                mm(bank[1][:, 32:64], upper, am[:, 1, :], start=True, stop=False)
                mm(bank[1][:, 32:64], ones, am[:, 0, :], start=False, stop=True)
                mm(bank[1][:, 64:96], ones, am[:, 0, :], start=True, stop=False)
                mm(bank[1][:, 64:96], ones, am[:, 1, :], start=False, stop=True).then_inc(S["pos_ps"], 1)
                pe.wait_ge(S["pick_ready"], L + 1)
                for c in range(KT):
                    for t in range(NT):
                        last = mm(bank[(2 + c) % 8][:, :], x_tok[:, t, 128 * c:128 * c + 128], pick[:, t, :],
                                  start=(t == 0), stop=(t == NT - 1))
                    last.then_inc(S["gather_ps"], 1)
                pe.wait_ge(S["slot_ready"], L + 1)
                pe.wait_ge(S["gather_act"], 4 * L + 1)
                pe.wait_ge(S["gather_dve"], 4 * L + 1)
                for n in range(2):
                    for c in range(2):
                        for t in range(NT):
                            last = mm(bank[2 + n][:, 256 * c + 128 * t:256 * c + 128 * t + 128],
                                      slotw[:, n, c, t:t + 1].to_broadcast([128, 128]), ident, start=True, stop=True)
                    last.then_inc(S["rows_ps"], 1)
                pe.wait_ge(S["gather_act"], 4 * L + 4)
                pe.wait_ge(S["gather_dve"], 4 * L + 4)

                def gate_up(wg, wu, s):
                    for k in range(KT):
                        mm(bank[4][0:64, :], xw[:, k, :], wg[:, k, :], start=(k == 0), stop=(k == KT - 1))
                        last = mm(bank[4][64:128, :], xw[:, k, :], wu[:, k, :], start=(k == 0), stop=(k == KT - 1))
                    last.then_inc(s, 1)

                def turn(s):
                    for c in range(4):
                        last = tr(bank[5][:, 128 * c:128 * c + 128], gu[:, 128 * c:128 * c + 128], ident)
                    last.then_inc(s, 1)

                def down(wd, hin, s):
                    for k in range(4):
                        mm(bank[6][0:64, :], hin[:, k, :], wd[:, k, 0:512], start=(k == 0), stop=(k == 3))
                        last = mm(bank[6][64:128, :], hin[:, k, :], wd[:, k, 512:1024], start=(k == 0), stop=(k == 3))
                    last.then_inc(s, 1)

                def scatter(s, first=False, end=False, extra=False):
                    for h in range(2):
                        for t in range(NT):
                            last = mm(bank[2 * t + h][:, :], sel[h][:, 128 * t:128 * t + 128], yw, start=first, stop=end,
                                      skip_group_check=extra)
                            if end:
                                last.then_inc(S["resid_ps"], 1)
                    if not end:
                        last.then_inc(s, 1)

                def arrive(n0, i, k):
                    pe.wait_ge(full[slot_of(n0)], i * 16 + arrived(n0))
                    return ring[:, slot_of(n0), :].rearrange("p (k c) -> p k c", k=k)

                def expert_in(e, r, i):
                    pe.wait_ge(S["xw_ready"], e + (NE * L + 1))
                    wg, wu = [arrive(EXP_BASE[L] + 3 * r + k, i, KT) for k in range(2)]
                    gate_up(wg, wu, S["gu_done"])

                def expert_turn(e):
                    pe.wait_ge(S["gu_evac"], e + (NE * L + 1))
                    turn(S["turn_done"])

                def expert_down(e, r, i):
                    pe.wait_ge(S["h_ready"], e + (NE * L + 1))
                    down(arrive(EXP_BASE[L] + 3 * r + 2, i, 4), hT, S["down_done"])

                def expert_out(e, first=False, end=False):
                    pe.wait_ge(S["y_evac"], e + (NE * L + 1))
                    pe.wait_ge(S["sel_ready"], e + (NE * L + 1))
                    scatter(S["sc_out"], first, end)

                expert_in(0, 0, 0)
                expert_turn(0)
                expert_in(1, 1, 0)
                expert_down(0, 0, 0)
                expert_turn(1)
                pe.wait_ge(S["rows_evac"], 2 * (L + 1))
                expert_out(0, first=True)
                expert_in(2, 2, 0)
                expert_down(1, 1, 0)
                expert_turn(2)
                expert_out(1)
                with pe.Fori(0, 9) as i:
                    for r in range(3, 6):
                        expert_in(i * 3 + r, r, i)
                        expert_down(i * 3 + (r - 1), r - 1, i)
                        expert_turn(i * 3 + r)
                        expert_out(i * 3 + (r - 1))
                for e in (30, 31):
                    expert_in(e, e, 0)
                    expert_down(e - 1, e - 1, 0)
                    expert_turn(e)
                    expert_out(e - 1)
                pe.wait_ge(S["h_ready"], NE * (L + 1))
                most = pe.value_load(mxi[0:1, 0:1], min_val=0, max_val=SEQ)
                with pe.If(most > WIN):
                    v = ovf[L]
                    wg, wu = [ring[:, slot_of(EXP_BASE[L] + k), :].rearrange("p (k c) -> p k c", k=KT) for k in range(2)]
                    wd = ring[:, slot_of(EXP_BASE[L] + 2), :].rearrange("p (k c) -> p k c", k=4)
                    with pe.Fori(0, NE) as e:
                        for n in ("gate_in", "up_in", "down_in"):
                            pe.wait_ge(v[n], e * 16 + 16)
                        for w in range(1, NWIN):
                            c = e * (NWIN - 1) + w
                            pe.wait_ge(v["xw"], c)
                            gate_up(wg, wu, v["gu"])
                            pe.wait_ge(v["gu_evac"], c)
                            turn(v["turn"])
                            pe.wait_ge(v["h"], c)
                            down(wd, hT2, v["down"])
                            pe.wait_ge(v["y_evac"], c)
                            pe.wait_ge(v["sel"], 2 * c)
                            scatter(v["out"], extra=True)
                expert_down(31, 31, 0)
                expert_out(31, end=True)

            pe.wait_ge(S["consts_loaded"], 16)
            mixer0()
            moe(0)
            mixer1()
            moe(1)

        @block.scalar
        def _(act):
            fn = nc.scalar.activation
            act.dma_start(par[:, :], a["params"]).then_inc(S["params_loaded"], 16)
            act.dma_start(wbd, a["wbd"]).then_inc(S["params_loaded"], 16)
            act.dma_start(cst[:, :], a["consts"]).then_inc(S["consts_loaded"], 16)
            act.dma_start(x_tok[:, :, :], a["x"][0].rearrange("(t p) d -> p t d", p=128)).then_inc(S["x_loaded"], 16)

            def evac_T(dst, s_ps, base, s_done, banks=(4, 5, 6, 7)):
                for t in range(NT):
                    for hf in range(2):
                        act.wait_ge(s_ps, base + 2 * t + hf + 1)
                        fn(dst[:, 4 * hf:4 * hf + 4, 128 * t:128 * t + 128],
                           bank[banks[2 * t + hf]][:, :].rearrange("p (c t) -> p c t", c=4), ACT.Copy).then_inc(s_done, 1)

            def layernorm(q):
                act.wait_ge(S["consts_loaded"], 16)
                act.wait_ge(S["var_ready"], 2 * (q + 1))
                fn(sd[:, :], mv[:, :, 1], ACT.Sqrt, bias=eps).then_inc(S["sd_ready"], 1)

            def mixer0():
                act.wait_ge(S["softplus_e"], 1)
                fn(sp_t[:, 2, :], sp_t[:, 1, :], ACT.Exp, scale=-1.0).then_inc(S["act_step"], 1)
                act.wait_ge(S["pads_zeroed"], 1)
                for b in range(2):
                    act.wait_ge(S["z0_done"], b + 1)
                    fn(xl[:, 2 * b:2 * b + 2, 3:259], bank[b][:, :].rearrange("p (c t) -> p c t", c=2), ACT.Copy).then_inc(S["z0_act"], 1)
                for b in range(2):
                    act.wait_ge(S["z0_done"], 2 + b + 1)
                    fn(gate[:, 2 * b:2 * b + 2, :], bank[2 + b][:, :].rearrange("p (c t) -> p c t", c=2), ACT.Gelu_apprx_tanh).then_inc(S["z0_act"], 1)
                for g in range(8):
                    act.wait_ge(S["gate_ps"], g // 2 + 1)
                    dst = (rg if g < 4 else ig)[:, g % 4, :]
                    bias = par[:, (P_BA if g < 4 else P_BX) + g % 4:(P_BA if g < 4 else P_BX) + g % 4 + 1]
                    fn(dst, bank[4 + g // 2][:, 256 * (g % 2):256 * (g % 2) + 256], ACT.Sigmoid, bias=bias).then_inc(S["gate_sig"], 1)
                act.wait_ge(S["softplus_done"], 1)
                act.wait_ge(S["gate_sig"], 8)
                for c in range(4):
                    fn(th[:, c, :], rg[:, c, :], ACT.Tanh, scale=sp_t[:, 4, c:c + 1]).then_inc(S["lru_T"], 1)
                act.wait_ge(S["lru_T"], 4)
                for c in range(4):
                    fn(rg[:, c, :], rg[:, c, :], ACT.Exp, scale=sp_t[:, 5, c:c + 1]).then_inc(S["lru_exp"], 1)
                act.wait_ge(S["lru_m2"], 1)
                fn(th[:, :, :], th[:, :, :], ACT.Sqrt, scale=2.0).then_inc(S["lru_mult"], 1)
                act.wait_ge(S["pads_zeroed"], 2)
                for b in range(2):
                    act.wait_ge(S["z0_done"], 4 + b + 1)
                    fn(cghc[:, 2 * b:2 * b + 2, 2:258], bank[b][:, :].rearrange("p (c t) -> p c t", c=2), ACT.Copy).then_inc(S["z0_act"], 1)

            def mixer1():
                evac_T(xT1, S["xT_ps"], 4, S["xT_evac"])
                for c in range(5):
                    for t in range(NT):
                        act.wait_ge(S["z1_done"], 2 * c + t + 1)
                        bk = bank[2 * (c % 2) + t]
                        if c < 2:
                            fn(z[:, t, 512 * c:512 * c + 512], bk[:, :], ACT.Copy).then_inc(S["z1_evac"], 1)
                            continue
                        if c > 2:
                            act.wait_ge(S["z1_rope"], 4 + 2 * (c - 3) + t + 1)
                        if c == 2:
                            src = bk[:, 256:512].rearrange("p (g d) -> p g d", g=NKV)
                            for u in range(2):
                                fn(kd[:, 1, t, :, u, :], src, ACT.Copy).then_inc(S["act_step"], 1)
                        else:
                            fn(z[:, t, 1280 + 256 * (c - 3):1536 + 256 * (c - 3)], bk[:, 256:512], ACT.Copy).then_inc(S["act_step"], 1)
                        fn(z[:, t, 1024:1280], bk[:, 0:256], ACT.Copy).then_inc(S["z1_evac"], 1)
                act.wait_ge(S["z1_done"], 11)
                fn(gates[:, :, :], bank[4][:, 0:128].rearrange("p (t c) -> p t c", t=NT)[:, :, 0:GL], ACT.Sigmoid).then_inc(S["z1_evac"], 1)
                for n in range(2):
                    lo = CT2[n][0]
                    for t in range(NT):
                        act.wait_ge(S["ct_ps"], 2 * n + t + 1)
                        v0 = w_(lo, 1024, 64).rearrange("p (g t) -> p g t", g=NKV)
                        v1 = w_(lo, 1024, 64, 64).rearrange("p (g t) -> p g t", g=NKV)
                        src = bank[5 + t][:, :].rearrange("p (g t) -> p g t", g=NKV)
                        s0 = 1 - t
                        fn(v1[:, :, 128 * t - 1 + s0:128 * t + 127], src[64:128, :, s0:128], ACT.Copy).then_inc(S["act_step"], 1)
                        fn(v0[:, :, 128 * t:128 * t + 128], src[0:64, :, :], ACT.Copy).then_inc(S["ct_evac"], 1)
                act.wait_ge(S["blk_ready"], 2)
                for n in range(2):
                    for t in range(NT):
                        act.wait_ge(S["kT_ps"], 2 * n + t + 1)
                        fn(kT[n][:, :, 128 * t:128 * t + 128], bank[2 * n + t][:, :].rearrange("p (g t) -> p g t", g=NKV), ACT.Copy).then_inc(S["kT_evac"], 1)
                for n in range(2):
                    for m in range(2):
                        act.wait_ge(S["cmp1_done"], 2)
                        fn(hC[:, n, m, :], bank[7][:, 128 * n + 64 * m:128 * n + 64 * m + 60], ACT.Gelu_apprx_tanh).then_inc(S["cmp1_gelu"], 1)
                act.wait_ge(S["cmp2_done"], 1)
                fn(kcT, bank[4][:, 0:60], ACT.Copy).then_inc(S["cmp2_evac"], 1)
                fn(vcmp, bank[4][0:NBLK, 64:320], ACT.Copy).then_inc(S["cmp2_evac"], 1)
                for t in range(NT):
                    for hf in range(2):
                        act.wait_ge(S["qT_ps"], 2 * t + hf + 1)
                        fn(qT[:, 4 * hf:4 * hf + 4, 128 * t:128 * t + 128],
                           bank[2 * t + hf][:, :].rearrange("p (c t) -> p c t", c=4), ACT.Copy).then_inc(S["qT_evac"], 1)
                act.wait_ge(S["pc_sub"], 1)
                fn(pc[:, :, :, 0:NBLK], pc[:, :, :, 0:NBLK], ACT.Exp).then_inc(S["pc_exp"], 1)

                def exps(n):
                    N = 128 * (n // NH + 1)
                    act.wait_ge(S["nm_ready"], n + 1)
                    if n >= 2:
                        act.wait_ge(S["pt_ps"], n - 1)
                    for b in range(2):
                        fn(P[:, n % 2, b * N:b * N + N], bank[n % 2][:, b * N:b * N + N], ACT.Exp, scale=SCALE,
                           bias=asm[:, n % 2, 2 + b:3 + b], accum_out=asm[:, n % 2, 4 + b:5 + b]).then_inc(S["p_exp"], 1)

                def evac(n):
                    N = 256 * (n // NH + 1)
                    act.wait_ge(S["pt_ps"], n + 1)
                    if n >= 2:
                        act.wait_ge(S["pv_done"], n - 1)
                    fn(PT[:, n % 2, 0:N], bank[2 + n % 2][:, 0:N], ACT.Copy).then_inc(S["pt_evac"], 1)

                exps(0)
                exps(1)
                for n in range(2 * NH):
                    evac(n)
                    if n + 2 < 2 * NH:
                        exps(n + 2)
                evac_T(oT, S["oT_ps"], 0, S["oT_evac"], (2, 3, 4, 7))

            def moe(L):
                evac_T(moe_xT, S["xT_ps"], 8 * L, S["xT_evac"])
                for t in range(NT):
                    act.wait_ge(S["gneg_ready"], L + 1)
                    fn(rt[:, 640 + 4 * t:644 + 4 * t], rt[:, 0:72].rearrange("p (t c) -> p t c", t=NT)[:, t, 0:4], ACT.Exp,
                       bias=rt[:, 120 + t:121 + t], accum_out=rt[:, 122 + t:123 + t]).then_inc(S["gexp_done"], 1)
                for t in range(NT):
                    act.wait_ge(S["eneg_ready"], L + 1)
                    fn(rt[:, 144 + 8 * t:152 + 8 * t], rt[:, 128 + 8 * t:136 + 8 * t], ACT.Exp,
                       bias=rt[:, 160 + t:161 + t], accum_out=rt[:, 162 + t:163 + t]).then_inc(S["eexp_done"], 1)
                for c in range(0, KT, 2):
                    act.wait_ge(S["gather_ps"], 8 * L + c + 1)
                    fn(xsT[:, c, 0:NSLOT], bank[(2 + c) % 8][:, :], ACT.Copy).then_inc(S["gather_act"], 1)
                for n in range(2):
                    act.wait_ge(S["rows_ps"], 2 * L + n + 1)
                    fn(rows[:, n].rearrange("p c t -> p (c t)"), bank[2 + n][:, :], ACT.Copy).then_inc(S["rows_evac"], 1)

                def silu(hout, s):
                    fn(hout, bank[5][:, :].rearrange("p (k u s) -> p k u s", k=4, u=2)[:, :, 0, :], ACT.Silu).then_inc(s, 1)

                def expert(e, first=False):
                    act.wait_ge(S["gu_done"], e + (NE * L + 1))
                    fn(gu, bank[4][:, :], ACT.Copy).then_inc(S["gu_evac"], 1)
                    if not first:
                        act.wait_ge(S["down_done"], e + NE * L)
                        fn(yw, bank[6][:, :], ACT.Copy).then_inc(S["y_evac"], 1)
                    act.wait_ge(S["turn_done"], e + (NE * L + 1))
                    silu(hT, S["silu_done"])

                expert(0, first=True)
                with act.Fori(1, NE) as e:
                    expert(e)
                most = act.value_load(mxi[0:1, 0:1], min_val=0, max_val=SEQ)
                with act.If(most > WIN):
                    v = ovf[L]
                    with act.Fori(0, NE) as e:
                        for w in range(1, NWIN):
                            c = e * (NWIN - 1) + w
                            act.wait_ge(v["gu"], c)
                            fn(gu, bank[4][:, :], ACT.Copy).then_inc(v["gu_evac"], 1)
                            act.wait_ge(v["turn"], c)
                            silu(hT2, v["silu"])
                            act.wait_ge(v["down"], c)
                            fn(yw, bank[6][:, :], ACT.Copy).then_inc(v["y_evac"], 1)
                act.wait_ge(S["down_done"], NE * (L + 1))
                fn(yw, bank[6][:, :], ACT.Copy).then_inc(S["y_evac"], 1)

            mixer0()
            layernorm(0)
            moe(0)
            layernorm(1)
            mixer1()
            layernorm(2)
            moe(1)
            layernorm(3)

        @block.vector
        def _(dve):
            v = nc.vector
            st = Steps(dve, S["dve_step"])
            step, settle = st.step, st.settle

            def layernorm(q):
                L, which = q // 2, q % 2
                g, b = gb_view(L, which)
                if q == 0:
                    dve.wait_ge(S["x_loaded"], 16)
                order = [(t, h) for h in range(2) for t in range(NT)]
                for n, (t, h) in enumerate(order):
                    dve.wait_ge(S["resid_ps"], 4 * q + n + 1)
                    xs = x_tok[:, t, 512 * h:512 * h + 512]
                    step(v.scalar_tensor_tensor(xs, xs, ALPHA, bank[2 * t + h][:, :], ALU.mult, ALU.add))
                settle()
                for t, h in order:
                    step(v.bn_stats(stats[:, t, h, :], x_tok[:, t, 512 * h:512 * h + 512]))
                settle()
                for t in range(NT):
                    v.bn_aggr(mv[:, t, :], stats[:, t, :, :].rearrange("p h s -> p (h s)")).then_inc(S["var_ready"], 1)
                dve.wait_ge(S["sd_ready"], q + 1)
                step(v.reciprocal(rstd[:, :], sd[:, :]))
                settle()
                for t in range(NT):
                    step(v.tensor_scalar(x_tok[:, t, :], x_tok[:, t, :], mv[:, t, 0:1], rstd[:, t:t + 1], ALU.subtract, ALU.mult))
                dve.wait_ge(S["gb_loaded"], 32 * (q + 1))
                settle()
                for t in range(NT):
                    step(v.tensor_tensor(x_tok[:, t, :], x_tok[:, t, :], g, ALU.mult))
                settle()
                for t in range(NT):
                    v.tensor_tensor(x_tok[:, t, :], x_tok[:, t, :], b, ALU.add).then_inc(S["x_ready"], 1)

            def mixer0():
                dve.wait_ge(S["params_loaded"], 32)
                lam = par[:, P_LAM:P_LAM + 4]
                step(v.tensor_scalar(sp_t[:, 0, :], lam, -1.0, 0.0, ALU.mult, ALU.max))
                step(v.tensor_scalar(sp_t[:, 3, :], lam, -1.0, None, ALU.mult))
                settle()
                v.tensor_tensor(sp_t[:, 1, :], lam, sp_t[:, 3, :], ALU.max).then_inc(S["softplus_e"], 1)
                dve.wait_ge(S["act_step"], 1)
                y, s_, s2, p = sp_t[:, 2, :], sp_t[:, 1, :], sp_t[:, 3, :], sp_t[:, 4, :]
                step(v.tensor_scalar(p, y, 2.0, None, ALU.add))
                settle()
                step(v.reciprocal(s2, p))
                settle()
                step(v.tensor_tensor(s_, y, s2, ALU.mult))
                settle()
                step(v.tensor_tensor(s2, s_, s_, ALU.mult))
                settle()
                step(v.tensor_scalar(p, s2, 1.0 / 17, 1.0 / 15, ALU.mult, ALU.add))
                for c in (13, 11, 9, 7, 5, 3, 1):
                    settle()
                    step(v.tensor_tensor(p, p, s2, ALU.mult))
                    settle()
                    step(v.tensor_scalar(p, p, 1.0 / c, None, ALU.add))
                settle()
                step(v.tensor_tensor(p, p, s_, ALU.mult))
                settle()
                step(v.scalar_tensor_tensor(s2, p, 2.0, sp_t[:, 0, :], ALU.mult, ALU.add))
                settle()
                step(v.tensor_scalar(sp_t[:, 4, :], s2, 8.0, None, ALU.mult))
                v.tensor_scalar(sp_t[:, 5, :], s2, -8.0, None, ALU.mult).then_inc(S["softplus_done"], 1)
                settle()
                for c in range(4):
                    dve.wait_ge(S["z0_act"], c // 2 + 1)
                    step(v.tensor_scalar(xc[:, c, :], xl[:, c, 0:256], par[:, P_LCONV + 4 * c:P_LCONV + 4 * c + 1],
                                         par[:, P_LCB + c:P_LCB + c + 1], ALU.mult, ALU.add))
                for k in range(1, 4):
                    settle()
                    for c in range(4):
                        ins = v.scalar_tensor_tensor(xc[:, c, :], xl[:, c, k:k + 256],
                                                     par[:, P_LCONV + 4 * c + k:P_LCONV + 4 * c + k + 1], xc[:, c, :], ALU.mult, ALU.add)
                        if k < 3:
                            step(ins)
                        else:
                            ins.then_inc(S["xc_ready"], 1)
                dve.wait_ge(S["xc_ready"], 4)
                dve.wait_ge(S["lru_T"], 4)
                m2 = yT[:, 4:8, :]
                step(v.tensor_scalar(m2, th, 1.0, None, ALU.add))
                dve.wait_ge(S["gate_sig"], 8)
                step(v.tensor_tensor(ig, ig, xc, ALU.mult))
                settle()
                step(v.reciprocal(m2, m2))
                settle()
                v.tensor_tensor(th, th, m2, ALU.mult).then_inc(S["lru_m2"], 1)
                dve.wait_ge(S["lru_mult"], 1)
                step(v.tensor_tensor(ig, ig, th, ALU.mult))
                settle()
                for c in range(4):
                    dve.wait_ge(S["lru_exp"], c + 1)
                    step(v.tensor_tensor_scan(yT[:, 4 + c, :], rg[:, c, :], ig[:, c, :], 0.0, ALU.mult, ALU.add))
                settle()
                dve.wait_ge(S["z0_act"], 4)
                for c in range(4):
                    v.tensor_tensor(yT[:, 4 + c, :], yT[:, 4 + c, :], gate[:, c, :], ALU.mult).then_inc(S["ylru_ready"], 1)
                for b in range(2):
                    dve.wait_ge(S["z0_act"], 4 + b + 1)
                    dve.wait_ge(S["z0_done"], 6 + b + 1)
                    cv = cghc[:, 2 * b:2 * b + 2, 2:258]
                    v.tensor_tensor(cv, bank[2 + b][:, :].rearrange("p (c t) -> p c t", c=2), cv, ALU.mult).then_inc(S["z0_dve"], 1)
                for c in range(4):
                    dve.wait_ge(S["z0_dve"], c // 2 + 1)
                    step(v.tensor_scalar(yT[:, c, :], cghc[:, c, 0:256], par[:, P_CONV + 3 * c:P_CONV + 3 * c + 1], None, ALU.mult))
                for k in range(1, 3):
                    settle()
                    for c in range(4):
                        step(v.scalar_tensor_tensor(yT[:, c, :], cghc[:, c, k:k + 256],
                                                    par[:, P_CONV + 3 * c + k:P_CONV + 3 * c + k + 1], yT[:, c, :], ALU.mult, ALU.add))
                settle()
                for b in range(2):
                    dve.wait_ge(S["z0_done"], 8 + b + 1)
                    yv = yT[:, 2 * b:2 * b + 2, :]
                    v.tensor_tensor(yv, bank[b][:, :].rearrange("p (c t) -> p c t", c=2), yv, ALU.mult).then_inc(S["z0_dve"], 1)

            def rotate(src, dst, t, H, s_done):
                cs = rope[:, t, 0, :].unsqueeze(1).to_broadcast([128, H, 32])
                sn = rope[:, t, 1, :].unsqueeze(1).to_broadcast([128, H, 32])
                tm = rtmp[:, 0:64 * H].rearrange("p (h d) -> p h d", h=H)
                step(v.tensor_tensor(tm[:, :, 0:32], src[:, :, 32:64], sn, ALU.mult))
                step(v.tensor_tensor(tm[:, :, 32:64], src[:, :, 0:32], sn, ALU.mult))
                settle()
                step(v.tensor_tensor(dst[:, :, 0:32], src[:, :, 0:32], cs, ALU.mult))
                step(v.tensor_tensor(dst[:, :, 32:64], src[:, :, 32:64], cs, ALU.mult))
                settle()
                step(v.tensor_tensor(dst[:, :, 0:32], dst[:, :, 0:32], tm[:, :, 0:32], ALU.subtract))
                v.tensor_tensor(dst[:, :, 32:64], dst[:, :, 32:64], tm[:, :, 32:64], ALU.add).then_inc(s_done, 1)
                settle()

            def mixer1():
                dve.wait_ge(S["l1small_loaded"], 96)
                nr = 0
                for c in range(2):
                    for t in range(NT):
                        dve.wait_ge(S["z1_evac"], 2 * c + t + 1)
                        q = z[:, t, 512 * c:512 * c + 512].rearrange("p (h d) -> p h d", d=64)
                        rotate(q, q, t, 8, S["z1_rope"])
                        nr += 1
                        dve.wait_ge(S["z1_rope"], nr)
                for c in range(2, 5):
                    n = (0, 2, 3)[c - 2]
                    for t in range(NT):
                        dve.wait_ge(S["z1_evac"], 2 * c + t + 1)
                        rotate(z[:, t, 1024:1280].rearrange("p (g d) -> p g d", d=64), kd[:, n, t, :, 0, :], t, NKV, S["z1_rope"])
                        nr += 1
                        dve.wait_ge(S["z1_rope"], nr)
                        v.tensor_copy(kd[:, n, t, :, 1, :], kd[:, n, t, :, 0, :]).then_inc(S["kdup_done"], 1)
                dve.wait_ge(S["l1small_loaded"], 96)
                for n in range(2):
                    dve.wait_ge(S["ct_evac"], 2 * n + 2)
                    if n == 0:
                        dve.wait_ge(S["ct_ps"], 4)
                    ct = w_(CT2[n][0], 1024).rearrange("p (g t) -> p g t", g=NKV)
                    for g in range(NKV):
                        lo = ct[:, g, 0:240].rearrange("p (b k u) -> p k b u", b=15, u=2)[:, :, :, 0]
                        hi = ct[:, g, 16:256].rearrange("p (b k u) -> p k b u", b=15, u=2)[:, :, :, 0]
                        for half, src in ((0, lo), (1, hi)):
                            ins = v.tensor_tensor(blk[n][:, 8 * half:8 * half + 8, g, :], src,
                                                  pe_[:, n, 8 * half:8 * half + 8].unsqueeze(2).to_broadcast([128, 8, 15]), ALU.add)
                            if g == NKV - 1 and half:
                                settle()
                                ins.then_inc(S["blk_ready"], 1)
                            else:
                                step(ins)
                dve.wait_ge(S["qT_ps"], 4)
                for par_ in range(2):
                    dve.wait_ge(S["sc_cmp"], par_ + 1)
                    src = bank[5 + par_][:, 0:256].rearrange("p (t j c) -> p t j c", t=NT, c=16)
                    dst = pc.rearrange("p t (j u) c -> p t j u c", u=2)
                    for t in range(NT):
                        step(v.scalar_tensor_tensor(dst[:, t, :, par_, 0:NBLK], src[:, t, :, 0:NBLK], SCALE,
                                                    cmp_add[:, t, 0:NBLK].unsqueeze(1).to_broadcast([128, 8, NBLK]), ALU.mult, ALU.add))
                settle()
                pv = pc[:, :, :, 0:NBLK]
                step(v.tensor_reduce(cmx[:, :, :], pv, axis=AX.X, op=ALU.max))
                settle()
                v.tensor_tensor(pv, pv, cmx[:, :, :].unsqueeze(3).to_broadcast([128, NT, NH, NBLK]), ALU.subtract).then_inc(S["pc_sub"], 1)
                dve.wait_ge(S["pc_exp"], 1)
                step(v.tensor_tensor(pv, pv, cmp_mul[:, :, 0:NBLK].unsqueeze(2).to_broadcast([128, NT, NH, NBLK]), ALU.mult))
                settle()
                step(v.tensor_reduce(cmx[:, :, :], pv, axis=AX.X, op=ALU.add))
                settle()
                step(v.tensor_scalar(cmx[:, :, :], cmx[:, :, :], TINY, None, ALU.max))
                settle()
                step(v.reciprocal(cmx[:, :, :], cmx[:, :, :]))
                settle()
                gv = gates[:, :, :].rearrange("p t (h b) -> p t h b", b=3)
                step(v.tensor_tensor(cmx[:, :, :], cmx[:, :, :], gv[:, :, :, 0], ALU.mult))
                settle()
                v.tensor_tensor(pv, pv, cmx[:, :, :].unsqueeze(3).to_broadcast([128, NT, NH, NBLK]), ALU.mult).then_inc(S["pc_ready"], 1)

                def maxes(n):
                    t = n // NH
                    N = 128 * (t + 1)
                    sc = bank[n % 2][:, 0:2 * N].rearrange("p (b s) -> p b s", b=2)
                    dve.wait_ge(S["sc_done"], n + 1)
                    diag = sc[:, :, 128 * t:128 * t + 128]
                    step(v.tensor_tensor(diag, diag, causal.unsqueeze(1).to_broadcast([128, 2, 128]), ALU.add))
                    settle()
                    step(v.tensor_reduce(asm[:, n % 2, 0:2], sc, axis=AX.X, op=ALU.max))
                    settle()
                    v.tensor_scalar(asm[:, n % 2, 2:4], asm[:, n % 2, 0:2], -SCALE, None, ALU.mult).then_inc(S["nm_ready"], 1)

                def scales(n):
                    t, h = n // NH, n % NH
                    dve.wait_ge(S["p_exp"], 2 * n + 2)
                    step(v.reciprocal(arec[:, n % 2, :], asm[:, n % 2, 4:6]))
                    settle()
                    v.tensor_tensor(arec[:, n % 2, :], arec[:, n % 2, :], gv[:, t, h, 1:3], ALU.mult).then_inc(S["rs_ready"], 1)

                def evac_c(n):
                    dve.wait_ge(S["pt_ps"], n + 1)
                    if n >= 2:
                        dve.wait_ge(S["pv_done"], n - 1)
                    v.tensor_copy(PT[0:NBLK, n % 2, 512:640], bank[4 if n % 2 else 7][0:NBLK, 0:128]).then_inc(S["ptc_evac"], 1)

                maxes(0)
                maxes(1)
                for n in range(2 * NH):
                    if n >= 2:
                        dve.wait_ge(S["p_norm"], n - 1)
                    scales(n)
                    evac_c(n)
                    if n + 2 < 2 * NH:
                        maxes(n + 2)
                    if n % 8 == 0 and n:
                        q = n // 8 - 1
                        dve.wait_ge(S["pv_done"], n)
                        v.tensor_copy(o[:, q // 2, 512 * (q % 2):512 * (q % 2) + 512], bank[(5, 6)[q % 2]][:, :]).then_inc(S["o_evac"], 1)
                dve.wait_ge(S["pv_done"], 2 * NH)
                v.tensor_copy(o[:, 1, 512:1024], bank[6][:, :]).then_inc(S["o_evac"], 1)

            def moe(L):
                lg = rt[:, 0:72].rearrange("p (t c) -> p t c", t=NT)
                g8 = rt[:, 72:88].rearrange("p (t c) -> p t c", t=NT)
                gm = rt[:, 88:104].rearrange("p (t c) -> p t c", t=NT)
                gi = rt[:, 104:120].rearrange("p (t c) -> p t c", t=NT)
                oh = rt[:, 112:120].rearrange("p (t c) -> p t c", t=NT)
                le = rt[:, 128:144].rearrange("p (t c) -> p t c", t=NT)
                pr = rt[:, 144:160].rearrange("p (t c) -> p t c", t=NT)
                ev = rt[:, 168:184].rearrange("p (t c) -> p t c", t=NT)
                ei = rt[:, 184:200].rearrange("p (t c) -> p t c", t=NT)
                gidx, eidx, wsum = rt[:, 200:202], rt[:, 202:206].rearrange("p (t c) -> p t c", t=NT), rt[:, 206:208]
                am = rt[:, 256:320].rearrange("p (t e) -> p t e", t=NT)
                onehot = rt[:, 320:448].rearrange("p (c t e) -> p c t e", c=2, t=NT)
                prod = rt[:, 448:576].rearrange("p (c t e) -> p c t e", c=2, t=NT)
                incl, offs, scol = rt[:, 576:608], rt[:, 608:640], rt[:, 640:704].rearrange("p (t e) -> p t e", t=NT)
                offw = rt[:, 0:128].rearrange("p (w e) -> p w e", w=NWIN)
                gif = rt[:, 704:720].bitcast(u32).rearrange("p (t c) -> p t c", t=NT)
                eif = rt[:, 720:736].bitcast(u32).rearrange("p (t c) -> p t c", t=NT)
                slot, wt = slotw[:, 0], slotw[:, 1]
                dve.wait_ge(S["x_ready"], 4 * L + 2)
                step(v.memset(g8, -3.0e38))
                dve.wait_ge(S["router_ps"], L + 1)
                dve.wait_ge(S["rbias_loaded"], 16 * (L + 1))
                step(v.tensor_tensor(lg, bank[0][:, 0:128].rearrange("p (t c) -> p t c", t=NT)[:, :, 0:36],
                                     rbias[:, :].unsqueeze(1).to_broadcast([128, NT, 36]), ALU.add))
                settle()
                step(v.tensor_copy(g8[:, :, 0:4], lg[:, :, 0:4]))
                settle()
                for t in range(NT):
                    step(v.max(gm[:, t, :], g8[:, t, :]))
                settle()
                for t in range(NT):
                    step(v.max_index(gif[:, t, :], gm[:, t, :], g8[:, t, :]))
                v.tensor_scalar(rt[:, 120:122], gm[:, :, 0], -1.0, None, ALU.mult).then_inc(S["gneg_ready"], 1)
                settle()
                step(v.tensor_copy(gidx, gif[:, :, 0]))
                settle()
                for t in range(NT):
                    step(v.tensor_scalar(oh[:, t, :], iota[:, 0:4], gidx[:, t:t + 1], None, ALU.is_equal))
                settle()
                for t in range(NT):
                    step(v.tensor_scalar(le[:, t, :], lg[:, t, 4:12], oh[:, t, 0:1], None, ALU.mult))
                for g in range(1, NG):
                    settle()
                    for t in range(NT):
                        step(v.scalar_tensor_tensor(le[:, t, :], lg[:, t, 4 + 8 * g:12 + 8 * g], oh[:, t, g:g + 1], le[:, t, :], ALU.mult, ALU.add))
                settle()
                step(v.tensor_reduce(rt[:, 164:166], le, axis=AX.X, op=ALU.max))
                settle()
                v.tensor_scalar(rt[:, 160:162], rt[:, 164:166], -1.0, None, ALU.mult).then_inc(S["eneg_ready"], 1)
                dve.wait_ge(S["gexp_done"], 2 * (L + 1))
                step(v.reciprocal(rt[:, 124:126], rt[:, 122:124]))
                dve.wait_ge(S["eexp_done"], 2 * (L + 1))
                step(v.reciprocal(rt[:, 166:168], rt[:, 162:164]))
                settle()
                for t in range(NT):
                    step(v.tensor_scalar(pr[:, t, :], pr[:, t, :], rt[:, 166 + t:167 + t], None, ALU.mult))
                settle()
                for t in range(NT):
                    step(v.max(ev[:, t, :], pr[:, t, :]))
                settle()
                for t in range(NT):
                    step(v.max_index(eif[:, t, :], ev[:, t, :], pr[:, t, :]))
                step(v.tensor_tensor(wsum, ev[:, :, 0], ev[:, :, 1], ALU.add))
                settle()
                step(v.tensor_copy(eidx, eif[:, :, 0:2]))
                step(v.reciprocal(wsum, wsum))
                settle()
                for t in range(NT):
                    step(v.scalar_tensor_tensor(eidx[:, t, :], gidx[:, t:t + 1].to_broadcast([128, 2]), 8.0, eidx[:, t, :], ALU.mult, ALU.add))
                step(v.tensor_tensor(wsum, wsum, rt[:, 124:126], ALU.mult))
                settle()
                for c in range(2):
                    step(v.tensor_tensor(wt[:, c, :], ev[:, :, c], wsum, ALU.mult))
                    for t in range(NT):
                        step(v.tensor_scalar(onehot[:, c, t, :], iota[:, 0:NE], eidx[:, t, c:c + 1], None, ALU.is_equal))
                settle()
                v.tensor_tensor(am, onehot[:, 0], onehot[:, 1], ALU.add).then_inc(S["assign_ready"], 1)
                dve.wait_ge(S["pos_ps"], L + 1)
                cnt = rt[:, 128:160]
                step(v.tensor_copy(cnt, bank[1][:, 64:96]))
                settle()
                step(v.tensor_tensor_scan(incl, ones[:, 0:NE], cnt, 0.0, ALU.mult, ALU.add))
                settle()
                step(v.tensor_tensor(offs, incl, cnt, ALU.subtract))
                settle()
                step(v.tensor_tensor(scol, bank[1][:, 0:64].rearrange("p (t e) -> p t e", t=NT),
                                     offs.unsqueeze(1).to_broadcast([128, NT, NE]), ALU.add))
                settle()
                step(v.tensor_tensor(prod, onehot, scol.unsqueeze(1).to_broadcast([128, 2, NT, NE]), ALU.mult))
                settle()
                v.tensor_reduce(slot, prod, axis=AX.X, op=ALU.add).then_inc(S["slot_ready"], 1)
                dve.wait_ge(S["slot_ready"], L + 1)
                for t in range(NT):
                    step(v.tensor_scalar(pick[:, t, :], iota, slot[:, 0, t:t + 1], None, ALU.is_equal))
                settle()
                for t in range(NT):
                    ins = v.scalar_tensor_tensor(pick[:, t, :], iota, slot[:, 1, t:t + 1], pick[:, t, :], ALU.is_equal, ALU.add)
                    if t == NT - 1:
                        ins.then_inc(S["pick_ready"], 1)
                    else:
                        step(ins)
                        settle()
                for w in range(NWIN):
                    step(v.tensor_scalar(offw[:, w, :], offs, float(WIN * w), float(NSLOT), ALU.add, ALU.min))
                step(v.tensor_reduce(rt[:, 736:737], cnt, axis=AX.X, op=ALU.max))
                settle()
                step(v.tensor_copy(offi[0:1, :], offw[0:1].rearrange("p w e -> p (w e)")))
                settle()
                v.tensor_copy(mxi[0:1, 0:1], rt[0:1, 736:737]).then_inc(S["offs_ready"], 1)
                for c in range(1, KT, 2):
                    dve.wait_ge(S["gather_ps"], 8 * L + c + 1)
                    v.tensor_copy(xsT[:, c, 0:NSLOT], bank[(2 + c) % 8][:, :]).then_inc(S["gather_dve"], 1)
                used = rt[:, 320:448].rearrange("p (w e) -> p w e", w=NWIN)
                for w in range(NWIN):
                    step(v.tensor_scalar(colid[:, w, :], offs, row, float(WIN * w + 1), ALU.add, ALU.add))
                    step(v.tensor_scalar(used[:, w, :], cnt, row, float(WIN * w), ALU.subtract, ALU.is_gt))
                settle()
                step(v.tensor_tensor(colid, colid, used, ALU.mult))
                settle()
                step(v.tensor_scalar(colid, colid, -1.0, None, ALU.add))
                settle()
                dve.wait_ge(S["rows_evac"], 2 * (L + 1))
                dve.wait_ge(S["sel_zeroed"], 2 * (L + 1))

                def times_up(h, s):
                    v.tensor_tensor(h, h, bank[5][:, :].rearrange("p (k u s) -> p k u s", k=4, u=2)[:, :, 1, :], ALU.mult).then_inc(s, 1)

                def select(w, e, s_eq, eq_done, s):
                    for c in range(2):
                        v.scalar_tensor_tensor(eq[c], rows[:, 0, c], colid[:, w, bass.ds(e, 1)], rows[:, 1, c],
                                               ALU.is_equal, ALU.mult).then_inc(s_eq, 1)
                    dve.wait_ge(s_eq, eq_done)
                    for h in range(2):
                        p = slice(64 * h, 64 * h + 64)
                        v.tensor_tensor(sel[h][p, :], eq[0][p, :], eq[1][p, :], ALU.add).then_inc(s[h], 1)

                def expert(e, last=False):
                    dve.wait_ge(S["silu_done"], e + (NE * L + 1))
                    times_up(hT, S["h_ready"])
                    if not last:
                        dve.wait_ge(S["sc_out"], e + (NE - 1) * L)
                        select(0, e, S["eq_done"], e * 2 + (2 * NE * L + 2), (S["sel_half"], S["sel_ready"]))

                dve.wait_ge(S["silu_done"], NE * L + 1)
                times_up(hT, S["h_ready"])
                select(0, 0, S["eq_done"], 2 * NE * L + 2, (S["sel_half"], S["sel_ready"]))
                with dve.Fori(1, NE - 1) as e:
                    expert(e)
                expert(NE - 1, last=True)
                most = dve.value_load(mxi[0:1, 0:1], min_val=0, max_val=SEQ)
                with dve.If(most > WIN):
                    vo = ovf[L]
                    dve.wait_ge(S["sc_out"], (NE - 1) * (L + 1))
                    with dve.Fori(0, NE) as e:
                        for w in range(1, NWIN):
                            c = e * (NWIN - 1) + w
                            select(w, e, vo["eq"], c * 2, (vo["sel"], vo["sel"]))
                            dve.wait_ge(vo["silu"], c)
                            times_up(hT2, vo["h"])
                            dve.wait_ge(vo["out"], c)
                dve.wait_ge(S["sc_out"], (NE - 1) * (L + 1))
                select(0, NE - 1, S["eq_done"], 2 * NE * (L + 1), (S["sel_half"], S["sel_ready"]))

            dve.wait_ge(S["consts_loaded"], 16)
            mixer0()
            layernorm(0)
            moe(0)
            layernorm(1)
            mixer1()
            layernorm(2)
            moe(1)
            layernorm(3)


def constants():
    import numpy as np
    c = np.zeros((128, N_CONST), np.float32)
    i = np.arange(128)
    c[:, C_ID:C_ID + 128] = np.eye(128)
    c[:, C_UP:C_UP + 128] = i[:, None] < i[None, :]
    c[:, C_ONE:C_ONE + 128] = 1.0
    c[:, C_CAUS:C_CAUS + 128] = np.where(i[None, :] <= i[:, None], 0.0, -1e30)
    c[:, C_IOTA:C_IOTA + 512] = np.arange(512)
    c[:, C_EPS] = LN_EPS
    c[:, C_ROW] = i % WIN
    return c


def attention_constants():
    import numpy as np
    c = np.zeros((128, N_ATT), np.float32)
    i = np.arange(128)
    inv = np.float32(10000.0) ** (-np.arange(0, DK, 2, dtype=np.float32) / DK)
    for t in range(NT):
        ang = ((i + 128 * t).astype(np.float32)[:, None] * inv[None, :].astype(np.float32)).astype(np.float32)
        c[:, A_ROPE + 64 * t:A_ROPE + 64 * t + 32] = np.cos(ang)
        c[:, A_ROPE + 64 * t + 32:A_ROPE + 64 * t + 64] = np.sin(ang)
        seen = (16 * np.arange(NBLK) + 31)[None, :] <= (i + 128 * t)[:, None]
        c[:, A_CMPA + 16 * t:A_CMPA + 16 * t + NBLK] = np.where(seen, 0.0, -1e30)
        c[:, A_CMPM + 16 * t:A_CMPM + 16 * t + NBLK] = seen
    return c


def kernel(**inputs):
    import numpy as np
    import concourse.bacc as bacc
    from concourse.bass_utils import run_bass_kernel_spmd as run

    x = {k: np.ascontiguousarray(np.asarray(v)) for k, v in inputs.items()}

    def channels(v):
        v = v.reshape(-1, 4, 128)
        return np.transpose(v, (2, 1, 0)).reshape(128, -1)

    arrays = {"x": x["x"], "xT": np.ascontiguousarray(x["x"][0].T), "consts": constants(),
              "att_consts": attention_constants()}
    arrays["params"] = np.concatenate([channels(x[k]) for k in (
        "l0_conv_w", "l0_lru_conv_w", "l0_lru_conv_b", "l0_lru_b_a", "l0_lru_b_x", "l0_lru_lambda")], axis=1)
    wbd = np.zeros((128, 8, 128), np.float32)
    for n, k in enumerate(("l0_lru_w_a", "l0_lru_w_x")):
        for c in range(4):
            for u in range(2):
                wbd[64 * u:64 * u + 64, 4 * n + c, 64 * u:64 * u + 64] = x[k][2 * c + u]
    arrays["wbd"] = wbd
    arrays["pe"] = np.stack([np.transpose(x[k].reshape(16, 2, 64), (1, 2, 0)).reshape(128, 16)
                             for k in ("l1_cmp_k_pe", "l1_cmp_v_pe")], axis=1)
    for L in range(2):
        arrays[f"wr{L}"] = np.concatenate([x[f"l{L}_router_group_w"], x[f"l{L}_router_expert_w"]], axis=1)
        arrays[f"br{L}"] = np.concatenate([x[f"l{L}_router_group_b"], x[f"l{L}_router_expert_b"]])
    for k in ("l0_w_in l0_w_out l0_ln1_g l0_ln1_b l0_ln2_g l0_ln2_b l1_w_in l1_cmp_k_w1 l1_cmp_k_w2 l1_cmp_v_w1 "
              "l1_cmp_v_w2 l1_w_out l1_ln1_g l1_ln1_b l1_ln2_g l1_ln2_b").split():
        arrays[k] = x[k]
    for L in range(2):
        for k in ("gate", "up", "down"):
            arrays[f"l{L}_expert_w_{k}"] = x[f"l{L}_expert_w_{k}"]

    nc = bacc.Bacc("TRN2", target_bir_lowering=False, num_devices=1)
    arrays = {k: np.ascontiguousarray(v) for k, v in arrays.items()}
    aps = {k: nc.dram_tensor("in_" + k, v.shape, mybir.dt.from_np(v.dtype), kind="ExternalInput").ap()
           for k, v in arrays.items()}
    out = nc.dram_tensor("out", (1, SEQ, D), mybir.dt.float32, kind="ExternalOutput").ap()
    program(nc, aps, out)
    r = run(nc, [{"in_" + k: v for k, v in arrays.items()}], core_ids=[0])
    return r.results[0]["out"]
```

```python
import concourse.bass as bass
from concourse import mybir
from contextlib import ExitStack

SEQ, D, FF, NE, NG = 256, 1024, 512, 32, 4
CW = 512
KT = D // 128
NT = SEQ // 128
WIN = 64
NSLOT = 2 * SEQ
NPAD = NSLOT + WIN
NWIN = SEQ // WIN
ALPHA = (2 * 2) ** 0.25
LN_EPS = 1e-5
NH, DK, NKV = 16, 64, 4
NBLK = SEQ // 16 - 1
NB = NBLK + 1
SCALE = DK ** -0.5
TINY = 1e-30
RING = 9
GL = 48

L0_COLS = [4 * CW, 3 * CW, CW, 2 * CW, 0]
L0_UNITS = 7
L1_UNITS = 9
MIX_BASE = [0, L0_UNITS + 3 * NE]
EXP_BASE = [L0_UNITS, L0_UNITS + 3 * NE + L1_UNITS]

L1_COLS = [2, 3, 4, 0, 1]

C_ID, C_UP, C_ONE, C_CAUS, C_IOTA, C_EPS, C_ROW, C_ALPHA = 0, 128, 256, 384, 512, 1024, 1025, 1026
N_CONST = 1154
A_ROPE, A_CMPA, A_CMPM, A_OWN, N_ATT = 0, 128, 160, 192, 200
P_CONV, P_LCONV, P_LCB, P_BA, P_BX, P_LAM = 0, 12, 28, 32, 36, 40
N_PARAM = 44


def program(nc, a, out):
    f32, i32, u32 = mybir.dt.float32, mybir.dt.int32, mybir.dt.uint32
    ALU, ACT, AX = mybir.AluOpType, mybir.ActivationFunctionType, mybir.AxisListType
    ctx = ExitStack()
    with ctx:
        def sb(name, shape, dt=f32):
            return ctx.enter_context(nc.sbuf_tensor(name, shape, dt))

        def sem(name):
            return ctx.enter_context(nc.semaphore(name))

        ring = sb("ring", [128, RING, 4096])
        x_tok = sb("x_tok", [128, NT, D])
        cst = sb("cst", [128, N_CONST])
        work = sb("work", [128, 12560])
        par = sb("par", [128, N_PARAM])
        sp_t = sb("sp_t", [128, 6, 4])
        stats = sb("stats", [128, NT, 2, 6])
        mv = sb("mv", [128, NT, 2])
        sd = sb("sd", [128, NT])
        rstd = sb("rstd", [128, NT])
        rbias = sb("rbias", [128, 36])
        exp_warm = sb("exp_warm", [128, 1])
        slotw = sb("slotw", [128, 2, 2, NT])
        offi = sb("offi", [1, NWIN * NE], i32)
        mxi = sb("mxi", [1, 1], i32)
        small = sb("small", [128, 176])
        gates = small[:, 0:NT * GL].rearrange("p (t h b) -> p t h b", t=NT, b=3)
        asm = small[:, 96:132].rearrange("p (n c) -> p n c", n=3)
        arec = small[:, 132:144].rearrange("p (n c) -> p n c", n=3)
        cmx = small[:, 144:176].rearrange("p (t h) -> p t h", t=NT)
        bank = [ctx.enter_context(nc.psum_tensor(f"bank{i}", [128, 512], f32)) for i in range(8)]

        def w_(lo, n, parts=128, p0=0):
            return work[p0:p0 + parts, lo:lo + n]

        ident, upper, ones = cst[:, C_ID:C_ID + 128], cst[:, C_UP:C_UP + 128], cst[:, C_ONE:C_ONE + 128]
        causal, iota = cst[:, C_CAUS:C_CAUS + 128], cst[:, C_IOTA:C_IOTA + 512]
        catt = w_(12320, N_ATT)
        rope = catt[:, A_ROPE:A_ROPE + 128].rearrange("p (t s d) -> p t s d", t=NT, s=2)
        cmp_add = catt[:, A_CMPA:A_CMPA + 32].rearrange("p (t c) -> p t c", t=NT)
        cmp_mul = catt[:, A_CMPM:A_CMPM + 32].rearrange("p (t c) -> p t c", t=NT)
        own = catt[:, A_OWN:A_OWN + 8]
        alpha = cst[:, C_ALPHA:C_ALPHA + 128]
        eps = cst[:, C_EPS:C_EPS + 1]
        row = cst[:, C_ROW:C_ROW + 1]

        xT0 = w_(0, 2048).rearrange("p (k t) -> p k t", k=KT)
        xl = w_(2048, 1040).rearrange("p (c t) -> p c t", c=4)
        gate = w_(3088, 1024).rearrange("p (c t) -> p c t", c=4)
        cghc = w_(4112, 1040).rearrange("p (c t) -> p c t", c=4)
        xc = w_(5152, 1024).rearrange("p (c t) -> p c t", c=4)
        rg = w_(6176, 1024).rearrange("p (c t) -> p c t", c=4)
        ig = w_(7200, 1024).rearrange("p (c t) -> p c t", c=4)
        yT = w_(8224, 2048).rearrange("p (k t) -> p k t", k=KT)
        wbd = w_(10272, 1024).rearrange("p (c n) -> p c n", c=8)
        th = w_(11296, 1024).rearrange("p (c t) -> p c t", c=4)
        xsT = w_(0, 8 * NPAD).rearrange("p (k s) -> p k s", k=KT)
        rows = w_(4608, 1024).rearrange("p (n c t) -> p n c t", n=2, c=2)
        xw = w_(5632, 512).rearrange("p (k s) -> p k s", k=KT)
        gu = w_(6144, 512)
        hT = w_(6656, 256).rearrange("p (k s) -> p k s", k=4)
        sel = [w_(6912 + 256 * h, 256) for h in range(2)]
        yw = w_(7424, 512)
        colid = w_(7936, 128).rearrange("p (w e) -> p w e", w=NWIN)
        eq = [w_(8064 + 256 * c, 256) for c in range(2)]
        hT2 = w_(8576, 256).rearrange("p (k s) -> p k s", k=4)
        moe_xT = w_(0, 2048).rearrange("p (k t) -> p k t", k=KT)
        pick = w_(8576, 1024).rearrange("p (t s) -> p t s", t=NT)
        wr = w_(7680, 288).rearrange("p (k n) -> p k n", k=KT)
        rt = w_(11776, 768)
        xT1 = w_(0, 2048).rearrange("p (k t) -> p k t", k=KT)
        qz = w_(2048, 2048).rearrange("p (t a j u d) -> p t a j u d", t=NT, a=2, j=4, u=2)
        vv = w_(4096, 1024).rearrange("p (t b g d) -> p t b g d", t=NT, b=2, g=NKV)
        kd = w_(5120, 2048).rearrange("p (n t g u d) -> p n t g u d", n=2, t=NT, g=NKV, u=2)
        ct = [w_(7168 + 1024 * n, 1024).rearrange("p (g t) -> p g t", g=NKV) for n in range(2)]
        krot = w_(9216, 1024).rearrange("p (b t a c) -> p b t a c", b=2, t=NT, a=2)
        kraw = w_(10240, 512).rearrange("p (n c) -> p n c", n=2)
        rtmp = w_(10752, 512)
        gT = w_(11264, SEQ, GL)
        hc = w_(11264, 256)
        glw = w_(11520, 384).rearrange("p (k n) -> p k n", k=KT)
        w2k = w_(11904, 256).rearrange("p (m n) -> p m n", m=2)
        w2v = w_(12160, 128).rearrange("p (m n) -> p m n", m=2)
        pe_ = w_(12288, 32).rearrange("p (n k) -> p n k", n=2)
        blk = [w_(5120 + 1024 * n, 1024).rearrange("p (k g b) -> p k g b", k=16, g=NKV) for n in range(2)]
        qT = w_(5120, 2048).rearrange("p (t a j q) -> p t a j q", t=NT, a=2, j=4)
        kpad = w_(0, 2048).rearrange("p (a u b t) -> p a u b t", a=2, u=2, b=2)
        hk = w_(7168, 128).rearrange("p (m c) -> p m c", m=2)
        hx = w_(7424, 512).rearrange("p (m a r) -> p m a r", m=2, a=2)
        kcbd = w_(7936, 64).rearrange("p (a u c) -> p a u c", a=2, u=2)
        vbd = w_(8192, 1024).rearrange("p (a h d) -> p a h d", a=2, h=8)
        P = w_(10752, 1536).rearrange("p (n s) -> p n s", n=3)
        pcT = w_(7168, 512).rearrange("p (t a q) -> p t a q", t=NT, a=2)
        pc = w_(10240, 512).rearrange("p (t h c) -> p t h c", t=NT, h=NH)
        oT = [w_(lo, 1024).rearrange("p (k q) -> p k q", k=KT) for lo in (9216, 5120)]
        GB = [2048, 9600]

        S = {n: sem(n) for n in (
            "x0T_ps x0T_act x0T_dve wbd_loaded ident_loaded unit0_half consts_loaded x_loaded params_loaded router_loaded rbias_loaded gb1_loaded gb2_loaded "
            "l1small_loaded pads_zeroed z0_done z0_act z0_dve xc_ready softplus_e softplus_done gate_ps gate_sig "
            "lru_T lru_m2 lru_mult lru_exp ylru_ready resid_ps var_ready sd_ready x_half x_ready xT_ps xT_evac "
            "router_ps gneg_ready gexp_done eneg_ready eexp_done assign_ready pos_ps slot_ready pick_ready "
            "gather_ps gather_act gather_dve rows_ps rows_evac sel_zeroed offs_ready xw_ready gu_done gu_evac turn_done "
            "silu_done h_ready down_done y_evac sel_ready sel_half eq_done sc_out dve_step act_step "
            "z1_done z1_evac z1_rope gl_done gT_ready gl_evac kdup_done ct_ps ct_evac blk_zeroed blk_ready cmp1_done cmp1_gelu hc_ps hc_evac cmp2_done "
            "kc_zeroed kc_evac vbd_ready kT_ps kpad_zeroed kpad_ready qT_ps qT_evac sc_cmp pc_sub pc_exp pc_ready pcT_ps pcT_evac "
            "sc_done nm_ready p_exp rs_ready p_scaled pt_ps pt_evac pv_done "
            "o_evac out_done").split()}
        full = [sem(f"ring_full{i}") for i in range(RING)]
        ovf = [{n: sem(f"ovf{L}_{n}") for n in "gate_in up_in down_in xw gu gu_evac turn silu h down y_evac sel eq out".split()} for L in range(2)]

        block = ctx.enter_context(nc.Block())

        UNITS = 24

        def unit_of(n):
            if n < 8:
                return 0, n // 4, n % 4, (0, 1)
            n -= 8
            return 1, n // 8, n % 8 // 2, (n % 2,)

        BLOCK_END = [3, 7, 15, 23]
        PT = [ring[:, (MIX_BASE[1] + 5 + i) % RING, :] for i in range(2)]

        GATHER = [0, 1, 7, 2, 3, 0, 1, 7]

        def resid(q, t, h):
            return bank[7 if (q, t, h) == (2, 0, 0) else 2 * t + h][:, :]

        def slot_of(n):
            return n % RING

        def arrived(n):
            parts = n // RING + 1
            for h in range(2):
                m = MIX_BASE[1] + 7 + h
                if n >= m and (n - m) % RING == 0:
                    parts += 3
            return 16 * parts

        def gb_view(L, which):
            lo = GB[which]
            return w_(lo, 1024), w_(lo + 1024, 1024)

        class Steps:
            def __init__(self, eng, s):
                self.eng, self.s, self.n = eng, s, 0

            def step(self, ins):
                ins.then_inc(self.s, 1)
                self.n += 1

            def settle(self):
                self.eng.wait_ge(self.s, self.n)

        @block.sync
        def _(sp):
            def load(n, src):
                dst = ring[:, slot_of(n), :].rearrange("p (k c) -> p k c", k=src.shape[1])
                sp.dma_start(dst, src).then_inc(full[slot_of(n)], 16)

            def cols(w, lo, width):
                return w[:, lo:lo + width].rearrange("(k p) c -> p k c", p=128)

            def expert_srcs(L, e):
                g, u, d = a[f"l{L}_expert_w_gate"], a[f"l{L}_expert_w_up"], a[f"l{L}_expert_w_down"]
                if type(e) is int:
                    return [w[e].rearrange("(k p) c -> p k c", p=128) for w in (g, u, d)]
                return [w[bass.ds(e, 1)].rearrange("o (k p) c -> p (o k) c", p=128) for w in (g, u, d)]

            sp.dma_start(ident, a["consts"][:, C_ID:C_ID + 128]).then_inc(S["ident_loaded"], 16)
            sp.dma_start(x_tok[:, :, :], a["x"][0].rearrange("(t p) d -> p t d", p=128)).then_inc(S["x_loaded"], 16)
            for L in range(2):
                base = MIX_BASE[L]
                for n in range(L0_UNITS if L == 0 else L1_UNITS):
                    if L == 0:
                        src = cols(a["l0_w_in"], L0_COLS[n], 512) if n < 5 else cols(a["l0_w_out"], 512 * (n - 5), 512)
                    else:
                        prev = base + n - RING - EXP_BASE[0]
                        used = ("gu_done", "gu_done", "down_done")[prev % 3]
                        sp.wait_ge(S[used], prev // 3 + 1)
                        if n < 5:
                            src = cols(a["l1_w_in"], 512 * L1_COLS[n], 512)
                        elif n < 7:
                            src = cols(a["l1_cmp_k_w1" if n == 5 else "l1_cmp_v_w1"], 0, 256)
                        else:
                            w = a["l1_w_out"][:, 512 * (n - 7):512 * (n - 6)].rearrange("(a u j d) c -> u d a j c", a=2, u=2, j=4)
                            for u in range(2):
                                for x in range(2):
                                    dst = ring[64 * u:64 * u + 64, slot_of(base + n), 2048 * x:2048 * x + 2048]
                                    sp.dma_start(dst.rearrange("p (j c) -> p j c", j=4), w[u, :, x]).then_inc(full[slot_of(base + n)], 16)
                            continue
                    if base + n == 0:
                        half = ring[:, 0, 0:2048].rearrange("p (k c) -> p k c", k=4)
                        sp.dma_start(half, src[:, 0:4]).then_inc(S["unit0_half"], 16)
                        half = ring[:, 0, 2048:4096].rearrange("p (k c) -> p k c", k=4)
                        sp.dma_start(half, src[:, 4:8]).then_inc(full[0], 16)
                        continue
                    load(base + n, src)
                    if base + n == 1:
                        sp.dma_start(wbd, a["wbd"]).then_inc(S["wbd_loaded"], 16)
                    if base + n == 3:
                        sp.dma_start(cst[:, 128:], a["consts"][:, 128:]).then_inc(S["consts_loaded"], 16)
                for e in range(3):
                    for k, src in enumerate(expert_srcs(L, e)):
                        n = EXP_BASE[L] + 3 * e + k
                        m = n - RING - MIX_BASE[L]
                        if m >= 0:
                            if L == 0:
                                sp.wait_ge(*((S["z0_done"], 2 * m + 2) if m < 5 else (S["resid_ps"], m - 2)))
                            else:
                                sp.wait_ge(*((S["z1_done"], 2 * m + 2) if m < 5 else
                                             (S["pv_done"], 4) if m < 7 else (S["resid_ps"], 8 + m - 4)))
                        load(n, src)

                def expert_loads(e, r):
                    for k, src in enumerate(expert_srcs(L, e)):
                        used = ("gu_done", "gu_done", "down_done")[k]
                        sp.wait_ge(S[used], NE * L + e - 2)
                        load(EXP_BASE[L] + 3 * r + k, src)
                with sp.Fori(0, 9) as i:
                    for r in range(3):
                        e = sp.snap(i * 3 + 3 + r)
                        expert_loads(e, r)
                for e in (30, 31):
                    expert_loads(e, e % 3)
                sp.wait_ge(S["offs_ready"], L + 1)
                most = sp.value_load(mxi[0:1, 0:1], min_val=0, max_val=SEQ)
                with sp.If(most > WIN):
                    v = ovf[L]
                    sp.wait_ge(S["down_done"], NE * L + NE - 1)

                    def again(e):
                        srcs = expert_srcs(L, e)
                        if not (type(e) is int and e == 0):
                            sp.wait_ge(v["down"], e * (NWIN - 1))
                        for k, src in enumerate(srcs):
                            dst = ring[:, slot_of(EXP_BASE[L] + k), :].rearrange("p (k c) -> p k c", k=src.shape[1])
                            sp.dma_start(dst, src).then_inc(v[("gate_in", "up_in", "down_in")[k]], 16)
                    again(0)
                    with sp.Fori(1, NE) as e:
                        again(sp.snap(e + 0))
                    sp.wait_ge(v["down"], NE * (NWIN - 1))
            for t in range(NT):
                for h in range(2):
                    sp.wait_ge(S[("x_half", "x_ready")[h]], 6 + t + 1)
                    cs = slice(512 * h, 512 * h + 512)
                    sp.dma_start(out[0, 128 * t:128 * (t + 1), cs], x_tok[:, t, cs]).then_inc(S["out_done"], 16)
            sp.wait_ge(S["out_done"], 64)

        @block.gpsimd
        def _(pool):
            pool.memset(xl[:, :, 0:3], 0.0).then_inc(S["pads_zeroed"], 1)
            pool.memset(cghc[:, :, 0:2], 0.0).then_inc(S["pads_zeroed"], 1)

            def bcast(src, n):
                return src.rearrange("(o n) -> o n", o=1).to_broadcast([128, n])

            def load_gb(L, which):
                g, b = gb_view(L, which)
                k = f"l{L}_ln{which + 1}"
                pool.dma_start(g, bcast(a[k + "_g"], D)).then_inc(S[("gb1_loaded", "gb2_loaded")[which]], 16)
                pool.dma_start(b, bcast(a[k + "_b"], D)).then_inc(S[("gb1_loaded", "gb2_loaded")[which]], 16)

            for L in range(2):
                if L == 1:
                    pool.wait_ge(S["x_ready"], 4)
                    pool.dma_start(glw, a["l1_w_in"][:, 2560:2608].rearrange("(k p) c -> p k c", p=128)).then_inc(S["l1small_loaded"], 16)
                    for u in range(2):
                        pool.dma_start(w2k[:, :, 64 * u:64 * u + 64], a["l1_cmp_k_w2"].rearrange("(m p) c -> p m c", p=128)).then_inc(S["l1small_loaded"], 16)
                    pool.dma_start(w2v, a["l1_cmp_v_w2"].rearrange("(m p) c -> p m c", p=128)).then_inc(S["l1small_loaded"], 16)
                    pool.dma_start(pe_, a["pe"]).then_inc(S["l1small_loaded"], 16)
                    pool.dma_start(catt, a["att_consts"]).then_inc(S["l1small_loaded"], 16)
                    pool.wait_ge(S["ct_ps"], 4)
                    for n in range(2):
                        pool.memset(blk[n][:, :, :, NBLK], 0.0).then_inc(S["blk_zeroed"], 1)
                    pool.wait_ge(S["blk_ready"], 2)
                    pool.memset(kcbd, 0.0).then_inc(S["kc_zeroed"], 1)
                    pool.wait_ge(S["z1_done"], 10)
                    pool.wait_ge(S["kc_zeroed"], 1)
                    for u in range(2):
                        if u:
                            pool.wait_ge(S["kpad_zeroed"], 1)
                        pool.memset(kpad[64 - 64 * u:128 - 64 * u, :, u], 0.0).then_inc(S["kpad_zeroed"], 1)
                    pool.wait_ge(S["kpad_zeroed"], 2)
                    for n in range(UNITS):
                        k = 4 if n < 8 else 2
                        pool.wait_ge(S["rs_ready"], n + 1)
                        pv = P[:, n % 3, :].rearrange("p (k s) -> p k s", k=k)
                        pool.tensor_tensor(pv, pv, arec[:, n % 3, 0:k].unsqueeze(2).to_broadcast([128, k, 512 // k]),
                                           ALU.mult).then_inc(S["p_scaled"], 1)
                if L == 0:
                    pool.wait_ge(S["ylru_ready"], 4)
                else:
                    pool.wait_ge(S["qT_ps"], 4)
                    pool.wait_ge(S["sc_cmp"], 2)
                load_gb(L, 0)
                pool.dma_start(wr, a[f"wr{L}"].rearrange("(k p) n -> p k n", p=128)).then_inc(S["router_loaded"], 16)
                pool.dma_start(rbias[:, :], bcast(a[f"br{L}"], 36)).then_inc(S["rbias_loaded"], 16)
                pool.wait_ge(S["resid_ps"], 8 * L + 4)
                load_gb(L, 1)
                pool.wait_ge(S["x_ready"], 4 * L + 2)
                pool.wait_ge(S["router_ps"], L + 1)
                pool.memset(xsT[:, :, NSLOT:NPAD], 0.0).then_inc(S["pads_zeroed"], 1)
                for h in range(2):
                    pool.wait_ge(*((S["pads_zeroed"], 3 + L) if h == 0 else (S["sel_zeroed"], 2 * L + 1)))
                    pool.memset(sel[h][64 - 64 * h:128 - 64 * h, :], 0.0).then_inc(S["sel_zeroed"], 1)
                pool.wait_ge(S["gather_ps"], 10 * (L + 1))
                pool.wait_ge(S["gather_act"], 5 * (L + 1))
                pool.wait_ge(S["gather_dve"], 5 * (L + 1))
                pool.wait_ge(S["pads_zeroed"], 3 + L)
                pool.wait_ge(S["offs_ready"], L + 1)

                def window(i, s):
                    off = pool.value_load(offi[0:1, bass.ds(i, 1)], min_val=0, max_val=NSLOT)
                    return lambda: pool.tensor_copy(xw, xsT[:, :, bass.ds(off, WIN)]).then_inc(s, 1)

                window(1, S["xw_ready"])()
                with pool.Fori(2, NE) as e:
                    copy = window(e, S["xw_ready"])
                    pool.wait_ge(S["gu_done"], e + NE * L)
                    copy()
                pool.wait_ge(S["gu_done"], NE * (L + 1))
                most = pool.value_load(mxi[0:1, 0:1], min_val=0, max_val=SEQ)
                with pool.If(most > WIN):
                    with pool.Fori(0, NE) as e:
                        for w in range(1, NWIN):
                            window(e + NE * w, ovf[L]["xw"])()
                            pool.wait_ge(ovf[L]["gu"], e * (NWIN - 1) + w)

        @block.tensor
        def _(pe):
            mm, tr = nc.tensor.matmul, nc.tensor.transpose

            def unit(n, k=KT):
                pe.wait_ge(full[slot_of(n)], arrived(n))
                return ring[:, slot_of(n), :].rearrange("p (k c) -> p k c", k=k)

            def keep_clock(n):
                for _ in range(n):
                    mm(bank[6][:, 0:128], ident, ident, start=True, stop=True)

            def transpose_x(t, count):
                for hf in range(2):
                    pe.wait_ge(S[("x_half", "x_ready")[hf]], count)
                    for c in range(4):
                        last = tr(bank[4 + 2 * t + hf][:, 128 * c:128 * c + 128],
                                  x_tok[:, t, 512 * hf + 128 * c:512 * hf + 128 * c + 128], ident)
                    last.then_inc(S["xT_ps"], 1)

            def project_out(L, src, t, h, ks=range(KT)):
                w = unit(MIX_BASE[L] + (5 if L == 0 else 7) + h)
                for k in ks:
                    last = mm(resid(2 * L, t, h), src[t][:, k, :], w[:, k, :], start=(k == 0), stop=(k == KT - 1))
                if ks[-1] == KT - 1:
                    last.then_inc(S["resid_ps"], 1)

            def mixer0():
                pe.wait_ge(S["x_loaded"], 16)
                for t in range(NT):
                    for hf in range(2):
                        for c in range(4):
                            last = tr(bank[2 * t + hf][:, 128 * c:128 * c + 128],
                                      x_tok[:, t, 512 * hf + 128 * c:512 * hf + 128 * c + 128], ident)
                        last.then_inc(S["x0T_ps"], 1)
                pe.wait_ge(S["unit0_half"], 16)
                pe.wait_ge(S["x0T_act"], 2)
                for k in range(KT):
                    if k == 4:
                        pe.wait_ge(S["x0T_dve"], 2)
                        w = unit(0)
                    else:
                        w = ring[:, 0, :].rearrange("p (k c) -> p k c", k=KT)
                    for m in range(4):
                        last = mm(bank[4 + m][:, 0:256], w[:, k, 128 * m:128 * m + 128], xT0[:, k, :], start=(k == 0), stop=(k == KT - 1))
                        if k == KT - 1 and m % 2:
                            last.then_inc(S["z0_done"], 1)
                for u in range(1, 5):
                    w = unit(u)
                    if u >= 3:
                        pe.wait_ge(S["z0_act"], 2 * (u - 1))
                    for m in range(4):
                        for k in range(KT):
                            last = mm(bank[2 * (u % 2) + m // 2][:, 256 * (m % 2):256 * (m % 2) + 256],
                                      w[:, k, 128 * m:128 * m + 128], xT0[:, k, :], start=(k == 0), stop=(k == KT - 1))
                        if m % 2:
                            last.then_inc(S["z0_done"], 1)
                    if u == 1:
                        pe.wait_ge(S["wbd_loaded"], 16)
                        pe.wait_ge(S["xc_ready"], 4)
                        for g in range(8):
                            last = mm(bank[4 + g // 2][:, 256 * (g % 2):256 * (g % 2) + 256], wbd[:, g, :], xc[:, g % 4, :],
                                      start=True, stop=True)
                            if g % 2:
                                last.then_inc(S["gate_ps"], 1)
                pe.wait_ge(S["ylru_ready"], 4)
                pe.wait_ge(S["z0_dve"], 4)
                for t in range(NT):
                    for h in range(2):
                        if t and h:
                            transpose_x(0, 1)
                        project_out(0, [yT[:, :, 128 * u:128 * u + 128] for u in range(NT)], t, h)

            def mixer1():
                for t in range(NT):
                    transpose_x(t, 3 + t)
                pe.wait_ge(S["xT_evac"], 4 * 2)

                def project_in(c, t):
                    w = unit(MIX_BASE[1] + c)
                    if c >= 2:
                        pe.wait_ge(S["z1_evac"], 2 * (c - 2) + t + 1)
                    for k in range(KT):
                        last = mm(bank[2 * (c % 2) + t][:, :], xT1[:, k, 128 * t:128 * t + 128], w[:, k, :],
                                  start=(k == 0), stop=(k == KT - 1))
                    last.then_inc(S["z1_done"], 1)

                def turn_c(n):
                    for t in range(NT):
                        if n == 0:
                            pe.wait_ge(S["kdup_done"], t + 1)
                            pe.wait_ge(S["z1_evac"], t + 1)
                        else:
                            pe.wait_ge(S["ct_evac"], t + 1)
                        for g in range(NKV):
                            last = tr(bank[5 + t][:, 128 * g:128 * g + 128], kd[:, n, t].rearrange("p g u d -> p g (u d)")[:, g, :], ident)
                        last.then_inc(S["ct_ps"], 1)

                def turn_q(t, x, b):
                    for j in range(4):
                        last = tr(bank[b][:, 128 * j:128 * j + 128], qz[:, t, x, j].rearrange("p u d -> p (u d)"), ident)
                    last.then_inc(S["qT_ps"], 1)

                project_in(0, 0)
                project_in(0, 1)
                project_in(1, 0)
                project_in(1, 1)
                pe.wait_ge(S["l1small_loaded"], 96)
                for k in range(KT):
                    last = mm(bank[4][0:GL, 0:SEQ], glw[:, k, :], xT1[:, k, :], start=(k == 0), stop=(k == KT - 1))
                last.then_inc(S["gl_done"], 1)
                turn_c(0)
                project_in(2, 0)
                pe.wait_ge(S["gT_ready"], 1)
                for t in range(NT):
                    last = tr(bank[4][:, 256 + 64 * t:256 + 64 * t + GL], gT[:, 128 * t:128 * t + 128], ident[0:GL, 0:GL])
                last.then_inc(S["gl_done"], 1)
                project_in(2, 1)
                turn_c(1)
                project_in(3, 0)
                project_in(3, 1)
                for b in range(2):
                    pe.wait_ge(S["ct_evac"], 4)
                    pe.wait_ge(S["z1_rope"], 4 + 2 * b)
                    for x in range(2):
                        for t in range(NT):
                            last = tr(bank[5 + b][:, 256 * x + 128 * t:256 * x + 128 * t + 128], krot[:, b, t, x], ident)
                    last.then_inc(S["kT_ps"], 1)
                project_in(4, 0)
                project_in(4, 1)
                w1 = [unit(MIX_BASE[1] + 5 + n, 16) for n in range(2)]
                pe.wait_ge(S["blk_ready"], 2)
                for k in range(16):
                    for n in range(2):
                        last = mm(bank[7][64 * n:64 * n + 64, 0:256], blk[n][:, k].rearrange("p g b -> p (g b)"), w1[n][:, k, :],
                                  start=(k == 0), stop=(k == 15))
                last.then_inc(S["cmp1_done"], 1)
                for t in range(NT):
                    pe.wait_ge(S["z1_rope"], 7 + t)
                    turn_q(t, 0, 2 + t)
                pe.wait_ge(S["cmp1_gelu"], 1)
                for m in range(2):
                    last = tr(bank[7][:, 256 + 128 * m:384 + 128 * m], hc[:, 128 * m:128 * m + 128], ident)
                last.then_inc(S["hc_ps"], 1)

                def compress():
                    pe.wait_ge(S["hc_evac"], 3)
                    pe.wait_ge(S["kpad_ready"], 2)
                    for m in range(2):
                        mm(bank[5][:, 0:64], w2k[:, m, :], hk[:, m, :], start=(m == 0), stop=(m == 1))
                    for x in range(2):
                        for m in range(2):
                            last = mm(bank[5][:, 64 + 64 * x:128 + 64 * x], hx[:, m, x, :], w2v[:, m, :], start=(m == 0), stop=(m == 1))
                    last.then_inc(S["cmp2_done"], 1)

                def scores(n):
                    t, x, j, us = unit_of(n)
                    N = 512 // len(us)
                    if n == 0:
                        pe.wait_ge(S["z1_evac"], 10)
                        pe.wait_ge(S["kpad_ready"], 4)
                        pe.wait_ge(S["qT_evac"], 2)
                    if n == 4:
                        pe.wait_ge(S["qT_evac"], 4)
                    if n >= 3:
                        pe.wait_ge(S["p_exp"], n - 2)
                    for i, u in enumerate(us):
                        last = mm(bank[n % 3][:, N * i:N * i + N], qT[:, t, x, j], kpad[:, x, u, :, 0:128 * (t + 1)], start=True, stop=True)
                    last.then_inc(S["sc_done"], 1)

                def turn(n):
                    if n >= 2:
                        pe.wait_ge(S["pt_evac"], n - 1)
                    if n < 2:
                        pe.wait_ge(S["qT_evac"], 4)
                    pe.wait_ge(S["p_scaled"], n + 1)
                    for i in range(4):
                        last = tr(bank[3 + n % 2][:, 128 * i:128 * i + 128], P[:, n % 3, 128 * i:128 * i + 128], ident)
                    last.then_inc(S["pt_ps"], 1)

                def values(B):
                    t, x = B // 2, B % 2
                    pe.wait_ge(S["pt_evac"], BLOCK_END[B] + 1)
                    if B == 0:
                        pe.wait_ge(S["vbd_ready"], 2)
                        pe.wait_ge(S["kc_evac"], 2)
                    if B >= 2:
                        pe.wait_ge(S["o_evac"], B - 1)
                    ob = bank[5 + x]
                    if t == 0:
                        pt = PT[x][:, 0:2048].rearrange("p (j u b q) -> p u b j q", j=4, u=2, b=2)
                    else:
                        pt = PT[x].rearrange("p (j u b q) -> p u b j q", j=4, u=2, b=4)
                    parts = 2 * (t + 1)

                    def add(i, first=False, end=False):
                        for u in range(2):
                            last = mm(ob[64 * u:64 * u + 64, :], vv[:, i % (t + 1), i // (t + 1), 2 * x + u, :], pt[:, u, i],
                                      start=first, stop=end)
                        return last
                    for i in range(parts - 1):
                        add(i, first=(i == 0))
                    if B == 0:
                        pe.wait_ge(S["pcT_evac"], 1)
                    for j in range(4):
                        for u in range(2):
                            mm(ob[64 * u:64 * u + 64, 128 * j:128 * j + 128], vbd[:, x, 2 * j + u, :], pcT[:, t, x, :], start=False, stop=False)
                    add(parts - 1, end=True).then_inc(S["pv_done"], 1)

                scores(0)
                scores(1)
                scores(2)
                compress()
                for t in range(NT):
                    pe.wait_ge(S["z1_rope"], 9 + t)
                    if t == 0:
                        pe.wait_ge(S["gl_evac"], 4)
                    else:
                        pe.wait_ge(S["qT_evac"], 2)
                    turn_q(t, 1, 4 - t)
                def scores_c(t):
                    pe.wait_ge(S["qT_evac"], 3 + t)
                    pe.wait_ge(S["kc_evac"], 2)
                    for x in range(2):
                        for j in range(4):
                            lo = 32 * (8 * t + 4 * x + j)
                            last = mm(bank[7][:, lo:lo + 32], qT[:, t, x, j], kcbd[:, x].rearrange("p u c -> p (u c)"), start=True, stop=True)
                    last.then_inc(S["sc_cmp"], 1)

                for n in range(UNITS):
                    if n + 3 < UNITS:
                        scores(n + 3)
                    if n == 0:
                        scores_c(0)
                    turn(n)
                    if n == 1:
                        scores_c(1)
                    if n == 5:
                        pe.wait_ge(S["pc_ready"], 1)
                        for t in range(NT):
                            for x in range(2):
                                last = tr(bank[7][:, 256 * t + 128 * x:256 * t + 128 * x + 128],
                                          pc[:, t, 8 * x:8 * x + 8].rearrange("p h c -> p (h c)"), ident)
                        last.then_inc(S["pcT_ps"], 1)
                    if n == 6:
                        values(0)
                    if n > 6 and n - 1 in BLOCK_END:
                        values(BLOCK_END.index(n - 1))
                    if n >= UNITS - 4:
                        pe.wait_ge(S["o_evac"], 2)
                        m = n - (UNITS - 4)
                        project_out(1, oT, 0, 0, range(2 * m, 2 * m + 2))
                values(3)
                project_out(1, oT, 0, 1)
                pe.wait_ge(S["o_evac"], 4)
                project_out(1, oT, 1, 0)
                transpose_x(0, 5)
                project_out(1, oT, 1, 1)

            def moe(L):
                for t in range(NT):
                    if t:
                        keep_clock(10)
                        transpose_x(t, 4 * L + t + 1)
                    pe.wait_ge(S["router_loaded"], 16 * (L + 1))
                    pe.wait_ge(S["xT_evac"], 4 * (2 * L) + 2 * t + 2)
                    for k in range(KT):
                        last = mm(bank[0][:, 64 * t:64 * t + 36], moe_xT[:, k, 128 * t:128 * t + 128], wr[:, k, :],
                                  start=(k == 0), stop=(k == KT - 1))
                last.then_inc(S["router_ps"], 1)
                keep_clock(16)
                am = rt[:, 256:320].rearrange("p (t e) -> p t e", t=NT)
                pe.wait_ge(S["assign_ready"], L + 1)
                mm(bank[1][:, 0:64], upper, am.rearrange("p t e -> p (t e)"), start=True, stop=False)
                mm(bank[1][:, 32:64], ones, am[:, 0, :], start=False, stop=True)
                mm(bank[1][:, 64:96], ones, am[:, 0, :], start=True, stop=False)
                mm(bank[1][:, 64:96], ones, am[:, 1, :], start=False, stop=True).then_inc(S["pos_ps"], 1)
                keep_clock(12)
                pe.wait_ge(S["pick_ready"], 2 * L + 1)
                for c in range(KT):
                    for t in range(NT):
                        last = mm(bank[2 + c // 4][:, 128 * (c % 4):128 * (c % 4) + 128], x_tok[:, t, 128 * c:128 * c + 128],
                                  pick[:, t, 0:128], start=(t == 0), stop=(t == NT - 1))
                    if c % 4 == 3:
                        last.then_inc(S["gather_ps"], 1)

                def gather(c):
                    for t in range(NT):
                        last = mm(bank[GATHER[c]][:, 0:384], x_tok[:, t, 128 * c:128 * c + 128], pick[:, t, 128:512],
                                  start=(t == 0), stop=(t == NT - 1))
                    last.then_inc(S["gather_ps"], 1)
                pe.wait_ge(S["pick_ready"], 2 * L + 2)
                gather(0)
                gather(1)

                def gate_up(wg, wu, s, window=xw):
                    for k in range(KT):
                        mm(bank[4][0:64, :], window[:, k, :], wg[:, k, :], start=(k == 0), stop=(k == KT - 1))
                        last = mm(bank[4][64:128, :], window[:, k, :], wu[:, k, :], start=(k == 0), stop=(k == KT - 1))
                    last.then_inc(s, 1)

                def turn(s):
                    for c in range(4):
                        last = tr(bank[5][:, 128 * c:128 * c + 128], gu[:, 128 * c:128 * c + 128], ident)
                    last.then_inc(s, 1)

                def down(wd, hin, s):
                    for k in range(4):
                        mm(bank[6][0:64, :], hin[:, k, :], wd[:, k, 0:512], start=(k == 0), stop=(k == 3))
                        last = mm(bank[6][64:128, :], hin[:, k, :], wd[:, k, 512:1024], start=(k == 0), stop=(k == 3))
                    last.then_inc(s, 1)

                def scatter(s, end=False, extra=False):
                    for t in range(NT):
                        for h in range(2):
                            last = mm(bank[2 * t + h][:, :], sel[h][:, 128 * t:128 * t + 128], yw, start=False, stop=end,
                                      skip_group_check=extra)
                            if end:
                                last.then_inc(S["resid_ps"], 1)
                    if not end:
                        last.then_inc(s, 1)

                def arrive(n0, i, k):
                    pe.wait_ge(full[slot_of(n0)], i * 16 + arrived(n0))
                    return ring[:, slot_of(n0), :].rearrange("p (k c) -> p k c", k=k)

                def expert_in(e, r, i):
                    pe.wait_ge(S["xw_ready"], e + (NE - 1) * L)
                    wg, wu = [arrive(EXP_BASE[L] + 3 * r + k, i, KT) for k in range(2)]
                    gate_up(wg, wu, S["gu_done"])

                def expert_turn(e):
                    pe.wait_ge(S["gu_evac"], e + (NE * L + 1))
                    turn(S["turn_done"])

                def expert_down(e, r, i):
                    pe.wait_ge(S["h_ready"], e + (NE * L + 1))
                    down(arrive(EXP_BASE[L] + 3 * r + 2, i, 4), hT, S["down_done"])

                def expert_out(e, end=False):
                    pe.wait_ge(S["y_evac"], e + (NE * L + 1))
                    pe.wait_ge(S["sel_ready"], e + (NE * L + 1))
                    scatter(S["sc_out"], end)

                pe.wait_ge(S["gather_act"], 5 * L + 1)
                pe.wait_ge(S["gather_dve"], 5 * L + 1)
                gate_up(arrive(EXP_BASE[L], 0, KT), arrive(EXP_BASE[L] + 1, 0, KT), S["gu_done"], xsT[:, :, 0:WIN])
                gather(2)
                gather(3)
                expert_turn(0)
                gather(4)
                pe.wait_ge(S["gather_act"], 5 * L + 2)
                gather(5)
                expert_down(0, 0, 0)
                pe.wait_ge(S["gather_dve"], 5 * L + 2)
                gather(6)
                pe.wait_ge(S["gather_act"], 5 * L + 3)
                gather(7)
                pe.wait_ge(S["gather_dve"], 5 * L + 3)
                pe.wait_ge(S["gather_act"], 5 * L + 4)
                for n in range(2):
                    for c in range(2):
                        for t in range(NT):
                            last = mm(bank[2 + n][:, 256 * c + 128 * t:256 * c + 128 * t + 128],
                                      slotw[:, n, c, t:t + 1].to_broadcast([128, 128]), ident, start=True, stop=True)
                    last.then_inc(S["rows_ps"], 1)
                def alpha_x(t):
                    for h in range(2):
                        mm(bank[2 * t + h][:, :], alpha, x_tok[:, t, 512 * h:512 * h + 512], start=True, stop=False)
                pe.wait_ge(S["gather_dve"], 5 * L + 4)
                pe.wait_ge(S["gather_act"], 5 * (L + 1))
                alpha_x(0)
                expert_in(1, 1, 0)
                expert_turn(1)
                pe.wait_ge(S["rows_evac"], 2 * (L + 1))
                alpha_x(1)
                expert_down(1, 1, 0)
                expert_in(2, 2, 0)
                expert_out(0)
                expert_turn(2)
                expert_out(1)
                with pe.Fori(0, 9) as i:
                    for r in range(3, 6):
                        expert_in(i * 3 + r, r, i)
                        expert_down(i * 3 + (r - 1), r - 1, i)
                        expert_turn(i * 3 + r)
                        expert_out(i * 3 + (r - 1))
                expert_in(30, 30, 0)
                expert_down(29, 29, 0)
                expert_turn(30)
                expert_out(29)
                expert_down(30, 30, 0)
                expert_in(31, 31, 0)
                expert_turn(31)
                expert_out(30)
                pe.wait_ge(S["h_ready"], NE * (L + 1))
                most = pe.value_load(mxi[0:1, 0:1], min_val=0, max_val=SEQ)
                with pe.If(most > WIN):
                    v = ovf[L]
                    wg, wu = [ring[:, slot_of(EXP_BASE[L] + k), :].rearrange("p (k c) -> p k c", k=KT) for k in range(2)]
                    wd = ring[:, slot_of(EXP_BASE[L] + 2), :].rearrange("p (k c) -> p k c", k=4)
                    with pe.Fori(0, NE) as e:
                        for n in ("gate_in", "up_in", "down_in"):
                            pe.wait_ge(v[n], e * 16 + 16)
                        for w in range(1, NWIN):
                            c = e * (NWIN - 1) + w
                            pe.wait_ge(v["xw"], c)
                            gate_up(wg, wu, v["gu"])
                            pe.wait_ge(v["gu_evac"], c)
                            turn(v["turn"])
                            pe.wait_ge(v["h"], c)
                            down(wd, hT2, v["down"])
                            pe.wait_ge(v["y_evac"], c)
                            pe.wait_ge(v["sel"], 2 * c)
                            scatter(v["out"], extra=True)
                expert_down(31, 31, 0)
                expert_out(31, end=True)

            pe.wait_ge(S["ident_loaded"], 16)
            mixer0()
            pe.wait_ge(S["consts_loaded"], 16)
            moe(0)
            mixer1()
            moe(1)

        @block.scalar
        def _(act):
            fn = nc.scalar.activation
            act.dma_start(par[:, :], a["params"]).then_inc(S["params_loaded"], 16)

            def evac_T(dst, s_ps, base, s_done, banks=(4, 5, 6, 7), tiles=range(NT)):
                for t in tiles:
                    for hf in range(2):
                        act.wait_ge(s_ps, base + 2 * t + hf + 1)
                        fn(dst[:, 4 * hf:4 * hf + 4, 128 * t:128 * t + 128],
                           bank[banks[2 * t + hf]][:, :].rearrange("p (c t) -> p c t", c=4), ACT.Copy).then_inc(s_done, 1)

            def layernorm(q):
                act.wait_ge(S["consts_loaded"], 16)
                for t in range(NT):
                    if t and q % 2 == 0:
                        evac_T(moe_xT, S["xT_ps"], 4 * q, S["xT_evac"], tiles=[0])
                    act.wait_ge(S["var_ready"], 2 * q + t + 1)
                    fn(sd[:, t:t + 1], mv[:, t, 1:2], ACT.Sqrt, bias=eps).then_inc(S["sd_ready"], 1)

            def mixer0():
                for b in (0, 2):
                    act.wait_ge(S["x0T_ps"], b + 1)
                    fn(xT0[:, 0:4, 64 * b:64 * b + 128], bank[b][:, :].rearrange("p (c t) -> p c t", c=4), ACT.Copy).then_inc(S["x0T_act"], 1)
                act.wait_ge(S["softplus_e"], 1)
                fn(sp_t[:, 2, :], sp_t[:, 1, :], ACT.Exp, scale=-1.0).then_inc(S["act_step"], 1)
                act.wait_ge(S["pads_zeroed"], 1)
                for b in range(2):
                    act.wait_ge(S["z0_done"], b + 1)
                    for c in (2 * b, 2 * b + 1):
                        last = fn(xl[:, c, 3:259], bank[4 + c][:, 0:256], ACT.Copy)
                    last.then_inc(S["z0_act"], 1)
                for b in range(2):
                    act.wait_ge(S["z0_done"], 2 + b + 1)
                    fn(gate[:, 2 * b:2 * b + 2, :], bank[2 + b][:, :].rearrange("p (c t) -> p c t", c=2), ACT.Gelu_apprx_tanh).then_inc(S["z0_act"], 1)
                for g in range(8):
                    act.wait_ge(S["gate_ps"], g // 2 + 1)
                    dst = (rg if g < 4 else ig)[:, g % 4, :]
                    bias = par[:, (P_BA if g < 4 else P_BX) + g % 4:(P_BA if g < 4 else P_BX) + g % 4 + 1]
                    fn(dst, bank[4 + g // 2][:, 256 * (g % 2):256 * (g % 2) + 256], ACT.Sigmoid, bias=bias).then_inc(S["gate_sig"], 1)
                act.wait_ge(S["softplus_done"], 1)
                act.wait_ge(S["gate_sig"], 8)
                for c in range(4):
                    fn(th[:, c, :], rg[:, c, :], ACT.Tanh, scale=sp_t[:, 4, c:c + 1]).then_inc(S["lru_T"], 1)
                act.wait_ge(S["lru_T"], 4)
                for c in range(4):
                    fn(rg[:, c, :], rg[:, c, :], ACT.Exp, scale=sp_t[:, 5, c:c + 1]).then_inc(S["lru_exp"], 1)
                act.wait_ge(S["lru_m2"], 1)
                fn(th[:, :, :], th[:, :, :], ACT.Sqrt, scale=2.0).then_inc(S["lru_mult"], 1)
                act.wait_ge(S["pads_zeroed"], 2)
                for b in range(2):
                    act.wait_ge(S["z0_done"], 4 + b + 1)
                    fn(cghc[:, 2 * b:2 * b + 2, 2:258], bank[b][:, :].rearrange("p (c t) -> p c t", c=2), ACT.Copy).then_inc(S["z0_act"], 1)

            def mixer1():
                evac_T(xT1, S["xT_ps"], 4, S["xT_evac"])

                def chunk(c, t):
                    act.wait_ge(S["z1_done"], 2 * c + t + 1)
                    bk = bank[2 * (c % 2) + t]
                    if c >= 3:
                        fn(qz[:, t, c - 3].rearrange("p j u d -> p u j d"),
                           bk[:, :].rearrange("p (u j d) -> p u j d", u=2, j=4), ACT.Copy).then_inc(S["z1_evac"], 1)
                        return
                    if 2 * c + t >= 2:
                        act.wait_ge(S["z1_rope"], 2 * c + t - 1)
                    fn(kraw[:, t], bk[:, 0:256], ACT.Copy).then_inc(S["act_step"], 1)
                    src = bk[:, 256:512].rearrange("p (g d) -> p g d", g=NKV)
                    if c == 0:
                        for u in range(2):
                            ins = fn(kd[:, 1, t, :, u, :], src, ACT.Copy)
                            ins.then_inc(S["z1_evac" if u else "act_step"], 1)
                    else:
                        fn(vv[:, t, c - 1], src, ACT.Copy).then_inc(S["z1_evac"], 1)

                def evac_c(n):
                    for t in range(NT):
                        act.wait_ge(S["ct_ps"], 2 * n + t + 1)
                        src = bank[5 + t][:, :].rearrange("p (g t) -> p g t", g=NKV)
                        s0 = 1 - t
                        fn(ct[n][64:128, :, 128 * t - 1 + s0:128 * t + 127], src[64:128, :, s0:128], ACT.Copy).then_inc(S["act_step"], 1)
                        fn(ct[n][0:64, :, 128 * t:128 * t + 128], src[0:64, :, :], ACT.Copy).then_inc(S["ct_evac"], 1)

                chunk(0, 0)
                chunk(0, 1)
                chunk(1, 0)
                chunk(1, 1)
                act.wait_ge(S["gl_done"], 1)
                fn(gT, bank[4][0:GL, 0:SEQ], ACT.Sigmoid).then_inc(S["gT_ready"], 1)
                evac_c(0)
                chunk(2, 0)
                act.wait_ge(S["gl_done"], 2)
                for t in range(NT):
                    for x in range(2):
                        fn(gates[:, t, 8 * x:8 * x + 8].rearrange("p (j u) b -> p u j b", u=2),
                           bank[4][:, 256 + 64 * t + 24 * x:280 + 64 * t + 24 * x].rearrange("p (u j b) -> p u j b", u=2, j=4),
                           ACT.Copy).then_inc(S["gl_evac"], 1)
                chunk(2, 1)
                evac_c(1)
                chunk(3, 0)
                chunk(3, 1)
                chunk(4, 0)
                chunk(4, 1)
                for b in range(2):
                    act.wait_ge(S["kT_ps"], b + 1)
                    for u in range(2):
                        if b == 0:
                            act.wait_ge(S["z1_done"], 10)
                            act.wait_ge(S["kpad_zeroed"], 2)
                        fn(kpad[64 * u:64 * u + 64, :, u, b, :], bank[5 + b][64 * u:64 * u + 64, :].rearrange("p (a t) -> p a t", a=2),
                           ACT.Copy).then_inc(S["kpad_ready"], 1)

                def evac_q(t, x, b):
                    act.wait_ge(S["qT_ps"], 2 * x + t + 1)
                    fn(qT[:, t, x].rearrange("p j q -> p (j q)"), bank[b][:, :], ACT.Copy).then_inc(S["qT_evac"], 1)
                act.wait_ge(S["cmp1_done"], 1)
                act.wait_ge(S["gl_evac"], 4)
                fn(hc, bank[7][:, 0:256], ACT.Gelu_apprx_tanh).then_inc(S["cmp1_gelu"], 1)
                evac_q(0, 0, 2)
                evac_q(1, 0, 3)
                fn(exp_warm[:, :], eps, ACT.Exp).then_inc(S["act_step"], 1)

                def exps(n):
                    k = 4 if n < 8 else 2
                    W = 512 // k
                    act.wait_ge(S["nm_ready"], n + 1)
                    if n >= 3:
                        act.wait_ge(S["pt_ps"], n - 2)
                    for i in range(k):
                        last = fn(P[:, n % 3, W * i:W * i + W], bank[n % 3][:, W * i:W * i + W], ACT.Exp, scale=SCALE,
                                  bias=asm[:, n % 3, 4 + i:5 + i], accum_out=asm[:, n % 3, 8 + i:9 + i])
                    last.then_inc(S["p_exp"], 1)

                def evac(n):
                    t, x, j, us = unit_of(n)
                    at = 512 * j if t == 0 else 512 * (2 * j + us[0])
                    act.wait_ge(S["pt_ps"], n + 1)
                    if t == 1:
                        act.wait_ge(S["pv_done"], x + 1)
                    fn(PT[x][:, at:at + 512], bank[3 + n % 2][:, :], ACT.Copy).then_inc(S["pt_evac"], 1)

                exps(0)
                act.wait_ge(S["cmp2_done"], 1)
                act.wait_ge(S["kc_zeroed"], 1)
                for u in range(2):
                    fn(kcbd[64 * u:64 * u + 64, :, u, :], bank[5][64 * u:64 * u + 64, 0:64].rearrange("p (a u c) -> p a u c", a=2, u=2)[:, :, u, :],
                       ACT.Copy).then_inc(S["kc_evac"], 1)
                evac_q(0, 1, 4)
                evac_q(1, 1, 3)
                exps(1)
                exps(2)
                for n in range(UNITS):
                    evac(n)
                    if n + 3 < UNITS:
                        exps(n + 3)
                    if n == 1:
                        act.wait_ge(S["pc_sub"], 1)
                        fn(pc, pc, ACT.Exp).then_inc(S["pc_exp"], 1)
                    if n == 5:
                        act.wait_ge(S["pcT_ps"], 1)
                        fn(pcT.rearrange("p t a q -> p (t a q)"), bank[7][:, :], ACT.Copy).then_inc(S["pcT_evac"], 1)

            def moe(L):
                evac_T(moe_xT, S["xT_ps"], 8 * L, S["xT_evac"], tiles=[1])
                for t in range(NT):
                    act.wait_ge(S["gneg_ready"], L + 1)
                    fn(rt[:, 640 + 4 * t:644 + 4 * t], rt[:, 0:72].rearrange("p (t c) -> p t c", t=NT)[:, t, 0:4], ACT.Exp,
                       bias=rt[:, 120 + t:121 + t], accum_out=rt[:, 122 + t:123 + t]).then_inc(S["gexp_done"], 1)
                for t in range(NT):
                    act.wait_ge(S["eneg_ready"], L + 1)
                    fn(rt[:, 144 + 8 * t:152 + 8 * t], rt[:, 128 + 8 * t:136 + 8 * t], ACT.Exp,
                       bias=rt[:, 160 + t:161 + t], accum_out=rt[:, 162 + t:163 + t]).then_inc(S["eexp_done"], 1)
                for t in range(NT):
                    fn(rt[:, 208 + 2 * t:210 + 2 * t], rt[:, 168 + 8 * t:170 + 8 * t], ACT.Exp,
                       bias=rt[:, 160 + t:161 + t]).then_inc(S["eexp_done"], 1)
                act.wait_ge(S["gather_ps"], 10 * L + 1)
                fn(xsT[:, 0:4, 0:128], bank[2][:, :].rearrange("p (c s) -> p c s", c=4), ACT.Copy).then_inc(S["gather_act"], 1)

                def gathered(c):
                    act.wait_ge(S["gather_ps"], 10 * L + 3 + c)
                    fn(xsT[:, c, 128:NSLOT], bank[GATHER[c]][:, 0:384], ACT.Copy).then_inc(S["gather_act"], 1)
                gathered(0)
                act.wait_ge(S["gu_done"], NE * L + 1)
                fn(gu, bank[4][:, :], ACT.Copy).then_inc(S["gu_evac"], 1)
                gathered(2)

                def silu(hout, s):
                    fn(hout, bank[5][:, :].rearrange("p (k u s) -> p k u s", k=4, u=2)[:, :, 0, :], ACT.Silu).then_inc(s, 1)

                def gate_up_out(e):
                    act.wait_ge(S["gu_done"], e + (NE * L + 1))
                    fn(gu, bank[4][:, :], ACT.Copy).then_inc(S["gu_evac"], 1)

                def down_out(e):
                    act.wait_ge(S["down_done"], e + (NE * L + 1))
                    fn(yw, bank[6][:, :], ACT.Copy).then_inc(S["y_evac"], 1)

                def gated(e):
                    act.wait_ge(S["turn_done"], e + (NE * L + 1))
                    silu(hT, S["silu_done"])

                gated(0)
                gathered(4)
                gathered(6)
                for n in range(2):
                    act.wait_ge(S["rows_ps"], 2 * L + n + 1)
                    fn(rows[:, n].rearrange("p c t -> p (c t)"), bank[2 + n][:, :], ACT.Copy).then_inc(S["rows_evac"], 1)
                down_out(0)
                gate_up_out(1)
                gated(1)
                gate_up_out(2)
                act.wait_ge(S["sc_out"], (NE - 1) * L + 1)
                down_out(1)
                gated(2)
                with act.Fori(3, NE - 1) as e:
                    gate_up_out(e)
                    down_out(e - 1)
                    gated(e)
                down_out(NE - 2)
                gate_up_out(NE - 1)
                gated(NE - 1)
                most = act.value_load(mxi[0:1, 0:1], min_val=0, max_val=SEQ)
                with act.If(most > WIN):
                    v = ovf[L]
                    with act.Fori(0, NE) as e:
                        for w in range(1, NWIN):
                            c = e * (NWIN - 1) + w
                            act.wait_ge(v["gu"], c)
                            fn(gu, bank[4][:, :], ACT.Copy).then_inc(v["gu_evac"], 1)
                            act.wait_ge(v["turn"], c)
                            silu(hT2, v["silu"])
                            act.wait_ge(v["down"], c)
                            fn(yw, bank[6][:, :], ACT.Copy).then_inc(v["y_evac"], 1)
                down_out(NE - 1)

            mixer0()
            layernorm(0)
            moe(0)
            layernorm(1)
            mixer1()
            layernorm(2)
            moe(1)
            layernorm(3)

        @block.vector
        def _(dve):
            v = nc.vector
            st = Steps(dve, S["dve_step"])
            step, settle = st.step, st.settle

            def layernorm(q):
                L, which = q // 2, q % 2
                g, b = gb_view(L, which)
                if q == 0:
                    dve.wait_ge(S["x_loaded"], 16)
                for t in range(NT):
                    xt = x_tok[:, t, :]
                    for h in range(2):
                        dve.wait_ge(S["resid_ps"], 4 * q + 2 * t + h + 1)
                        xs = x_tok[:, t, 512 * h:512 * h + 512]
                        if which == 0:
                            step(v.scalar_tensor_tensor(xs, xs, ALPHA, resid(q, t, h), ALU.mult, ALU.add))
                            settle()
                        else:
                            xs = bank[2 * t + h][:, :]
                        step(v.bn_stats(stats[:, t, h, :], xs))
                    settle()
                    v.bn_aggr(mv[:, t, :], stats[:, t, :, :].rearrange("p h s -> p (h s)")).then_inc(S["var_ready"], 1)
                    dve.wait_ge(S["var_ready"], 2 * q + t + 1)
                    dve.wait_ge(S[("gb1_loaded", "gb2_loaded")[which]], 32 * (L + 1))
                    for h in range(2):
                        xs = x_tok[:, t, 512 * h:512 * h + 512]
                        step(v.scalar_tensor_tensor(xs, bank[2 * t + h][:, :] if which else xs, mv[:, t, 0:1], g[:, 512 * h:512 * h + 512],
                                                    ALU.subtract, ALU.mult))
                    dve.wait_ge(S["sd_ready"], 2 * q + t + 1)
                    step(v.reciprocal(rstd[:, t:t + 1], sd[:, t:t + 1]))
                    settle()
                    for h in range(2):
                        cs = slice(512 * h, 512 * h + 512)
                        v.scalar_tensor_tensor(xt[:, cs], xt[:, cs], rstd[:, t:t + 1], b[:, cs],
                                               ALU.mult, ALU.add).then_inc(S[("x_half", "x_ready")[h]], 1)

            def mixer0():
                for b in (1, 3):
                    dve.wait_ge(S["x0T_ps"], b + 1)
                    v.tensor_copy(xT0[:, 4:8, 64 * b - 64:64 * b + 64], bank[b][:, :].rearrange("p (c t) -> p c t", c=4)).then_inc(S["x0T_dve"], 1)
                dve.wait_ge(S["params_loaded"], 16)
                lam = par[:, P_LAM:P_LAM + 4]
                step(v.tensor_scalar(sp_t[:, 0, :], lam, -1.0, 0.0, ALU.mult, ALU.max))
                step(v.tensor_scalar(sp_t[:, 3, :], lam, -1.0, None, ALU.mult))
                settle()
                v.tensor_tensor(sp_t[:, 1, :], lam, sp_t[:, 3, :], ALU.max).then_inc(S["softplus_e"], 1)
                dve.wait_ge(S["act_step"], 1)
                y, s_, s2, p = sp_t[:, 2, :], sp_t[:, 1, :], sp_t[:, 3, :], sp_t[:, 4, :]
                step(v.tensor_scalar(p, y, 2.0, None, ALU.add))
                settle()
                step(v.reciprocal(s2, p))
                settle()
                step(v.tensor_tensor(s_, y, s2, ALU.mult))
                settle()
                step(v.tensor_tensor(s2, s_, s_, ALU.mult))
                settle()
                step(v.tensor_scalar(p, s2, 1.0 / 17, 1.0 / 15, ALU.mult, ALU.add))
                for c in (13, 11, 9, 7, 5, 3, 1):
                    settle()
                    step(v.tensor_tensor(p, p, s2, ALU.mult))
                    settle()
                    step(v.tensor_scalar(p, p, 1.0 / c, None, ALU.add))
                settle()
                step(v.tensor_tensor(p, p, s_, ALU.mult))
                settle()
                step(v.scalar_tensor_tensor(s2, p, 2.0, sp_t[:, 0, :], ALU.mult, ALU.add))
                settle()
                step(v.tensor_scalar(sp_t[:, 4, :], s2, 8.0, None, ALU.mult))
                v.tensor_scalar(sp_t[:, 5, :], s2, -8.0, None, ALU.mult).then_inc(S["softplus_done"], 1)
                settle()
                for c in range(4):
                    dve.wait_ge(S["z0_act"], c // 2 + 1)
                    step(v.tensor_scalar(xc[:, c, :], xl[:, c, 0:256], par[:, P_LCONV + 4 * c:P_LCONV + 4 * c + 1],
                                         par[:, P_LCB + c:P_LCB + c + 1], ALU.mult, ALU.add))
                for k in range(1, 4):
                    settle()
                    for c in range(4):
                        ins = v.scalar_tensor_tensor(xc[:, c, :], xl[:, c, k:k + 256],
                                                     par[:, P_LCONV + 4 * c + k:P_LCONV + 4 * c + k + 1], xc[:, c, :], ALU.mult, ALU.add)
                        if k < 3:
                            step(ins)
                        else:
                            ins.then_inc(S["xc_ready"], 1)
                dve.wait_ge(S["xc_ready"], 4)
                dve.wait_ge(S["lru_T"], 4)
                m2 = yT[:, 4:8, :]
                step(v.tensor_scalar(m2, th, 1.0, None, ALU.add))
                dve.wait_ge(S["gate_sig"], 8)
                step(v.tensor_tensor(ig, ig, xc, ALU.mult))
                settle()
                step(v.reciprocal(m2, m2))
                settle()
                v.tensor_tensor(th, th, m2, ALU.mult).then_inc(S["lru_m2"], 1)
                dve.wait_ge(S["lru_mult"], 1)
                step(v.tensor_tensor(ig, ig, th, ALU.mult))
                settle()
                for c in range(4):
                    dve.wait_ge(S["lru_exp"], c + 1)
                    step(v.tensor_tensor_scan(yT[:, 4 + c, :], rg[:, c, :], ig[:, c, :], 0.0, ALU.mult, ALU.add))
                settle()
                dve.wait_ge(S["z0_act"], 4)
                for c in range(4):
                    v.tensor_tensor(yT[:, 4 + c, :], yT[:, 4 + c, :], gate[:, c, :], ALU.mult).then_inc(S["ylru_ready"], 1)
                for b in range(2):
                    dve.wait_ge(S["z0_act"], 4 + b + 1)
                    dve.wait_ge(S["z0_done"], 6 + b + 1)
                    cv = cghc[:, 2 * b:2 * b + 2, 2:258]
                    v.tensor_tensor(cv, bank[2 + b][:, :].rearrange("p (c t) -> p c t", c=2), cv, ALU.mult).then_inc(S["z0_dve"], 1)
                for c in range(4):
                    dve.wait_ge(S["z0_dve"], c // 2 + 1)
                    step(v.tensor_scalar(yT[:, c, :], cghc[:, c, 0:256], par[:, P_CONV + 3 * c:P_CONV + 3 * c + 1], None, ALU.mult))
                for k in range(1, 3):
                    settle()
                    for c in range(4):
                        step(v.scalar_tensor_tensor(yT[:, c, :], cghc[:, c, k:k + 256],
                                                    par[:, P_CONV + 3 * c + k:P_CONV + 3 * c + k + 1], yT[:, c, :], ALU.mult, ALU.add))
                settle()
                for b in range(2):
                    dve.wait_ge(S["z0_done"], 8 + b + 1)
                    yv = yT[:, 2 * b:2 * b + 2, :]
                    v.tensor_tensor(yv, bank[b][:, :].rearrange("p (c t) -> p c t", c=2), yv, ALU.mult).then_inc(S["z0_dve"], 1)

            def rotate(src, dst, t, H, s_done):
                cs = rope[:, t, 0, :].unsqueeze(1).to_broadcast([128, H, 32])
                sn = rope[:, t, 1, :].unsqueeze(1).to_broadcast([128, H, 32])
                tm = rtmp[:, 0:64 * H].rearrange("p (h d) -> p h d", h=H)
                step(v.tensor_tensor(tm[:, :, 0:32], src[:, :, 32:64], sn, ALU.mult))
                step(v.tensor_tensor(tm[:, :, 32:64], src[:, :, 0:32], sn, ALU.mult))
                settle()
                step(v.tensor_tensor(dst[:, :, 0:32], src[:, :, 0:32], cs, ALU.mult))
                step(v.tensor_tensor(dst[:, :, 32:64], src[:, :, 32:64], cs, ALU.mult))
                settle()
                step(v.tensor_tensor(dst[:, :, 0:32], dst[:, :, 0:32], tm[:, :, 0:32], ALU.subtract))
                v.tensor_tensor(dst[:, :, 32:64], dst[:, :, 32:64], tm[:, :, 32:64], ALU.add).then_inc(s_done, 1)
                settle()

            def mixer1():
                dve.wait_ge(S["l1small_loaded"], 96)
                turned = [0]

                def rotate_k(c, t):
                    dve.wait_ge(S["z1_evac"], 2 * c + t + 1)
                    src = kraw[:, t].rearrange("p (g d) -> p g d", d=64)
                    dst = kd[:, 0, t, :, 0, :] if c == 0 else krot[:, c - 1, t].rearrange("p a (u d) -> p (a u) d", u=2)
                    rotate(src, dst, t, NKV, S["z1_rope"])
                    turned[0] += 1
                    dve.wait_ge(S["z1_rope"], turned[0])
                    if c == 0:
                        v.tensor_copy(kd[:, 0, t, :, 1, :], kd[:, 0, t, :, 0, :]).then_inc(S["kdup_done"], 1)

                def rotate_q(x, t):
                    dve.wait_ge(S["z1_evac"], 2 * (3 + x) + t + 1)
                    q = qz[:, t, x].rearrange("p j u d -> p (j u) d")
                    rotate(q, q, t, 8, S["z1_rope"])
                    turned[0] += 1
                    dve.wait_ge(S["z1_rope"], turned[0])

                def blocks(n):
                    dve.wait_ge(S["ct_evac"], 2 * n + 2)
                    if n == 0:
                        dve.wait_ge(S["blk_zeroed"], 2)
                    for g in range(NKV):
                        lo = ct[n][:, g, 0:240].rearrange("p (b k u) -> p k b u", b=NBLK, u=2)[:, :, :, 0]
                        hi = ct[n][:, g, 16:256].rearrange("p (b k u) -> p k b u", b=NBLK, u=2)[:, :, :, 0]
                        for half, src in ((0, lo), (1, hi)):
                            ins = v.tensor_tensor(blk[n][:, 8 * half:8 * half + 8, g, 0:NBLK], src,
                                                  pe_[:, n, 8 * half:8 * half + 8].unsqueeze(2).to_broadcast([128, 8, NBLK]), ALU.add)
                            if g == NKV - 1 and half:
                                settle()
                                ins.then_inc(S["blk_ready"], 1)
                            else:
                                step(ins)

                for c in range(3):
                    rotate_k(c, 0)
                    rotate_k(c, 1)
                blocks(0)
                blocks(1)
                rotate_q(0, 0)
                rotate_q(0, 1)
                rotate_q(1, 0)
                rotate_q(1, 1)
                dve.wait_ge(S["hc_ps"], 1)
                turned_h = bank[7][:, 256:512].rearrange("p (m c) -> p m c", m=2)
                v.tensor_copy(hk, turned_h[:, :, 0:64]).then_inc(S["hc_evac"], 1)
                for m in range(2):
                    v.tensor_copy(hx[:, m].rearrange("p a (j r) -> p a j r", j=4),
                                  turned_h[:, m, 64:128].rearrange("p (a r) -> p a r", a=2).unsqueeze(2).to_broadcast([128, 2, 4, 32])).then_inc(S["hc_evac"], 1)

                def maxes(n):
                    t = 0 if n < 8 else 1
                    k = 4 if n < 8 else 2
                    sc = bank[n % 3][:, :].rearrange("p (k s) -> p k s", k=k)
                    dve.wait_ge(S["sc_done"], n + 1)
                    diag = sc[:, :, 128 * t:128 * t + 128]
                    step(v.tensor_tensor(diag, diag, causal.unsqueeze(1).to_broadcast([128, k, 128]), ALU.add))
                    settle()
                    step(v.tensor_reduce(asm[:, n % 3, 0:k], sc, axis=AX.X, op=ALU.max))
                    settle()
                    v.tensor_scalar(asm[:, n % 3, 4:4 + k], asm[:, n % 3, 0:k], -SCALE, None, ALU.mult).then_inc(S["nm_ready"], 1)

                def scales(n):
                    t, x, j, us = unit_of(n)
                    h, k = 8 * x + 2 * j + us[0], 2 * len(us)
                    dve.wait_ge(S["p_exp"], n + 1)
                    step(v.reciprocal(arec[:, n % 3, 0:k], asm[:, n % 3, 8:8 + k]))
                    settle()
                    r = arec[:, n % 3, 0:k].rearrange("p (u b) -> p u b", b=2)
                    v.tensor_tensor(r, r, gates[:, t, h:h + len(us), 1:3], ALU.mult).then_inc(S["rs_ready"], 1)

                for n in range(3):
                    maxes(n)
                def blocks_max():
                    dve.wait_ge(S["sc_cmp"], 2)
                    for t in range(NT):
                        step(v.scalar_tensor_tensor(pc[:, t], bank[7][:, 256 * t:256 * t + 256].rearrange("p (h c) -> p h c", h=NH), SCALE,
                                                    cmp_add[:, t].unsqueeze(1).to_broadcast([128, NH, NB]), ALU.mult, ALU.add))
                    settle()
                    step(v.tensor_reduce(cmx, pc, axis=AX.X, op=ALU.max))
                    settle()
                    v.tensor_tensor(pc, pc, cmx.unsqueeze(3).to_broadcast([128, NT, NH, NB]), ALU.subtract).then_inc(S["pc_sub"], 1)

                def own_rows():
                    dve.wait_ge(S["cmp2_done"], 1)
                    dve.wait_ge(S["kc_evac"], 2)
                    for x in range(2):
                        v.tensor_tensor(vbd[:, x], bank[5][:, 64 + 64 * x:128 + 64 * x].unsqueeze(1).to_broadcast([128, 8, 64]),
                                        own.unsqueeze(2).to_broadcast([128, 8, 64]), ALU.mult).then_inc(S["vbd_ready"], 1)

                def blocks_sum():
                    dve.wait_ge(S["pc_exp"], 1)
                    step(v.tensor_tensor(pc, pc, cmp_mul.unsqueeze(2).to_broadcast([128, NT, NH, NB]), ALU.mult))
                    settle()
                    step(v.tensor_reduce(cmx, pc, axis=AX.X, op=ALU.add))
                    settle()
                    step(v.tensor_scalar(cmx, cmx, TINY, None, ALU.max))
                    settle()
                    step(v.reciprocal(cmx, cmx))
                    settle()
                    dve.wait_ge(S["gl_evac"], 4)
                    step(v.tensor_tensor(cmx, cmx, gates[:, :, :, 0], ALU.mult))
                    settle()
                    v.tensor_tensor(pc, pc, cmx.unsqueeze(3).to_broadcast([128, NT, NH, NB]), ALU.mult).then_inc(S["pc_ready"], 1)

                def evac_o(B):
                    dve.wait_ge(S["pv_done"], B + 1)
                    v.tensor_copy(oT[B // 2][:, 4 * (B % 2):4 * (B % 2) + 4, :].rearrange("p k q -> p (k q)"), bank[5 + B % 2][:, :]).then_inc(S["o_evac"], 1)

                scales(0)
                for n in range(UNITS):
                    if n + 1 < UNITS:
                        scales(n + 1)
                    if n + 3 < UNITS:
                        maxes(n + 3)
                    if n == 0:
                        own_rows()
                    if n == 1:
                        blocks_max()
                    if n == 3:
                        blocks_sum()
                    if n == 8:
                        evac_o(0)
                    if n > 8 and n - 3 in BLOCK_END:
                        evac_o(BLOCK_END.index(n - 3))
                evac_o(3)

            def moe(L):
                lg = rt[:, 0:72].rearrange("p (t c) -> p t c", t=NT)
                g8 = rt[:, 72:88].rearrange("p (t c) -> p t c", t=NT)
                gm = rt[:, 88:104].rearrange("p (t c) -> p t c", t=NT)
                gi = rt[:, 104:120].rearrange("p (t c) -> p t c", t=NT)
                oh = rt[:, 112:120].rearrange("p (t c) -> p t c", t=NT)
                le = rt[:, 128:144].rearrange("p (t c) -> p t c", t=NT)
                top = rt[:, 208:212].rearrange("p (t c) -> p t c", t=NT)
                ev = rt[:, 168:184].rearrange("p (t c) -> p t c", t=NT)
                ei = rt[:, 184:200].rearrange("p (t c) -> p t c", t=NT)
                gidx, eidx, wsum = rt[:, 200:202], rt[:, 202:206].rearrange("p (t c) -> p t c", t=NT), rt[:, 206:208]
                am = rt[:, 256:320].rearrange("p (t e) -> p t e", t=NT)
                onehot = rt[:, 320:448].rearrange("p (c t e) -> p c t e", c=2, t=NT)
                prod = rt[:, 448:576].rearrange("p (c t e) -> p c t e", c=2, t=NT)
                incl, offs, scol = rt[:, 576:608], rt[:, 608:640], rt[:, 640:704].rearrange("p (t e) -> p t e", t=NT)
                offw = rt[:, 0:128].rearrange("p (w e) -> p w e", w=NWIN)
                gif = rt[:, 704:720].bitcast(u32).rearrange("p (t c) -> p t c", t=NT)
                eif = rt[:, 720:736].bitcast(u32).rearrange("p (t c) -> p t c", t=NT)
                slot, wt = slotw[:, 0], slotw[:, 1]
                dve.wait_ge(S["x_ready"], 4 * L + 2)
                step(v.memset(g8, -3.0e38))
                dve.wait_ge(S["router_ps"], L + 1)
                dve.wait_ge(S["rbias_loaded"], 16 * (L + 1))
                lps = bank[0][:, 0:128].rearrange("p (t c) -> p t c", t=NT)
                settle()
                step(v.tensor_tensor(g8[:, :, 0:4], lps[:, :, 0:4], rbias[:, 0:4].unsqueeze(1).to_broadcast([128, NT, 4]), ALU.add))
                step(v.tensor_tensor(lg, lps[:, :, 0:36], rbias[:, :].unsqueeze(1).to_broadcast([128, NT, 36]), ALU.add))
                settle()
                for t in range(NT):
                    step(v.max(gm[:, t, :], g8[:, t, :]))
                settle()
                for t in range(NT):
                    step(v.max_index(gif[:, t, :], gm[:, t, :], g8[:, t, :]))
                v.tensor_scalar(rt[:, 120:122], gm[:, :, 0], -1.0, None, ALU.mult).then_inc(S["gneg_ready"], 1)
                settle()
                step(v.tensor_copy(gidx, gif[:, :, 0]))
                settle()
                step(v.tensor_tensor(oh, iota[:, 0:4].unsqueeze(1).to_broadcast([128, NT, 4]), gidx.unsqueeze(2).to_broadcast([128, NT, 4]), ALU.is_equal))
                settle()
                own_lg = rt[:, 448:512].rearrange("p (t g j) -> p t g j", t=NT, g=NG)
                step(v.tensor_tensor(own_lg, lg[:, :, 4:36].rearrange("p t (g j) -> p t g j", g=NG), oh.unsqueeze(3).to_broadcast([128, NT, NG, 8]), ALU.mult))
                settle()
                step(v.tensor_reduce(le, own_lg.rearrange("p t g j -> p t j g"), axis=AX.X, op=ALU.add))
                settle()
                for t in range(NT):
                    step(v.max(ev[:, t, :], le[:, t, :]))
                settle()
                for t in range(NT):
                    step(v.max_index(eif[:, t, :], ev[:, t, :], le[:, t, :]))
                v.tensor_scalar(rt[:, 160:162], ev[:, :, 0], -1.0, None, ALU.mult).then_inc(S["eneg_ready"], 1)
                settle()
                step(v.tensor_copy(eidx, eif[:, :, 0:2]))
                settle()
                step(v.scalar_tensor_tensor(eidx, gidx.unsqueeze(2).to_broadcast([128, NT, 2]), 8.0, eidx, ALU.mult, ALU.add))
                settle()
                for c in range(2):
                    step(v.tensor_tensor(onehot[:, c], iota[:, 0:NE].unsqueeze(1).to_broadcast([128, NT, NE]),
                                         eidx[:, :, c:c + 1].to_broadcast([128, NT, NE]), ALU.is_equal))
                settle()
                v.tensor_tensor(am, onehot[:, 0], onehot[:, 1], ALU.add).then_inc(S["assign_ready"], 1)
                dve.wait_ge(S["gexp_done"], 2 * (L + 1))
                step(v.reciprocal(rt[:, 124:126], rt[:, 122:124]))
                dve.wait_ge(S["eexp_done"], 4 * (L + 1))
                step(v.reciprocal(rt[:, 166:168], rt[:, 162:164]))
                settle()
                step(v.tensor_tensor(top, top, rt[:, 166:168].unsqueeze(2).to_broadcast([128, NT, 2]), ALU.mult))
                settle()
                step(v.tensor_tensor(wsum, top[:, :, 0], top[:, :, 1], ALU.add))
                settle()
                step(v.reciprocal(wsum, wsum))
                settle()
                step(v.tensor_tensor(wsum, wsum, rt[:, 124:126], ALU.mult))
                settle()
                for c in range(2):
                    step(v.tensor_tensor(wt[:, c, :], top[:, :, c], wsum, ALU.mult))
                dve.wait_ge(S["pos_ps"], L + 1)
                cnt = rt[:, 128:160]
                step(v.tensor_tensor_scan(incl, ones[:, 0:NE], bank[1][:, 64:96], 0.0, ALU.mult, ALU.add))
                step(v.tensor_copy(cnt, bank[1][:, 64:96]))
                settle()
                step(v.tensor_tensor(offs, incl, cnt, ALU.subtract))
                settle()
                step(v.tensor_tensor(scol, bank[1][:, 0:64].rearrange("p (t e) -> p t e", t=NT),
                                     offs.unsqueeze(1).to_broadcast([128, NT, NE]), ALU.add))
                settle()
                step(v.tensor_tensor(prod, onehot, scol.unsqueeze(1).to_broadcast([128, 2, NT, NE]), ALU.mult))
                settle()
                v.tensor_reduce(slot, prod, axis=AX.X, op=ALU.add).then_inc(S["slot_ready"], 1)
                dve.wait_ge(S["slot_ready"], L + 1)
                for lo, hi in ((0, 128), (128, NSLOT)):
                    for t in range(NT):
                        step(v.tensor_scalar(pick[:, t, lo:hi], iota[:, lo:hi], slot[:, 0, t:t + 1], None, ALU.is_equal))
                    settle()
                    for t in range(NT):
                        ins = v.scalar_tensor_tensor(pick[:, t, lo:hi], iota[:, lo:hi], slot[:, 1, t:t + 1], pick[:, t, lo:hi],
                                                     ALU.is_equal, ALU.add)
                        if t == NT - 1:
                            ins.then_inc(S["pick_ready"], 1)
                        else:
                            step(ins)
                dve.wait_ge(S["gather_ps"], 10 * L + 2)
                v.tensor_copy(xsT[:, 4:8, 0:128], bank[3][:, :].rearrange("p (c s) -> p c s", c=4)).then_inc(S["gather_dve"], 1)
                for w in range(NWIN):
                    step(v.tensor_scalar(offw[:, w, :], offs, float(WIN * w), float(NSLOT), ALU.add, ALU.min))
                step(v.tensor_reduce(rt[:, 736:737], cnt, axis=AX.X, op=ALU.max))
                settle()
                step(v.tensor_copy(offi[0:1, :], offw[0:1].rearrange("p w e -> p (w e)")))
                settle()
                v.tensor_copy(mxi[0:1, 0:1], rt[0:1, 736:737]).then_inc(S["offs_ready"], 1)
                def times_up(h, s):
                    v.tensor_tensor(h, h, bank[5][:, :].rearrange("p (k u s) -> p k u s", k=4, u=2)[:, :, 1, :], ALU.mult).then_inc(s, 1)

                for c in range(1, KT, 2):
                    if c == 5:
                        dve.wait_ge(S["silu_done"], NE * L + 1)
                        times_up(hT, S["h_ready"])
                    dve.wait_ge(S["gather_ps"], 10 * L + 3 + c)
                    v.tensor_copy(xsT[:, c, 128:NSLOT], bank[GATHER[c]][:, 0:384]).then_inc(S["gather_dve"], 1)
                used = rt[:, 320:448].rearrange("p (w e) -> p w e", w=NWIN)
                for w in range(NWIN):
                    step(v.tensor_scalar(colid[:, w, :], offs, row, float(WIN * w + 1), ALU.add, ALU.add))
                    step(v.tensor_scalar(used[:, w, :], cnt, row, float(WIN * w), ALU.subtract, ALU.is_gt))
                settle()
                step(v.tensor_tensor(colid, colid, used, ALU.mult))
                settle()
                step(v.tensor_scalar(colid, colid, -1.0, None, ALU.add))
                settle()
                dve.wait_ge(S["rows_evac"], 2 * (L + 1))
                dve.wait_ge(S["sel_zeroed"], 2 * (L + 1))

                def select(w, e, s_eq, eq_done, s):
                    for c in range(2):
                        v.scalar_tensor_tensor(eq[c], rows[:, 0, c], colid[:, w, bass.ds(e, 1)], rows[:, 1, c],
                                               ALU.is_equal, ALU.mult).then_inc(s_eq, 1)
                    dve.wait_ge(s_eq, eq_done)
                    for h in range(2):
                        p = slice(64 * h, 64 * h + 64)
                        v.tensor_tensor(sel[h][p, :], eq[0][p, :], eq[1][p, :], ALU.add).then_inc(s[h], 1)

                def expert(e, last=False):
                    dve.wait_ge(S["silu_done"], e + (NE * L + 1))
                    times_up(hT, S["h_ready"])
                    if not last:
                        dve.wait_ge(S["sc_out"], e + (NE - 1) * L)
                        select(0, e, S["eq_done"], e * 2 + (2 * NE * L + 2), (S["sel_half"], S["sel_ready"]))

                select(0, 0, S["eq_done"], 2 * NE * L + 2, (S["sel_half"], S["sel_ready"]))
                with dve.Fori(1, NE - 1) as e:
                    expert(e)
                expert(NE - 1, last=True)
                most = dve.value_load(mxi[0:1, 0:1], min_val=0, max_val=SEQ)
                with dve.If(most > WIN):
                    vo = ovf[L]
                    dve.wait_ge(S["sc_out"], (NE - 1) * (L + 1))
                    with dve.Fori(0, NE) as e:
                        for w in range(1, NWIN):
                            c = e * (NWIN - 1) + w
                            select(w, e, vo["eq"], c * 2, (vo["sel"], vo["sel"]))
                            dve.wait_ge(vo["silu"], c)
                            times_up(hT2, vo["h"])
                            dve.wait_ge(vo["out"], c)
                dve.wait_ge(S["sc_out"], (NE - 1) * (L + 1))
                select(0, NE - 1, S["eq_done"], 2 * NE * (L + 1), (S["sel_half"], S["sel_ready"]))

            mixer0()
            dve.wait_ge(S["consts_loaded"], 16)
            layernorm(0)
            moe(0)
            layernorm(1)
            mixer1()
            layernorm(2)
            moe(1)
            layernorm(3)


def constants():
    import numpy as np
    c = np.zeros((128, N_CONST), np.float32)
    i = np.arange(128)
    c[:, C_ID:C_ID + 128] = np.eye(128)
    c[:, C_ALPHA:C_ALPHA + 128] = ALPHA * np.eye(128)
    c[:, C_UP:C_UP + 128] = i[:, None] < i[None, :]
    c[:, C_ONE:C_ONE + 128] = 1.0
    c[:, C_CAUS:C_CAUS + 128] = np.where(i[None, :] <= i[:, None], 0.0, -1e30)
    c[:, C_IOTA:C_IOTA + 512] = np.arange(512)
    c[:, C_EPS] = LN_EPS
    c[:, C_ROW] = i % WIN
    return c


def attention_constants():
    import numpy as np
    c = np.zeros((128, N_ATT), np.float32)
    i = np.arange(128)
    inv = np.float32(10000.0) ** (-np.arange(0, DK, 2, dtype=np.float32) / DK)
    for t in range(NT):
        ang = ((i + 128 * t).astype(np.float32)[:, None] * inv[None, :].astype(np.float32)).astype(np.float32)
        c[:, A_ROPE + 64 * t:A_ROPE + 64 * t + 32] = np.cos(ang)
        c[:, A_ROPE + 64 * t + 32:A_ROPE + 64 * t + 64] = np.sin(ang)
        seen = ((16 * np.arange(NB) + 31)[None, :] <= (i + 128 * t)[:, None]) & (np.arange(NB) < NBLK)
        c[:, A_CMPA + NB * t:A_CMPA + NB * (t + 1)] = np.where(seen, 0.0, -1e30)
        c[:, A_CMPM + NB * t:A_CMPM + NB * (t + 1)] = seen
    c[:, A_OWN:A_OWN + 8] = i[:, None] // NB == np.arange(8)
    return c


def kernel(**inputs):
    import numpy as np
    import concourse.bacc as bacc
    from concourse.bass_utils import run_bass_kernel_spmd as run

    x = {k: np.ascontiguousarray(np.asarray(v)) for k, v in inputs.items()}

    def channels(v):
        v = v.reshape(-1, 4, 128)
        return np.transpose(v, (2, 1, 0)).reshape(128, -1)

    arrays = {"x": x["x"], "consts": constants(),
              "att_consts": attention_constants()}
    arrays["params"] = np.concatenate([channels(x[k]) for k in (
        "l0_conv_w", "l0_lru_conv_w", "l0_lru_conv_b", "l0_lru_b_a", "l0_lru_b_x", "l0_lru_lambda")], axis=1)
    wbd = np.zeros((128, 8, 128), np.float32)
    for n, k in enumerate(("l0_lru_w_a", "l0_lru_w_x")):
        for c in range(4):
            for u in range(2):
                wbd[64 * u:64 * u + 64, 4 * n + c, 64 * u:64 * u + 64] = x[k][2 * c + u]
    arrays["wbd"] = wbd
    arrays["pe"] = np.stack([np.transpose(x[k].reshape(16, 2, 64), (1, 2, 0)).reshape(128, 16)
                             for k in ("l1_cmp_k_pe", "l1_cmp_v_pe")], axis=1)
    for L in range(2):
        arrays[f"wr{L}"] = np.concatenate([x[f"l{L}_router_group_w"], x[f"l{L}_router_expert_w"]], axis=1)
        arrays[f"br{L}"] = np.concatenate([x[f"l{L}_router_group_b"], x[f"l{L}_router_expert_b"]])
    for k in ("l0_w_in l0_w_out l0_ln1_g l0_ln1_b l0_ln2_g l0_ln2_b l1_w_in l1_cmp_k_w1 l1_cmp_k_w2 l1_cmp_v_w1 "
              "l1_cmp_v_w2 l1_w_out l1_ln1_g l1_ln1_b l1_ln2_g l1_ln2_b").split():
        arrays[k] = x[k]
    for L in range(2):
        for k in ("gate", "up", "down"):
            arrays[f"l{L}_expert_w_{k}"] = x[f"l{L}_expert_w_{k}"]

    nc = bacc.Bacc("TRN2", target_bir_lowering=False, num_devices=1)
    arrays = {k: np.ascontiguousarray(v) for k, v in arrays.items()}
    aps = {k: nc.dram_tensor("in_" + k, v.shape, mybir.dt.from_np(v.dtype), kind="ExternalInput").ap()
           for k, v in arrays.items()}
    out = nc.dram_tensor("out", (1, SEQ, D), mybir.dt.float32, kind="ExternalOutput").ap()
    program(nc, aps, out)
    r = run(nc, [{"in_" + k: v for k, v in arrays.items()}], core_ids=[0])
    return r.results[0]["out"]
```
